# Optimizing a Trainium2 kernel written in Bass

```python
import jax, jax.numpy as jnp
from jax import lax
import numpy as np

D_MODEL = 1024
BATCH = 1
SEQ = 256
DEPTH = 1

HEAD_DIM = 64
MIX_WIDTH = D_MODEL
FOX_WIDTH = MIX_WIDTH // 2
SB_WIDTH = MIX_WIDTH - FOX_WIDTH
N_FOX_HEADS = FOX_WIDTH // HEAD_DIM
N_SB_HEADS = SB_WIDTH // HEAD_DIM
IN_PROJ_WIDTH = 3 * FOX_WIDTH + 3 * SB_WIDTH + N_FOX_HEADS
Q_BLOCK = 128
N_MEM = 256
N_XATTN_HEADS = 4
XATTN_HEAD_DIM = D_MODEL // N_XATTN_HEADS
N_GROUPS = 4
EXPERTS_PER_GROUP = 4
N_EXPERTS = N_GROUPS * EXPERTS_PER_GROUP
TOP_K_IN_GROUP = 2
D_FF_EXPERT = D_MODEL // 4
EPS = 1e-6


def _rmsnorm(x, g):
    xf = x.astype(jnp.float32)
    y = xf * lax.rsqrt(jnp.mean(xf * xf, axis=-1, keepdims=True) + EPS)
    return (y * g.astype(jnp.float32)).astype(x.dtype)

def _heads(t, n_heads):
    b, s, _ = t.shape
    return t.reshape(b, s, n_heads, HEAD_DIM).transpose(0, 2, 1, 3)

def _query_blocks(t, n_heads):
    b, s, _ = t.shape
    return t.reshape(b, s // Q_BLOCK, Q_BLOCK, n_heads, HEAD_DIM).transpose(1, 0, 3, 2, 4)

def _merge_blocks(o):
    nb, b, h, qb, dh = o.shape
    return o.transpose(1, 0, 3, 2, 4).reshape(b, nb * qb, h * dh)

def _forgetting_attention(q, k, v, f_logit):
    b, s, _ = q.shape
    nb = s // Q_BLOCK
    c = jnp.cumsum(jax.nn.log_sigmoid(f_logit.astype(jnp.float32)), axis=1).transpose(0, 2, 1)
    c_blocks = c.reshape(b, N_FOX_HEADS, nb, Q_BLOCK).transpose(2, 0, 1, 3)
    qb = _query_blocks(q, N_FOX_HEADS)
    kh = _heads(k, N_FOX_HEADS)
    vh = _heads(v, N_FOX_HEADS)
    starts = jnp.arange(nb, dtype=jnp.int32) * Q_BLOCK
    kpos = jnp.arange(s, dtype=jnp.int32)
    scale = HEAD_DIM ** -0.5

    def one_block(args):
        q_blk, c_blk, start = args
        qpos = start + jnp.arange(Q_BLOCK, dtype=jnp.int32)
        logits = jnp.einsum('bhqd,bhkd->bhqk', q_blk, kh).astype(jnp.float32) * scale
        logits = logits + c_blk[..., None] - c[:, :, None, :]
        logits = jnp.where(kpos[None, :] <= qpos[:, None], logits, -jnp.inf)
        p = jax.nn.softmax(logits, axis=-1)
        return jnp.einsum('bhqk,bhkd->bhqd', p.astype(vh.dtype), vh)

    return _merge_blocks(lax.map(one_block, (qb, c_blocks, starts)))

def _stick_breaking_attention(q, k, v):
    b, s, _ = q.shape
    nb = s // Q_BLOCK
    qb = _query_blocks(q, N_SB_HEADS)
    kh = _heads(k, N_SB_HEADS)
    vh = _heads(v, N_SB_HEADS)
    starts = jnp.arange(nb, dtype=jnp.int32) * Q_BLOCK
    kpos = jnp.arange(s, dtype=jnp.int32)
    scale = HEAD_DIM ** -0.5

    def one_block(args):
        q_blk, start = args
        qpos = start + jnp.arange(Q_BLOCK, dtype=jnp.int32)
        mask = kpos[None, :] < qpos[:, None]
        z = jnp.einsum('bhqd,bhkd->bhqk', q_blk, kh).astype(jnp.float32) * scale
        log_one_minus = jnp.where(mask, jax.nn.log_sigmoid(-z), 0.0)
        tail = lax.cumsum(log_one_minus, axis=3, reverse=True) - log_one_minus
        weight = jnp.where(mask, jnp.exp(jax.nn.log_sigmoid(z) + tail), 0.0)
        return jnp.einsum('bhqk,bhkd->bhqd', weight.astype(vh.dtype), vh)

    return _merge_blocks(lax.map(one_block, (qb, starts)))

def _memory_cross_attention(hn, mn, w_xq, w_xkv, w_xo):
    b, s, d = hn.shape
    m = mn.shape[1]
    q = (hn @ w_xq).reshape(b, s, N_XATTN_HEADS, XATTN_HEAD_DIM)
    kv = mn @ w_xkv
    k = kv[..., :d].reshape(b, m, N_XATTN_HEADS, XATTN_HEAD_DIM)
    v = kv[..., d:].reshape(b, m, N_XATTN_HEADS, XATTN_HEAD_DIM)
    logits = jnp.einsum('bshd,bmhd->bhsm', q, k).astype(jnp.float32) * (XATTN_HEAD_DIM ** -0.5)
    p = jax.nn.softmax(logits, axis=-1)
    o = jnp.einsum('bhsm,bmhd->bshd', p.astype(v.dtype), v).reshape(b, s, d)
    return o @ w_xo

def _hierarchical_moe(u, w_rg, b_rg, w_re, b_re, w_gate, w_up, w_down):
    b, s, d = u.shape
    t = u.reshape(b * s, d)
    tf = t.astype(jnp.float32)
    p_group = jax.nn.softmax(tf @ w_rg.astype(jnp.float32) + b_rg.astype(jnp.float32), axis=-1)
    g_val, g_idx = lax.top_k(p_group, 1)
    g_val, g_idx = g_val[:, 0], g_idx[:, 0]
    e_logits = (tf @ w_re.astype(jnp.float32) + b_re.astype(jnp.float32)).reshape(-1, N_GROUPS, EXPERTS_PER_GROUP)
    in_group = jnp.take_along_axis(e_logits, g_idx[:, None, None], axis=1)[:, 0, :]
    e_val, e_idx = lax.top_k(in_group, TOP_K_IN_GROUP)
    weights = g_val[:, None] * jax.nn.softmax(e_val, axis=-1)
    expert_id = g_idx[:, None] * EXPERTS_PER_GROUP + e_idx
    gate = jnp.sum(jax.nn.one_hot(expert_id, N_EXPERTS, dtype=jnp.float32) * weights[..., None], axis=1)
    y = jnp.zeros((b * s, d), jnp.float32)
    for e in range(N_EXPERTS):
        hidden = jax.nn.silu(t @ w_gate[e]) * (t @ w_up[e])
        y = y + gate[:, e:e + 1] * (hidden @ w_down[e]).astype(jnp.float32)
    return y.astype(u.dtype).reshape(b, s, d)

def first_inputs(seed: int = 0) -> dict:
    key = jax.random.key(seed)
    ks = jax.random.split(key, 24)
    f32 = jnp.float32
    nrm = lambda k, shape, scale: jax.random.normal(k, shape, f32) * scale
    gain = lambda k, shape: 1.0 + 0.02 * jax.random.normal(k, shape, f32)
    L = DEPTH
    return {
        "x": jax.random.normal(ks[0], (BATCH, SEQ, D_MODEL), f32),
        "mem": jax.random.normal(ks[1], (BATCH, N_MEM, D_MODEL), f32),
        "norm_mix": gain(ks[2], (L, D_MODEL)),
        "w_in": nrm(ks[3], (L, D_MODEL, IN_PROJ_WIDTH), D_MODEL ** -0.5),
        "b_forget": 3.0 + 0.5 * jax.random.normal(ks[4], (L, N_FOX_HEADS), f32),
        "norm_fox_out": gain(ks[5], (L, FOX_WIDTH)),
        "norm_sb_out": gain(ks[6], (L, SB_WIDTH)),
        "w_out": nrm(ks[7], (L, MIX_WIDTH, D_MODEL), MIX_WIDTH ** -0.5),
        "norm_xattn": gain(ks[8], (L, D_MODEL)),
        "norm_mem": gain(ks[9], (L, D_MODEL)),
        "w_xq": nrm(ks[10], (L, D_MODEL, D_MODEL), D_MODEL ** -0.5),
        "w_xkv": nrm(ks[11], (L, D_MODEL, 2 * D_MODEL), D_MODEL ** -0.5),
        "w_xo": nrm(ks[12], (L, D_MODEL, D_MODEL), D_MODEL ** -0.5),
        "norm_ffn": gain(ks[13], (L, D_MODEL)),
        "w_router_group": nrm(ks[14], (L, D_MODEL, N_GROUPS), D_MODEL ** -0.5),
        "b_router_group": nrm(ks[15], (L, N_GROUPS), 0.01),
        "w_router_expert": nrm(ks[16], (L, D_MODEL, N_EXPERTS), D_MODEL ** -0.5),
        "b_router_expert": nrm(ks[17], (L, N_EXPERTS), 0.01),
        "w_exp_gate": nrm(ks[18], (L, N_EXPERTS, D_MODEL, D_FF_EXPERT), D_MODEL ** -0.5),
        "w_exp_up": nrm(ks[19], (L, N_EXPERTS, D_MODEL, D_FF_EXPERT), D_MODEL ** -0.5),
        "w_exp_down": nrm(ks[20], (L, N_EXPERTS, D_FF_EXPERT, D_MODEL), D_FF_EXPERT ** -0.5),
        "norm_final": gain(ks[21], (D_MODEL,)),
    }

def first_block(x, mem, norm_mix, w_in, b_forget, norm_fox_out, norm_sb_out, w_out,
              norm_xattn, norm_mem, w_xq, w_xkv, w_xo, norm_ffn,
              w_router_group, b_router_group, w_router_expert, b_router_expert,
              w_exp_gate, w_exp_up, w_exp_down, norm_final):
    h = x
    F, S_ = FOX_WIDTH, SB_WIDTH
    for l in range(DEPTH):
        u = _rmsnorm(h, norm_mix[l])
        proj = u @ w_in[l]
        q_a = proj[..., 0:F]
        k_a = proj[..., F:2 * F]
        v_a = proj[..., 2 * F:3 * F]
        o0 = 3 * F
        q_b = proj[..., o0:o0 + S_]
        k_b = proj[..., o0 + S_:o0 + 2 * S_]
        v_b = proj[..., o0 + 2 * S_:o0 + 3 * S_]
        f_logit = proj[..., o0 + 3 * S_:] + b_forget[l]
        o_a = _forgetting_attention(q_a, k_a, v_a, f_logit)
        o_b = _stick_breaking_attention(q_b, k_b, v_b)
        mixed = jnp.concatenate([_rmsnorm(o_a, norm_fox_out[l]), _rmsnorm(o_b, norm_sb_out[l])], axis=-1)
        h = h + (mixed @ w_out[l]).astype(h.dtype)
        h = h + _memory_cross_attention(_rmsnorm(h, norm_xattn[l]), _rmsnorm(mem, norm_mem[l]),
                                        w_xq[l], w_xkv[l], w_xo[l]).astype(h.dtype)
        h = h + _hierarchical_moe(_rmsnorm(h, norm_ffn[l]), w_router_group[l], b_router_group[l],
                                  w_router_expert[l], b_router_expert[l],
                                  w_exp_gate[l], w_exp_up[l], w_exp_down[l]).astype(h.dtype)
    return _rmsnorm(h, norm_final)


DEPTH_2 = 2

GRID_W = 64
CTX_LEN = 256

F_GROUPS = 4
F_GROUP_DIM = D_MODEL // 16
F_WIDTH = F_GROUPS * F_GROUP_DIM
M_HEADS = 4
M_HEAD_DIM = 3 * D_MODEL // 32
M_WIDTH = M_HEADS * M_HEAD_DIM
M_CHUNK = 64
K_CONV = 5
A_HEADS = 4
A_NOPE = 64
A_ROPE = 32
A_V = 3 * D_MODEL // 32
A_WIDTH = A_HEADS * A_V
Q_LORA = D_MODEL // 4
KV_LORA = D_MODEL // 8
ROPE_THETA = 10000.0
MLP_HIDDEN = 4 * D_MODEL
IN_WIDTHS = (F_WIDTH, M_WIDTH, M_WIDTH, M_WIDTH, M_WIDTH, 4 * M_HEADS, Q_LORA, KV_LORA, A_ROPE)
IN_WIDTH = F_WIDTH + 4 * M_WIDTH + 4 * M_HEADS + Q_LORA + KV_LORA + A_ROPE
MIX_WIDTH_2 = F_WIDTH + M_WIDTH + A_WIDTH


def rmsnorm(x, g):
    xf = x.astype(jnp.float32)
    y = xf * lax.rsqrt(jnp.mean(xf * xf, axis=-1, keepdims=True) + EPS)
    return (y * g.astype(jnp.float32)).astype(x.dtype)

def modulate(h, shift, scale):
    return h * (1 + scale) + shift

def split_proj(p):
    out, off = [], 0
    for w in IN_WIDTHS:
        out.append(p[..., off:off + w])
        off += w
    return out

def axial_rope(n):
    rows = n // GRID_W
    row = jnp.repeat(jnp.arange(rows, dtype=jnp.float32), GRID_W)
    col = jnp.tile(jnp.arange(GRID_W, dtype=jnp.float32), rows)
    nf = A_ROPE // 4
    freqs = ROPE_THETA ** (-jnp.arange(nf, dtype=jnp.float32) / nf)
    ang = jnp.stack([row[:, None] * freqs, col[:, None] * freqs], axis=1)
    return jnp.cos(ang), jnp.sin(ang)

def apply_rope(x, cos, sin):
    xs = x.reshape(x.shape[:-1] + (2, 2, A_ROPE // 4)).astype(jnp.float32)
    x1, x2 = xs[..., 0, :], xs[..., 1, :]
    out = jnp.stack([x1 * cos - x2 * sin, x1 * sin + x2 * cos], axis=-2)
    return out.reshape(x.shape).astype(x.dtype)

def fourier_mix(u):
    B, N, _ = u.shape
    ug = u.astype(jnp.float32).reshape(B, N, F_GROUPS, F_GROUP_DIM)
    y = jnp.fft.fft2(ug, axes=(1, 3), norm="ortho").real
    return y.reshape(B, N, F_WIDTH).astype(u.dtype)

def dwconv_centred(u, w):
    C = u.shape[-1]
    pad = w.shape[0] // 2
    return lax.conv_general_dilated(u, w[:, None, :].astype(u.dtype), (1,), [(pad, pad)],
                                    dimension_numbers=("NWC", "WIO", "NWC"), feature_group_count=C)

def mlstm_inputs(mq, mk, mv, mg, conv_w, b_g):
    B, N, _ = mq.shape
    qk = jax.nn.silu(dwconv_centred(jnp.concatenate([mq, mk], axis=-1), conv_w))
    heads = lambda a: a.reshape(B, N, M_HEADS, M_HEAD_DIM).transpose(0, 2, 1, 3).astype(jnp.float32)
    q = heads(qk[..., :M_WIDTH]) * (M_HEAD_DIM ** -0.5)
    k = heads(qk[..., M_WIDTH:])
    v = heads(mv)
    g = (mg.astype(jnp.float32) + b_g.astype(jnp.float32)).reshape(B, N, 4, M_HEADS).transpose(2, 0, 3, 1)
    fwd = (q, k, v, g[0], jax.nn.log_sigmoid(g[1]))
    bwd = (q, k, v, g[2], jax.nn.log_sigmoid(g[3]))
    return fwd, bwd

def mlstm_zero_state(B):
    return (jnp.zeros((B, M_HEADS, M_HEAD_DIM, M_HEAD_DIM), jnp.float32),
            jnp.zeros((B, M_HEADS, M_HEAD_DIM), jnp.float32),
            jnp.zeros((B, M_HEADS), jnp.float32))

def mlstm_chunkwise(q, k, v, li, lf, state):
    B, H, N, _ = q.shape
    L = M_CHUNK
    nc = N // L
    to_chunks = lambda a: jnp.moveaxis(a.reshape((B, H, nc, L) + a.shape[3:]), 2, 0)
    tri = jnp.tril(jnp.ones((L, L), dtype=bool))

    def step(carry, inp):
        C, n, m = carry
        qb, kb, vb, ib, fb = inp
        b = jnp.cumsum(fb, axis=-1)
        dmat = jnp.where(tri, b[..., :, None] - b[..., None, :] + ib[..., None, :], -jnp.inf)
        inter = b + m[..., None]
        m_t = jnp.maximum(inter, dmat.max(axis=-1))
        w_intra = jnp.exp(dmat - m_t[..., None])
        w_inter = jnp.exp(inter - m_t)
        s = jnp.einsum("bhtd,bhsd->bhts", qb, kb) * w_intra
        num = jnp.einsum("bhts,bhsv->bhtv", s, vb) + w_inter[..., None] * jnp.einsum("bhtd,bhdv->bhtv", qb, C)
        den = s.sum(axis=-1) + w_inter * jnp.einsum("bhtd,bhd->bht", qb, n)
        h = num / jnp.maximum(jnp.abs(den), jnp.exp(-m_t))[..., None]
        b_last = b[..., -1]
        g = b_last[..., None] - b + ib
        m_new = jnp.maximum(b_last + m, g.max(axis=-1))
        decay = jnp.exp(b_last + m - m_new)
        wk = jnp.exp(g - m_new[..., None])
        C_new = decay[..., None, None] * C + jnp.einsum("bhs,bhsd,bhsv->bhdv", wk, kb, vb)
        n_new = decay[..., None] * n + jnp.einsum("bhs,bhsd->bhd", wk, kb)
        return (C_new, n_new, m_new), h

    state, hc = lax.scan(step, state, tuple(to_chunks(a) for a in (q, k, v, li, lf)))
    h = jnp.moveaxis(hc, 0, 2).reshape(B, H, N, -1)
    return h, state

def mlstm_direction(seq, state, reverse):
    if reverse:
        seq = tuple(jnp.flip(a, axis=2) for a in seq)
    h, state = mlstm_chunkwise(*seq, state)
    if reverse:
        h = jnp.flip(h, axis=2)
    return h, state

def mlstm_output(h_f, h_b, mo, g_m):
    B, H, N, dv = h_f.shape
    h = (h_f + h_b).transpose(0, 2, 1, 3)
    h = h * lax.rsqrt(jnp.mean(h * h, axis=-1, keepdims=True) + EPS)
    h = h.reshape(B, N, M_WIDTH) * g_m.astype(jnp.float32) * jax.nn.sigmoid(mo.astype(jnp.float32))
    return h.astype(mo.dtype)

def mla_queries(cq, g_qn, w_uq, rope):
    B, N, _ = cq.shape
    q = (rmsnorm(cq, g_qn) @ w_uq).reshape(B, N, A_HEADS, A_NOPE + A_ROPE).transpose(0, 2, 1, 3)
    qn, qr = q[..., :A_NOPE], q[..., A_NOPE:]
    if rope is not None:
        qr = apply_rope(qr, *rope)
    return qn, qr

def mla_keys(ckv, kr, g_kvn, w_ukv, rope):
    B, N, _ = ckv.shape
    kv = (rmsnorm(ckv, g_kvn) @ w_ukv).reshape(B, N, A_HEADS, A_NOPE + A_V).transpose(0, 2, 1, 3)
    kn, v = kv[..., :A_NOPE], kv[..., A_NOPE:]
    if rope is not None:
        kr = apply_rope(kr, *rope)
    return kn, kr, v

def softmax_attend(qn, qr, key_sets):
    scale = (A_NOPE + A_ROPE) ** -0.5
    s = jnp.concatenate([jnp.einsum("bhqd,bhkd->bhqk", qn, kn) + jnp.einsum("bhqr,bkr->bhqk", qr, kr)
                         for kn, kr, _ in key_sets], axis=-1)
    p = jax.nn.softmax(s.astype(jnp.float32) * scale, axis=-1)
    out, off = None, 0
    for _, _, v in key_sets:
        nk = v.shape[2]
        o = jnp.einsum("bhqk,bhkd->bhqd", p[..., off:off + nk].astype(v.dtype), v)
        out = o if out is None else out + o
        off += nk
    return out

def blocked_attend(qn, qr, key_sets):
    B, H, N, _ = qn.shape
    nb = N // Q_BLOCK
    blk = lambda a: jnp.moveaxis(a.reshape(B, H, nb, Q_BLOCK, a.shape[-1]), 2, 0)
    out = lax.map(lambda qs: softmax_attend(qs[0], qs[1], key_sets), (blk(qn), blk(qr)))
    return jnp.moveaxis(out, 0, 2).reshape(B, H, N, -1)

def merge_heads(y):
    B, H, N, dv = y.shape
    return y.transpose(0, 2, 1, 3).reshape(B, N, H * dv)

def sqrelu_mlp(h, w_up, w_down):
    return jnp.square(jax.nn.relu(h @ w_up)) @ w_down

def second_inputs(seed: int = 0) -> dict:
    key = jax.random.key(seed)
    ks = jax.random.split(key, 24)
    nrm = lambda k, shape, s: jax.random.normal(k, shape, jnp.float32) * s
    gain = lambda k, shape: 1.0 + 0.02 * jax.random.normal(k, shape, jnp.float32)
    f_bias = jnp.linspace(3.0, 6.0, M_HEADS, dtype=jnp.float32)
    z = jnp.zeros((M_HEADS,), jnp.float32)
    gate_base = jnp.concatenate([z, f_bias, z, f_bias])
    return {
        "x": nrm(ks[0], (BATCH, SEQ, D_MODEL), 1.0),
        "c": nrm(ks[1], (BATCH, D_MODEL), 1.0),
        "ctx": nrm(ks[2], (BATCH, CTX_LEN, D_MODEL), 1.0),
        "c_ctx": nrm(ks[3], (D_MODEL,), 1.0),
        "w_mod": nrm(ks[4], (DEPTH_2, D_MODEL, 6 * D_MODEL), 0.5 * D_MODEL ** -0.5),
        "b_mod": nrm(ks[5], (DEPTH_2, 6 * D_MODEL), 0.01),
        "g_norm1": gain(ks[6], (DEPTH_2, D_MODEL)),
        "g_norm2": gain(ks[7], (DEPTH_2, D_MODEL)),
        "w_in": nrm(ks[8], (DEPTH_2, D_MODEL, IN_WIDTH), D_MODEL ** -0.5),
        "b_gates": gate_base[None, :] + nrm(ks[9], (DEPTH_2, 4 * M_HEADS), 0.1),
        "conv_qk": nrm(ks[10], (DEPTH_2, K_CONV, 2 * M_WIDTH), K_CONV ** -0.5),
        "g_mlstm": gain(ks[11], (DEPTH_2, M_WIDTH)),
        "g_q_norm": gain(ks[12], (DEPTH_2, Q_LORA)),
        "g_kv_norm": gain(ks[13], (DEPTH_2, KV_LORA)),
        "w_uq": nrm(ks[14], (DEPTH_2, Q_LORA, A_HEADS * (A_NOPE + A_ROPE)), Q_LORA ** -0.5),
        "w_ukv": nrm(ks[15], (DEPTH_2, KV_LORA, A_HEADS * (A_NOPE + A_V)), KV_LORA ** -0.5),
        "w_out": nrm(ks[16], (DEPTH_2, MIX_WIDTH_2, D_MODEL), MIX_WIDTH_2 ** -0.5),
        "w_up": nrm(ks[17], (DEPTH_2, D_MODEL, MLP_HIDDEN), D_MODEL ** -0.5),
        "w_down": nrm(ks[18], (DEPTH_2, MLP_HIDDEN, D_MODEL), MLP_HIDDEN ** -0.5),
        "g_final": gain(ks[19], (D_MODEL,)),
    }

def second_block(x, c, ctx, c_ctx, w_mod, b_mod, g_norm1, g_norm2, w_in, b_gates, conv_qk, g_mlstm,
              g_q_norm, g_kv_norm, w_uq, w_ukv, w_out, w_up, w_down, g_final):
    B, S, _ = x.shape
    rope_lat = axial_rope(S)
    xc = ctx
    for l in range(DEPTH_2):
        last = l == DEPTH_2 - 1
        mod = (jax.nn.silu(c) @ w_mod[l] + b_mod[l])[:, None, :]
        mod_c = jax.nn.silu(c_ctx) @ w_mod[l] + b_mod[l]
        sh1, sc1, ga1, sh2, sc2, ga2 = jnp.split(mod, 6, axis=-1)
        sh1c, sc1c, ga1c, sh2c, sc2c, ga2c = jnp.split(mod_c, 6, axis=-1)

        h = modulate(rmsnorm(x, g_norm1[l]), sh1, sc1)
        hc = modulate(rmsnorm(xc, g_norm1[l]), sh1c, sc1c)
        pf, mq, mk, mv, mo, mg, cq, ckv, kr = split_proj(h @ w_in[l])
        pfc, mqc, mkc, mvc, moc, mgc, cqc, ckvc, krc = split_proj(hc @ w_in[l])

        y_f = fourier_mix(pf)

        fwd_c, bwd_c = mlstm_inputs(mqc, mkc, mvc, mgc, conv_qk[l], b_gates[l])
        fwd, bwd = mlstm_inputs(mq, mk, mv, mg, conv_qk[l], b_gates[l])
        zero = mlstm_zero_state(B)
        hcf, st_f = mlstm_direction(fwd_c, zero, False)
        hcb, st_b = mlstm_direction(bwd_c, zero, True)
        hf, _ = mlstm_direction(fwd, st_f, False)
        hb, _ = mlstm_direction(bwd, st_b, True)
        y_m = mlstm_output(hf, hb, mo, g_mlstm[l])

        ctx_keys = mla_keys(ckvc, krc, g_kv_norm[l], w_ukv[l], None)
        lat_keys = mla_keys(ckv, kr, g_kv_norm[l], w_ukv[l], rope_lat)
        qn, qr = mla_queries(cq, g_q_norm[l], w_uq[l], rope_lat)
        y_a = merge_heads(blocked_attend(qn, qr, (lat_keys, ctx_keys)))

        x = x + ga1 * (jnp.concatenate([y_f, y_m, y_a], axis=-1) @ w_out[l])
        x = x + ga2 * sqrelu_mlp(modulate(rmsnorm(x, g_norm2[l]), sh2, sc2), w_up[l], w_down[l])

        if not last:
            y_fc = fourier_mix(pfc)
            y_mc = mlstm_output(hcf, hcb, moc, g_mlstm[l])
            qn_c, qr_c = mla_queries(cqc, g_q_norm[l], w_uq[l], None)
            y_ac = merge_heads(softmax_attend(qn_c, qr_c, (ctx_keys,)))
            xc = xc + ga1c * (jnp.concatenate([y_fc, y_mc, y_ac], axis=-1) @ w_out[l])
            xc = xc + ga2c * sqrelu_mlp(modulate(rmsnorm(xc, g_norm2[l]), sh2c, sc2c), w_up[l], w_down[l])

    return rmsnorm(x, g_final)


def setup_inputs(seed=0):
    out = dict(first_inputs(seed))
    for name, value in second_inputs(seed + 1).items():
        if name != "x":
            out[name + "_2"] = value
    return out


def reference(
    x, mem, norm_mix, w_in, b_forget, norm_fox_out, norm_sb_out, w_out, norm_xattn, norm_mem,
    w_xq, w_xkv, w_xo, norm_ffn, w_router_group, b_router_group, w_router_expert,
    b_router_expert, w_exp_gate, w_exp_up, w_exp_down, norm_final, c_2, ctx_2, c_ctx_2, w_mod_2,
    b_mod_2, g_norm1_2, g_norm2_2, w_in_2, b_gates_2, conv_qk_2, g_mlstm_2, g_q_norm_2,
    g_kv_norm_2, w_uq_2, w_ukv_2, w_out_2, w_up_2, w_down_2, g_final_2,
):
    x = first_block(
        x, mem, norm_mix, w_in, b_forget, norm_fox_out, norm_sb_out, w_out, norm_xattn,
        norm_mem, w_xq, w_xkv, w_xo, norm_ffn, w_router_group, b_router_group, w_router_expert,
        b_router_expert, w_exp_gate, w_exp_up, w_exp_down, norm_final,
    )
    return second_block(
        x, c_2, ctx_2, c_ctx_2, w_mod_2, b_mod_2, g_norm1_2, g_norm2_2, w_in_2, b_gates_2,
        conv_qk_2, g_mlstm_2, g_q_norm_2, g_kv_norm_2, w_uq_2, w_ukv_2, w_out_2, w_up_2,
        w_down_2, g_final_2,
    )


_drawn_inputs = setup_inputs


def setup_inputs(seed=0):
    import zlib

    import numpy as np

    out = dict(_drawn_inputs(seed))
    spreads = {}
    factors = {'norm_fox_out': 2.827,
     'norm_sb_out': 2.868,
     'norm_xattn': 8.0,
     'norm_mem': 8.0,
     'norm_ffn': 3.016,
     'b_router_group': 64.0,
     'b_router_expert': 6.702,
     'norm_final': 2.692,
     'g_norm1_2': 8.0,
     'g_norm2_2': 4.611,
     'g_mlstm_2': 27.814,
     'g_q_norm_2': 8.0,
     'g_kv_norm_2': 8.0}
    for name, (base, spread) in spreads.items():
        noise = np.random.default_rng([zlib.crc32(name.encode()), seed]).standard_normal(out[name].shape)
        drawn = base * np.exp(spread * noise) if base else spread * noise
        out[name] = __import__('jax').numpy.asarray(drawn.astype(out[name].dtype))
    for name, factor in factors.items():
        out[name] = (out[name] * factor).astype(out[name].dtype)
    return out
```

```python
from contextlib import ExitStack

import numpy as np

import concourse.bass as bass
from concourse import mybir

F32 = mybir.dt.float32
ALU = mybir.AluOpType
ACT = mybir.ActivationFunctionType
AX_X = mybir.AxisListType.X

P = 128
D = 1024
KT = D // P
T = 256
TB = T // P
NF = 8
HD = 64
NX = 4
NE = 16
NL = 2
MH = 4
MD = 96
RD = 32
FF = 4096
MT = FF // P
EPS = 1e-6
BIG = -1e30
RING = 4
SLOT = 2048
CTX, LAT, ALL = slice(0, T), slice(T, 2 * T), slice(0, 2 * T)

N_QK, N_V, N_XKV, N_SQ = 8, 4, 8, 4
N_MOE = 6 * NE
N_IN2, N_OUT2, N_UP, N_DN = 11, 5, 16, 16
LAYER_SLOTS = N_IN2 + N_OUT2 + N_UP + N_DN
S_QK = 0
S_V = S_QK + N_QK
S_XKV = S_V + N_V
S_OUT = S_XKV + N_XKV
S_XQ = S_OUT + N_SQ
S_XO = S_XQ + N_SQ
S_MOE = S_XO + N_SQ
S_L = S_MOE + N_MOE
N_SLOTS = S_L + NL * LAYER_SLOTS

_COLS = [("ident", 128), ("ones", 128), ("zeros", 128), ("tri", 128), ("m_le", 512), ("m_ge", 512), ("m_gt", 512),
         ("neg01", 512), ("cdsd", 256), ("cn", 512), ("sn", 512), ("cos", 256), ("sin", 256), ("rot", 96), ("w4", 4),
         ("eps", 1), ("g_mix", 8), ("g_xattn", 8), ("g_mem", 8), ("g_ffn", 8), ("g_fin1", 8), ("g_fox", 4), ("g_sb", 4),
         ("b_forget", 1), ("b_route", 20), ("w_f", 64), ("w_route", 160), ("c", 16), ("b_mod", 192), ("g_fin2", 8)]
for _l in range(NL):
    _COLS += [(f"g1_{_l}", 16), (f"g2_{_l}", 16), (f"g_ml_{_l}", 4), (f"g_qn_{_l}", 2), (f"g_kvn_{_l}", 1),
              (f"conv_{_l}", 40), (f"b_g_{_l}", 4), (f"uq_{_l}", 768), (f"ukv_{_l}", 640), (f"w_g_{_l}", 128)]
COL = {}
_at = 0
for _name, _n in _COLS:
    COL[_name] = (_at, _n)
    _at += _n
N_COLS = _at

NORMS = ["mix", "mem", "fox", "sb", "xattn", "ffn", "fin1"]
for _l in range(NL):
    NORMS += [f"n1_{_l}", f"cq_{_l}", f"ckv_{_l}"] + [f"head_{_l}_{_h}" for _h in range(MH)] + [f"n2_{_l}"]
NORMS += ["fin2"]
NORM = {name: i for i, name in enumerate(NORMS)}

UNITS = [("fox", h, None) for h in range(NF)] + [("xat", h, None) for h in range(NX)]
for _l in range(NL):
    if _l == 0:
        UNITS += [(f"mctx{_l}", h, None) for h in range(MH)]
    UNITS += [(f"mlat{_l}", h, q) for h in range(MH) for q in range(TB)]
UNIT0 = {}
for _i, _u in enumerate(UNITS):
    UNIT0.setdefault(_u[0], _i)


class Jobs:

    def __init__(self):
        self.first, self.engines, self.counted = {}, [], []

    def add(self, phase, count, engine, counted=True):
        self.first[phase] = len(self.engines)
        self.engines += [engine] * count
        self.counted += [counted] * count

    def number(self, phase, j=0):
        return self.first[phase] + j

    def full(self, n):
        return self.counted[: n + 1].count(True)

    def emptied(self, n):
        engine = self.engines[n]
        if engine.startswith("mlstm"):
            return "ml_sum", MH * (int(engine[-1]) + 1)
        return f"job_emptied_{engine}", self.engines[: n + 1].count(engine)


JOBS = Jobs()
for _phase, _count, _engine in [("qk", N_QK, "act"), ("v", N_V, "act"), ("xkv", N_XKV, "act"), ("out1", 4, "dve"),
                                ("xq", 4, "act"), ("xo", 4, "dve")]:
    JOBS.add(_phase, _count, _engine)
JOBS.add("moe_y", 4, "dve", False)
for _l in range(NL):
    _w = 2 if _l == 0 else 1
    for _phase, _count, _engine in [("mqk", 8, "act"), ("mv", 4, "act"), ("mo", 4, "act"), ("cq", 2, "act"),
                                    ("ckv", 2, "act"), ("pf", 2, "act"), ("uq", 4, "act"), ("rot", 5, "dve"),
                                    ("kn", 4, "act"), ("va", 4, "act"),
                                    ("fa0", 2, "act"), ("fy0", 2, "act"), ("fa1", 2 * (_w - 1), "act"), ("fy1", 2 * (_w - 1), "act"),
                                    ("mlstm", 4, f"mlstm{_l}"),
                                    ("out", 8, "dve"), ("up", MT, "act"), ("dn", 8, "dve")]:
        JOBS.add(f"{_phase}_{_l}", _count, _engine, _phase != "mlstm")


def build(nc, w_stream, table_in, x_in, mem_in, ctx_in, out):
    with ExitStack() as stack:
        def sb(name, shape):
            return stack.enter_context(nc.sbuf_tensor(name, shape, F32))

        sems = {}

        def S(name):
            if name not in sems:
                sems[name] = stack.enter_context(nc.semaphore(name))
            return sems[name]

        bank = [stack.enter_context(nc.psum_tensor(f"bank{i}", [P, 512], F32)) for i in range(8)]
        ring = sb("ring", [P, RING, SLOT])
        table = sb("table", [P, N_COLS])
        res = sb("res", [P, KT, 2 * T])
        u = sb("u", [P, KT, 2 * T])
        sq = sb("sq", [P, KT * 2 * T])
        rstd = sb("rstd", [P, 2 * T])
        modv = sb("modv", [P, 192])
        gmod = sb("gmod", [P, 2 * NL, 16])
        silu_c = sb("silu_c", [P, KT, 2])
        small = sb("small", [P, 256])
        work = sb("work", [P, 20544])

        def tab(name, rows=P):
            a, n = COL[name]
            return table[0:rows, a:a + n]

        def view(lo, *shape, rows=P):
            n = int(np.prod(shape))
            v = work[0:rows, lo:lo + n]
            if len(shape) == 2:
                return v.rearrange("p (a b) -> p a b", a=shape[0])
            if len(shape) == 3:
                return v.rearrange("p (a b c) -> p a b c", a=shape[0], b=shape[1])
            return v

        ident, ones, zeros = tab("ident"), tab("ones"), tab("zeros")

        qk = view(0, 16, T)
        v1 = view(4096, TB, D)
        heads = view(6144, KT, T)
        kx = view(8192, KT, T)
        vx = view(10240, TB, D)
        qx = view(12288, KT, T)
        crow = view(14336, 5, T, rows=8)
        sbt = [view(15616 + i * 2048, 4, 512) for i in range(2)]
        gates = view(0, NE, T)
        hid = view(4096, 2, T)
        eg = view(4608, 512)
        prob = [sq[:, i * 512:(i + 1) * 512] for i in range(2)]
        probT = [sq[:, 1024 + i * 512:1536 + i * 512] for i in range(2)]
        qkp = work[0:MD, 0:4160].rearrange("p (h s t) -> p h s t", h=8, s=2)
        qa = view(0, MH, 512, rows=MD)
        ka = view(2048, MH, 512, rows=MD)
        qc = view(4160, 8, 512, rows=MD)
        mv = view(8256, 4, 384)
        mo = view(9792, MH, 512, rows=MD)
        va = view(11840, 4, 384)
        yf = view(13376, 2, 512)
        ym = view(14400, MH, 512, rows=MD)
        ya = view(16448, MH, 512, rows=MD)
        cq = view(18496, 2, 512)
        ckv = view(19520, 512)
        kr = view(20032, 512, rows=MD)
        pf = view(14400, 2, 512)
        hidden = view(0, MT, 512)
        scratch = u[:, :, :].rearrange("p a b -> p (a b)")
        fa = scratch[:, 2048:3072].rearrange("p (a b c) -> p a b c", a=2, b=TB)
        rows_buf = sb("rows_buf", [32 + MH, 5, 512])
        rows = [rows_buf[32 * d:32 * d + MH] for d in range(2)]
        row_ident = [ident[32 * d:32 * d + MH, 32 * d:32 * d + MH] for d in range(2)]
        gcol = sb("gcol", [P, 2, 4, MH])

        def slot(n):
            return ring[:, n % RING, :]

        def tile(n, j, m=P):
            return ring[:, n % RING, j * P:j * P + m]

        class Chain:

            def __init__(self, eng, name):
                self.eng, self.sem, self.n, self.more = eng, S(name), 0, None

            def link(self, ins):
                ins.then_inc(self.sem, 1)
                self.n += 1
                self.eng.wait_ge(self.sem, self.n if self.more is None else self.more + self.n)

            def loop(self, i, per):
                self.start, self.per, self.more = self.n, per, i * per

            def end(self, turns):
                assert self.n - self.start == self.per, (self.n - self.start, self.per)
                self.n, self.more = self.start + self.per * turns, None

        def full(eng, phase, j=0):
            n = JOBS.number(phase, j)
            eng.wait_ge(S("job_full"), JOBS.full(n))
            return bank[n % 4]

        def emptied(ins, engine):
            ins.then_inc(S(f"job_emptied_{engine}"), 1)

        def wait_emptied(eng, phase, j):
            sem, count = JOBS.emptied(JOBS.number(phase, j))
            eng.wait_ge(S(sem), count)

        def lin_cols(l):
            return ALL if l == 0 else LAT

        def mlb(l, i):
            return JOBS.number(f"mlstm_{l}", i) % 4

        def ml_args(l, h, kb, d):
            if l == 0:
                return 2 * (4 * h + kb) + d + 1
            return 2 * 4 * MH + 2 * (2 * h + kb - 2) + d + 1

        block = stack.enter_context(nc.Block())

        @block.sync
        def _(sp):
            sp.dma_start(res[:, :, LAT], x_in).then_inc(S("x_in"), 16)
            sp.dma_start(table[:, :], table_in).then_inc(S("table_in"), 16)
            for s in range(RING):
                sp.dma_start(ring[:, s, :], w_stream[s]).then_inc(S(f"slot_in{s}"), 16)
                if s == 1:
                    sp.dma_start(res[:, :, CTX], mem_in).then_inc(S("mem_in"), 16)
            with sp.Fori(1, N_SLOTS // RING) as i:
                for s in range(RING):
                    sp.wait_ge(S("slot_used"), i * RING + (s + 1 - RING))
                    sp.dma_start(ring[:, s, :], w_stream[i * RING + s]).then_inc(S(f"slot_in{s}"), 16)
            sp.wait_ge(S("norm_out"), NORM["fin2"] + 1)
            sp.dma_start(out, res[:, :, LAT]).then_inc(S("stored"), 16)
            sp.wait_ge(S("stored"), 16)

        @block.gpsimd
        def _(pool):
            pool.wait_ge(S("norm_out"), NORM["mem"] + 1)
            pool.dma_start(res[:, :, CTX], ctx_in).then_inc(S("ctx_in"), 16)

            for h in range(NF):
                t = sbt[h % 2]
                pool.wait_ge(S("sb_softplus"), h + 1)
                pool.tensor_tensor(t[:, 1, :], t[:, 1, :], tab("neg01"), ALU.mult).then_inc(S("sb_log"), 1)

        @block.scalar
        def _(act):
            ch = Chain(act, "act_step")

            def norm(name, src, dst, p, n, width):
                i = NORM[name]
                act.activation(dst, src, ACT.Square).then_inc(S("norm_sq"), 1)
                act.wait_ge(S("norm_ms"), i + 1)
                if i:
                    act.wait_ge(S("norm_out"), i)
                ch.link(act.activation(rstd[0:p, 0:n], bank[7][0:p, 0:n], ACT.Ln, bias=tab("eps")[0:p],
                                       scale=1.0 / width))
                act.activation(rstd[0:p, 0:n], rstd[0:p, 0:n], ACT.Exp, scale=-0.5).then_inc(S("norm_rstd"), 1)

            def sqv(k, n):
                return sq[:, 0:k * n].rearrange("p (k n) -> p k n", k=k)

            def softmax(i):
                g, w = (1, 512) if UNITS[i][2] is not None else (2, 256)
                act.wait_ge(S("sm_max"), i + 1)
                if i >= 2:
                    act.wait_ge(S("sm_tr"), i - 1)
                for k in range(g):
                    last = act.activation(prob[i % 2][:, k * w:(k + 1) * w], bank[4 + i % 2][:, k * w:(k + 1) * w],
                                          ACT.Exp, bias=smv(i, 0, k), accum_out=smv(i, 2, k))
                last.then_inc(S("sm_exp"), 1)

            def transposed(i):
                act.wait_ge(S("sm_tr"), i + 1)
                if i >= 2:
                    act.wait_ge(S("sm_o"), i - 1)
                act.activation(probT[i % 2], bank[6][:, :], ACT.Copy).then_inc(S("sm_pt"), 1)

            def smv(i, what, k):
                a = (i % 2) * 8 + what * 2 + k
                return small[:, a:a + 1]

            act.wait_ge(S("table_in"), 16)
            cin = tab("c").rearrange("p (k c) -> p k c", k=KT)
            act.activation(small[:, 64:80], tab("c"), ACT.Exp, scale=-1.0).then_inc(S("c_exp"), 1)
            act.wait_ge(S("x_in"), 16)
            norm("mix", res[:, :, LAT], sqv(KT, T), P, T, D)
            act.wait_ge(S("mem_in"), 16)
            norm("mem", res[:, :, CTX], sqv(KT, T), P, T, D)

            def log1p_rows(src, dst, sem_in, count, sem_out):
                act.wait_ge(S(sem_in), count)
                ch.link(act.activation(dst, src, ACT.Abs))
                ch.link(act.activation(dst, dst, ACT.Exp, scale=-1.0))
                act.activation(dst, dst, ACT.Ln, bias=1.0).then_inc(S(sem_out), 1)

            for s in range(N_QK):
                b = full(act, "qk", s)
                scale = HD ** -0.5 if s in (0, 1, 4, 5) else 1.0
                emptied(act.activation(qk[:, 2 * s:2 * s + 2, :], b[:, :], ACT.Copy, scale=scale), "act")
            log1p_rows(crow[:, 0, :], crow[:, 1, :], "fox_f", 1, "fox_ln")
            for s in range(N_V):
                b = full(act, "v", s)
                emptied(act.activation(v1[:, :, s * T:(s + 1) * T], b[:, :], ACT.Copy), "act")

            def xkv(s):
                b = full(act, "xkv", s)
                dst = kx[:, 2 * s:2 * s + 2, :] if s < 4 else vx[:, :, (s - 4) * T:(s - 3) * T]
                emptied(act.activation(dst, b[:, :], ACT.Copy), "act")

            for i in range(NF + 1):
                if i < NF:
                    softmax(i)
                    xkv(i)
                if i >= 1:
                    transposed(i - 1)

            def sb_exp(h):
                t = sbt[h % 2]
                act.wait_ge(S("sb_arg"), h + 1)
                act.activation(t[:, 3, :], t[:, 2, :], ACT.Exp).then_inc(S("sb_w"), 1)

            for h in range(NF + 1):
                if h < NF:
                    t = sbt[h % 2]
                    act.wait_ge(S("sb_z"), h + 1)
                    if h >= 2:
                        act.wait_ge(S("sb_softplus"), h - 1)
                    ch.link(act.activation(t[:, 0, :], bank[4 + h % 2][:, :], ACT.Abs))
                    ch.link(act.activation(t[:, 0, :], t[:, 0, :], ACT.Exp, scale=-1.0))
                    act.activation(t[:, 0, :], t[:, 0, :], ACT.Ln, bias=1.0).then_inc(S("sb_ln"), 1)
                if h >= 1:
                    sb_exp(h - 1)

            act.wait_ge(S("sb_out"), NF)
            norm("fox", heads[:, 0:4, :], sqv(4, T), P, T, 512)
            norm("sb", heads[:, 4:8, :], sqv(4, T), P, T, 512)
            wait_emptied(act, "out1", 3)
            norm("xattn", res[:, :, LAT], sqv(KT, T), P, T, D)
            for s in range(4):
                b = full(act, "xq", s)
                emptied(act.activation(qx[:, 2 * s:2 * s + 2, :], b[:, :], ACT.Copy, scale=256 ** -0.5), "act")
            for i in range(NX + 1):
                if i < NX:
                    softmax(UNIT0["xat"] + i)
                if i >= 1:
                    transposed(UNIT0["xat"] + i - 1)
            wait_emptied(act, "xo", 3)
            norm("ffn", res[:, :, LAT], sqv(KT, T), P, T, D)

            for b in range(TB):
                act.wait_ge(S("rt_max"), b + 1)
                r = small[:, 96 + 64 * b:160 + 64 * b]
                act.activation(r[:, 24:28], r[:, 0:4], ACT.Exp, bias=r[:, 20:21],
                               accum_out=r[:, 21:22]).then_inc(S("rt_exp"), 1)
                act.wait_ge(S("rt_diff"), b + 1)
                act.activation(r[:, 22:23], r[:, 23:24], ACT.Exp).then_inc(S("rt_exp2"), 1)
            for e in range(NE // 2):
                act.wait_ge(S("gate_full"), e + 1)
                act.activation(gates[:, 2 * e:2 * e + 2, :], bank[4 + e % 2][:, :], ACT.Copy).then_inc(S("gate_in"), 1)
            with act.Fori(0, NE) as e:
                act.wait_ge(S("moe_gate"), e + 1)
                act.wait_ge(S("moe_hid"), e + 1)
                act.activation(eg, bank[4][:, :], ACT.Exp, scale=-1.0).then_inc(S("moe_exp"), 1)
            wait_emptied(act, "moe_y", 3)
            norm("fin1", res[:, :, LAT], sqv(KT, T), P, T, D)

            def shift(l, k2):
                at = l * 48 + (0 if k2 == 0 else 24)
                act.wait_ge(S("norm_out"), NORM[f"n{k2 + 1}_{l}"] + 1)
                for k in range(KT):
                    for which, cols in ((0, LAT), (1, CTX)):
                        if k2 == 1 and l == NL - 1 and which == 1:
                            continue
                        last = act.activation(u[:, k, cols], u[:, k, cols], ACT.Identity,
                                              bias=modv[:, 2 * (at + k) + which:2 * (at + k) + which + 1])
                last.then_inc(S("u_mod"), 1)

            for l in range(NL):
                cols = lin_cols(l)
                n = cols.stop - cols.start
                if l == 0:
                    act.wait_ge(S("ctx_in"), 16)
                act.wait_ge(S("norm_out"), NORM["fin1"] + 1 if l == 0 else 1)
                if l:
                    wait_emptied(act, f"dn_{l - 1}", 7)
                norm(f"n1_{l}", res[:, :, :], sqv(KT, 2 * T), P, 2 * T, D)
                shift(l, 0)
                for d in range(2):
                    log1p_rows(rows[d][:, 1, :], rows[d][:, 2, :], "ml_f", 2 * l + d + 1, "ml_ln")
                for j in range(8):
                    b = full(act, f"mqk_{l}", j)
                    if j < 4 and l:
                        last = act.activation(qkp[:, j, 1, 2:258], b[0:MD, 0:T], ACT.Copy)
                    else:
                        last = act.activation(qkp[:, j, :, 2:258],
                                              b[0:MD, :].rearrange("p (s t) -> p s t", s=2), ACT.Copy)
                    emptied(last, "act")
                for j in range(4):
                    b = full(act, f"mv_{l}", j)
                    emptied(act.activation(mv[:, j, :], b[:, 0:384], ACT.Copy), "act")
                for j in range(4):
                    b = full(act, f"mo_{l}", j)
                    emptied(act.activation(mo[:, j, cols], b[0:MD, 0:n], ACT.Exp, scale=-1.0), "act")
                for j in range(2):
                    b = full(act, f"cq_{l}", j)
                    emptied(act.activation(cq[:, j, cols], b[:, 0:n], ACT.Copy), "act")
                b = full(act, f"ckv_{l}", 0)
                emptied(act.activation(ckv, b[:, :], ACT.Copy), "act")
                b = full(act, f"ckv_{l}", 1)
                emptied(act.activation(kr, b[0:MD, :], ACT.Copy), "act")
                for j in range(2):
                    b = full(act, f"pf_{l}", j)
                    emptied(act.activation(pf[:, j, cols], b[:, 0:n], ACT.Copy), "act")
                for j in range(8):
                    cc = cols if j < 4 else ALL
                    act.wait_ge(S("conv_sum"), 8 * l + j + 1)
                    act.activation(sq[0:MD, j * 512 + cc.start:j * 512 + cc.stop], qc[:, j, cc], ACT.Exp,
                                   scale=-1.0).then_inc(S("conv_exp"), 1)
                act.wait_ge(S("conv_done"), l + 1)
                for d in range(2):
                    act.wait_ge(S("gcol_full"), 2 * l + d + 1)
                    act.activation(gcol[:, d, :, :], bank[4 + d][:, 0:16], ACT.Copy).then_inc(S("gcol_in"), 1)
                norm(f"cq_{l}", cq[:, :, cols], sqv(2, n), P, n, 256)
                norm(f"ckv_{l}", ckv, sq[:, 0:512], P, 512, 128)
                for h in range(MH):
                    b = full(act, f"uq_{l}", h)
                    emptied(act.activation(qa[:, h, cols], b[0:MD, 0:n], ACT.Copy, scale=MD ** -0.5), "act")
                for h in range(MH):
                    b = full(act, f"kn_{l}", h)
                    emptied(act.activation(ka[0:64, h, :], b[0:64, :], ACT.Copy), "act")
                for j in range(4):
                    b = full(act, f"va_{l}", j)
                    emptied(act.activation(va[:, j, :], b[:, 0:384], ACT.Copy), "act")
                for s in range(n // T):
                    sc = slice(cols.start + s * T, cols.start + (s + 1) * T)
                    for ft in range(2):
                        b = full(act, f"fa{s}_{l}", ft)
                        emptied(act.activation(fa[:, ft, :, :], b[:, :], ACT.Copy), "act")
                    for ft in range(2):
                        b = full(act, f"fy{s}_{l}", ft)
                        emptied(act.activation(yf[:, ft, sc], b[:, 0:T], ACT.Copy), "act")
                units = range(UNIT0["mctx0"], UNIT0["mlat1"]) if l == 0 else range(UNIT0["mlat1"], len(UNITS))
                for i in range(units.start, units.stop + 1):
                    if i < units.stop:
                        softmax(i)
                    if i > units.start:
                        transposed(i - 1)

                rb = [scratch[:, d * 512:(d + 1) * 512] for d in range(2)]
                em = [scratch[0:MD, (2 + d) * 512:(3 + d) * 512] for d in range(2)]
                arg = [scratch[:, (4 + d) * 512:(5 + d) * 512] for d in range(2)]
                den = [scratch[0:MD, (6 + d) * 512:(7 + d) * 512] for d in range(2)]
                for h in range(MH):
                    g = l * MH + h
                    for d in range(2):
                        act.wait_ge(S("ml_rb"), 2 * g + d + 1)
                        if g:
                            act.wait_ge(S("ml_out"), g)
                        act.activation(rb[d][:, cols], bank[6 + d][:, cols], ACT.Copy).then_inc(S("ml_rb_in"), 1)
                    for d in range(2):
                        act.wait_ge(S("ml_em"), 2 * g + d + 1)
                        act.activation(em[d][:, cols], bank[6 + d][0:MD, cols], ACT.Exp).then_inc(S("ml_em_in"), 1)
                    for kb in range(4):
                        for d in range(2):
                            act.wait_ge(S("ml_rb_in"), 2 * g + d + 1)
                            if kb >= 2 or l == 0:
                                act.wait_ge(S("ml_arg"), ml_args(l, h, kb, d))
                            bias = gcol[:, d, kb, h:h + 1]
                            e = sq[:, (2 * (kb % 2) + d) * 512:(2 * (kb % 2) + d + 1) * 512]
                            if kb < 2:
                                if l == 0:
                                    act.activation(e[:, CTX], arg[d][:, CTX], ACT.Exp, bias=bias)
                                last = act.activation(e[:, LAT], rb[d][:, LAT], ACT.Exp, bias=bias)
                            else:
                                last = act.activation(e[:, LAT], arg[d][:, LAT], ACT.Exp, bias=bias)
                            last.then_inc(S("ml_e"), 1)
                    act.wait_ge(S("ml_v"), 4 * (g + 1))
                    for d in range(2):
                        act.activation(den[d][:, cols], bank[mlb(l, 2 * d + 1)][0:MD, cols],
                                       ACT.Abs).then_inc(S("ml_den"), 1)
                    act.wait_ge(S("ml_sum"), g + 1)
                    norm(f"head_{l}_{h}", ym[:, h, cols], sq[0:MD, 2048:2048 + n], MD, n, MD)
                wait_emptied(act, f"out_{l}", 7)
                norm(f"n2_{l}", res[:, :, cols], sqv(KT, n), P, n, D)
                shift(l, 1)
                b0, f0 = JOBS.number(f"up_{l}"), JOBS.full(JOBS.number(f"up_{l}"))
                per = 8
                with act.Fori(0, MT // per) as i:
                    for j in range(per):
                        act.wait_ge(S("job_full"), i * per + (f0 + j))
                        act.activation(hidden[:, bass.ds(i * per + j, 1), 0:n].rearrange("p a b -> p (a b)"),
                                       bank[(b0 + j) % 4][:, 0:n], ACT.Relu).then_inc(S("job_emptied_act"), 1)
            wait_emptied(act, f"dn_{NL - 1}", 7)
            norm("fin2", res[:, :, LAT], sqv(KT, T), P, T, D)

        @block.tensor
        def _(pe):
            begun = []

            def mm(*operands, **flags):
                ins = pe.matmul(*operands, **flags)
                if begun:
                    begun.clear()
                    ins.then_inc(S("slot_used"), 1)
                return ins

            def claim(phase, j=0):
                n = JOBS.number(phase, j)
                if n >= 4:
                    sem, count = JOBS.emptied(n - 4)
                    pe.wait_ge(S(sem), count)
                return bank[n % 4]

            def landed(n):
                pe.wait_ge(S(f"slot_in{n % RING}"), 16 * (n // RING + 1))
                if n:
                    begun.append(n)

            def norm(name, p, k, n):
                pe.wait_ge(S("norm_sq"), NORM[name] + 1)
                for j in range(k):
                    at = 2048 if name.startswith("head") else 0
                    last = mm(bank[7][0:p, 0:n], ones[0:p, 0:p], sq[0:p, at + j * n:at + (j + 1) * n],
                              start=(j == 0), stop=(j == k - 1))
                last.then_inc(S("norm_ms"), 1)

            def finish(ins):
                ins.then_inc(S("job_full"), 1)

            def linear256(phase, j, n, src, cols):
                b = claim(phase, j)
                landed(n)
                for m in range(2):
                    for k in range(KT):
                        last = mm(b[:, m * T:(m + 1) * T], tile(n, m * KT + k), src[:, k, cols],
                                  start=(k == 0), stop=(k == KT - 1))
                finish(last)

            def token_major(phase, j, n, src, c0):
                b = claim(phase, j)
                landed(n)
                for tb in range(TB):
                    for k in range(KT):
                        last = mm(b[:, tb * T:(tb + 1) * T], src[:, k, c0 + tb * P:c0 + (tb + 1) * P],
                                  slot(n)[:, k * T:(k + 1) * T], start=(k == 0), stop=(k == KT - 1))
                finish(last)

            pe.wait_ge(S("table_in"), 16)
            norm("mix", P, KT, T)
            norm("mem", P, KT, T)
            pe.wait_ge(S("norm_out"), NORM["mix"] + 1)
            wf = tab("w_f").rearrange("p (k f) -> p k f", k=KT)
            for k in range(KT):
                last = mm(bank[6][0:NF, 0:T], wf[:, k, :], u[:, k, LAT], start=(k == 0), stop=(k == KT - 1))
            last.then_inc(S("fox_f_full"), 1)
            for s in range(N_QK):
                linear256("qk", s, S_QK + s, u, LAT)
            for s in range(N_V):
                token_major("v", s, S_V + s, u, T)

            def scores(i):
                kind, h, q = UNITS[i]
                b = bank[4 + i % 2]
                if i >= 2:
                    pe.wait_ge(S("sm_exp"), i - 1)
                if kind == "fox":
                    r = slice((h % 2) * HD, (h % 2) * HD + HD)
                    for qb in range(TB):
                        o = b[:, qb * T:(qb + 1) * T]
                        mm(o, qk[r, h // 2, qb * P:(qb + 1) * P], qk[r, 4 + h // 2, :], start=True, stop=False)
                        mm(o, ident[0:NF, h:h + 1].to_broadcast([NF, P]), crow[:, 4, :], start=False, stop=False)
                        last = mm(o, ident, tab("m_le")[:, qb * T:(qb + 1) * T], start=False, stop=True)
                elif kind == "xat":
                    for qb in range(TB):
                        for k in range(2):
                            last = mm(b[:, qb * T:(qb + 1) * T], qx[:, 2 * h + k, qb * P:(qb + 1) * P],
                                      kx[:, 2 * h + k, :], start=(k == 0), stop=(k == 1))
                elif q is None:
                    for qb in range(TB):
                        last = mm(b[:, qb * T:(qb + 1) * T], qa[:, h, qb * P:(qb + 1) * P], ka[:, h, CTX],
                                  start=True, stop=True)
                else:
                    last = mm(b[:, :], qa[:, h, T + q * P:T + (q + 1) * P], ka[:, h, :], start=True, stop=True)
                last.then_inc(S("sm_s"), 1)

            def transposes(i):
                q = UNITS[i][2]
                pe.wait_ge(S("sm_p"), i + 1)
                if i:
                    pe.wait_ge(S("sm_pt"), i)
                for j in range(4):
                    at = j if q is not None else (j % 2) * 2 + j // 2
                    last = pe.transpose(bank[6][:, at * P:(at + 1) * P], prob[i % 2][:, j * P:(j + 1) * P], ident)
                last.then_inc(S("sm_tr"), 1)

            def weighted(i):
                kind, h, q = UNITS[i]
                pe.wait_ge(S("sm_pt"), i + 1)
                if i:
                    pe.wait_ge(S("sm_out"), i)
                pt = probT[i % 2].rearrange("p (k q) -> p k q", k=2 if q is None else 4)
                if kind == "fox":
                    r = slice((h % 2) * HD, (h % 2) * HD + HD)
                    for kb in range(TB):
                        last = mm(bank[7][r, 0:T], v1[:, kb, h * HD:(h + 1) * HD], pt[:, kb, :],
                                  start=(kb == 0), stop=(kb == TB - 1))
                elif kind == "xat":
                    for m in range(2):
                        for kb in range(TB):
                            c = h * 256 + m * P
                            last = mm(bank[7][:, m * T:(m + 1) * T], vx[:, kb, c:c + P], pt[:, kb, :],
                                      start=(kb == 0), stop=(kb == TB - 1))
                else:
                    nk, nq = (2, T) if q is None else (4, P)
                    for kb in range(nk):
                        last = mm(bank[7][0:MD, 0:nq], va[:, kb, h * MD:(h + 1) * MD], pt[:, kb, :],
                                  start=(kb == 0), stop=(kb == nk - 1))
                last.then_inc(S("sm_o"), 1)

            wait_emptied(pe, "v", N_V - 1)
            pe.wait_ge(S("fox_c"), 1)
            pe.wait_ge(S("norm_out"), NORM["mem"] + 1)
            for i in range(NF + 2):
                if i < NF:
                    scores(i)
                    if i < 4:
                        linear256("xkv", i, S_XKV + i, u, CTX)
                    else:
                        token_major("xkv", i, S_XKV + i, u, 0)
                if 1 <= i <= NF:
                    transposes(i - 1)
                if i >= 2:
                    weighted(i - 2)

            def sb_z(h, b, t_only=False):
                r = slice((h % 2) * HD, (h % 2) * HD + HD)
                return [(b[:, kb * T:(kb + 1) * T], qk[r, 12 + h // 2, kb * P:(kb + 1) * P], qk[r, 8 + h // 2, :])
                        for kb in range(TB)]

            for h in range(NF + 2):
                if h < NF:
                    if h >= 2:
                        pe.wait_ge(S("sb_softplus"), h - 1)
                    else:
                        pe.wait_ge(S("sm_exp"), NF)
                    for o, a, b in sb_z(h, bank[4 + h % 2]):
                        last = mm(o, a, b, start=True, stop=True)
                    last.then_inc(S("sb_z"), 1)
                if 1 <= h <= NF:
                    g = h - 1
                    pe.wait_ge(S("sb_log"), g + 1)
                    if g:
                        pe.wait_ge(S("sb_arg"), g)
                    else:
                        pe.wait_ge(S("sm_pt"), NF)
                    logs = sbt[g % 2][:, 1, :].rearrange("p (k t) -> p k t", k=2)
                    for kb, (o, a, b) in enumerate(sb_z(g, bank[6])):
                        mm(o, a, b, start=True, stop=False)
                        last = mm(o, tab("tri"), logs[:, kb, :], start=False, stop=(kb == 1))
                        if kb == 0:
                            last = mm(o, ones, logs[:, 1, :], start=False, stop=True)
                    last.then_inc(S("sb_t"), 1)
                if h >= 2:
                    g = h - 2
                    pe.wait_ge(S("sb_w"), g + 1)
                    if g:
                        pe.wait_ge(S("sb_out"), g)
                    else:
                        pe.wait_ge(S("sm_out"), NF)
                    r = slice((g % 2) * HD, (g % 2) * HD + HD)
                    wts = sbt[g % 2][:, 3, :].rearrange("p (k t) -> p k t", k=2)
                    for kb in range(TB):
                        last = mm(bank[7][r, 0:T], v1[:, kb, 512 + g * HD:512 + (g + 1) * HD], wts[:, kb, :],
                                  start=(kb == 0), stop=(kb == TB - 1))
                    last.then_inc(S("sb_o"), 1)
            norm("fox", P, 4, T)
            norm("sb", P, 4, T)
            pe.wait_ge(S("norm_out"), NORM["sb"] + 1)
            for s in range(4):
                linear256("out1", s, S_OUT + s, u, LAT)
            norm("xattn", P, KT, T)
            pe.wait_ge(S("norm_out"), NORM["xattn"] + 1)
            for s in range(4):
                linear256("xq", s, S_XQ + s, u, LAT)
            wait_emptied(pe, "xq", 3)
            a = UNIT0["xat"]
            for i in range(NX + 2):
                if i < NX:
                    scores(a + i)
                if 1 <= i <= NX:
                    transposes(a + i - 1)
                if i >= 2:
                    weighted(a + i - 2)
            pe.wait_ge(S("sm_out"), UNIT0["xat"] + NX)
            for s in range(4):
                linear256("xo", s, S_XO + s, heads, slice(0, T))
            norm("ffn", P, KT, T)
            pe.wait_ge(S("norm_out"), NORM["ffn"] + 1)
            wr = tab("w_route").rearrange("p (k f) -> p k f", k=KT)
            for b in range(TB):
                o = bank[6][:, b * 32:b * 32 + 20]
                mm(o, ones[0:1, :], tab("b_route", 1), start=True, stop=False)
                for k in range(KT):
                    last = mm(o, u[:, k, T + b * P:T + (b + 1) * P], wr[:, k, :], start=False, stop=(k == KT - 1))
                last.then_inc(S("rt_full"), 1)
            pe.wait_ge(S("rt_gate"), TB)
            for e in range(NE // 2):
                if e >= 2:
                    pe.wait_ge(S("gate_in"), e - 1)
                for j in range(2):
                    for b in range(TB):
                        w = 96 + 64 * b + 44 + 2 * e + j
                        last = mm(bank[4 + e % 2][:, j * T + b * P:j * T + (b + 1) * P],
                                  small[:, w:w + 1].to_broadcast([P, P]), ident, start=True, stop=True)
                last.then_inc(S("gate_full"), 1)
            for j in range(4):
                b = claim("moe_y", j)
                mm(b[:, :], zeros, table[:, 0:512], start=True, stop=False, skip_group_check=True)
            y0 = JOBS.number("moe_y")
            pe.wait_ge(S("gate_in"), NE // 2)
            pe.wait_ge(S("silu_c"), 1)
            with pe.Fori(0, NE // 2) as i:
                for e in range(2):
                    base = S_MOE + 6 * e

                    def slot_in(s):
                        n = base + s
                        pe.wait_ge(S(f"slot_in{n % RING}"), i * 48 + 16 * (n // RING + 1))
                        begun.append(n)
                        return n

                    pe.wait_ge(S("moe_hid"), i * 2 + (e + 1))
                    for s, b, name in ((0, 4, "moe_gate"), (1, 5, "moe_up")):
                        n = slot_in(s)
                        for m in range(2):
                            for k in range(KT):
                                last = mm(bank[b][:, m * T:(m + 1) * T], tile(n, m * KT + k), u[:, k, LAT],
                                          start=(k == 0), stop=(k == KT - 1))
                        last.then_inc(S(name), 1)
                    pe.wait_ge(S("mod_in"), i * 2 + (e + 1))
                    for s in range(3):
                        n = slot_in(2 + s)
                        for m in range(2):
                            for k in range(KT):
                                c = 2 * (2 * s + m)
                                last = mm(bank[6][:, c:c + 2], tile(n, m * KT + k), silu_c[:, k, :],
                                          start=(k == 0), stop=(k == KT - 1))
                    last.then_inc(S("mod_full"), 1)
                    n = slot_in(5)
                    pe.wait_ge(S("moe_hid"), i * 2 + (e + 2))
                    for m in range(KT):
                        for k in range(2):
                            last = mm(bank[(y0 + m // 2) % 4][:, (m % 2) * T:(m % 2 + 1) * T], tile(n, k * KT + m),
                                      hid[:, k, :], start=False, stop=False, skip_group_check=True)
                    last.then_inc(S("moe_down"), 1)
            norm("fin1", P, KT, T)

            for l in range(NL):
                cols = lin_cols(l)
                n = cols.stop - cols.start
                at = S_L + l * LAYER_SLOTS
                norm(f"n1_{l}", P, KT, 2 * T)
                pe.wait_ge(S("u_mod"), 2 * l + 1)
                wg = tab(f"w_g_{l}").rearrange("p (k g) -> p k g", k=KT)
                for d in range(2):
                    for g in range(2):
                        b = bank[4 + 2 * d + g]
                        for k in range(KT):
                            c = 4 * (2 * d + g)
                            last = mm(b[32 * d:32 * d + MH, :], wg[:, k, c:c + 4], u[:, k, :], start=(k == 0), stop=(k == KT - 1))
                    last.then_inc(S("ml_g_full"), 1)

                def head_tiles(phase, j, s, m, width, cc, src=u):
                    b = claim(phase, j)
                    w = cc.stop - cc.start
                    for k in range(KT):
                        last = mm(b[0:width, 0:w], tile(s, m * KT + k, width), src[:, k, cc],
                                  start=(k == 0), stop=(k == KT - 1))
                    finish(last)

                for s in range(4):
                    landed(at + s)
                    for m in range(2):
                        j = 2 * s + m
                        head_tiles(f"mqk_{l}", j, at + s, m, MD, cols if j < 4 else ALL)
                banks = [claim(f"mv_{l}", j) for j in range(4)]
                for s in range(2):
                    landed(at + 4 + s)
                    for tb in range(4):
                        for k in range(4):
                            last = mm(banks[tb][:, 0:384], u[:, 4 * s + k, tb * P:(tb + 1) * P],
                                      slot(at + 4 + s)[:, k * 384:(k + 1) * 384],
                                      start=(s == 0 and k == 0), stop=(s == 1 and k == 3))
                        if s == 1:
                            finish(last)
                for s in range(2):
                    landed(at + 6 + s)
                    for m in range(2):
                        head_tiles(f"mo_{l}", 2 * s + m, at + 6 + s, m, MD, cols)
                landed(at + 8)
                for m in range(2):
                    head_tiles(f"cq_{l}", m, at + 8, m, P, cols)
                landed(at + 9)
                head_tiles(f"ckv_{l}", 0, at + 9, 0, P, ALL)
                head_tiles(f"ckv_{l}", 1, at + 9, 1, MD, ALL)
                landed(at + 10)
                for m in range(2):
                    head_tiles(f"pf_{l}", m, at + 10, m, P, cols)
                for d in range(2):
                    pe.wait_ge(S("ml_rows"), 2 * l + d + 1)
                    for kb in range(4):
                        last = mm(bank[4 + d][:, kb * MH:(kb + 1) * MH], rows[d][:, 0, kb * P:(kb + 1) * P],
                                  row_ident[d], start=True, stop=True)
                    last.then_inc(S("gcol_full"), 1)
                norm(f"cq_{l}", P, 2, n)
                norm(f"ckv_{l}", P, 1, 512)
                pe.wait_ge(S("norm_out"), NORM[f"ckv_{l}"] + 1)
                uq = tab(f"uq_{l}").rearrange("p (k c) -> p k c", k=2)
                for h in range(MH):
                    b = claim(f"uq_{l}", h)
                    for k in range(2):
                        last = mm(b[0:MD, 0:n], uq[:, k, h * MD:(h + 1) * MD], cq[:, k, cols],
                                  start=(k == 0), stop=(k == 1))
                    finish(last)
                for h in range(MH + 1):
                    b = claim(f"rot_{l}", h)
                    if h < MH:
                        wait_emptied(pe, f"uq_{l}", h)
                    src = qa[:, h, LAT] if h < MH else kr[:, LAT]
                    finish(mm(b[0:MD, 0:T], tab("rot", MD), src, start=True, stop=True))
                ukv = tab(f"ukv_{l}")
                for h in range(MH):
                    b = claim(f"kn_{l}", h)
                    finish(mm(b[0:64, :], ukv[:, h * 64:(h + 1) * 64], ckv, start=True, stop=True))
                for j in range(4):
                    b = claim(f"va_{l}", j)
                    finish(mm(b[:, 0:384], ckv[:, j * P:(j + 1) * P], ukv[:, 256:640], start=True, stop=True))
                cn = tab("cn").rearrange("p (b n) -> p b n", b=2)
                sn = tab("sn").rearrange("p (b n) -> p b n", b=2)
                for s in range(n // T):
                    c0 = cols.start + s * T
                    for ft in range(2):
                        b = claim(f"fa{s}_{l}", ft)
                        wait_emptied(pe, f"pf_{l}", ft)
                        for nb in range(TB):
                            last = mm(b[:, nb * T:(nb + 1) * T], pf[:, ft, c0 + nb * P:c0 + (nb + 1) * P],
                                      tab("cdsd"), start=True, stop=True)
                        finish(last)
                    for ft in range(2):
                        b = claim(f"fy{s}_{l}", ft)
                        wait_emptied(pe, f"fa{s}_{l}", ft)
                        for nb in range(TB):
                            mm(b[:, 0:T], fa[:, ft, nb, 0:P], cn[:, nb, :], start=(nb == 0), stop=False)
                            last = mm(b[:, 0:T], fa[:, ft, nb, P:2 * P], sn[:, nb, :], start=False, stop=(nb == 1))
                        finish(last)
                pe.wait_ge(S("mla_keys"), l + 1)
                wait_emptied(pe, f"kn_{l}", MH - 1)
                wait_emptied(pe, f"va_{l}", 3)
                units = range(UNIT0["mctx0"], UNIT0["mlat1"]) if l == 0 else range(UNIT0["mlat1"], len(UNITS))
                for i in range(units.start, units.stop + 2):
                    if i < units.stop:
                        scores(i)
                    if units.start < i <= units.stop:
                        transposes(i - 1)
                    if i >= units.start + 2:
                        weighted(i - 2)
                pe.wait_ge(S("sm_out"), units.stop)
                pe.wait_ge(S("norm_out"), NORM[f"ckv_{l}"] + 1)
                for h in range(MH):
                    g = l * MH + h
                    for what, name in ((3, "ml_rb"), (4, "ml_em")):
                        m = P if what == 3 else MD
                        for d in range(2):
                            if what == 3 and g:
                                pe.wait_ge(S("norm_out"), NORM[f"head_{l}_{h - 1}"] + 1 if h else 1)
                            if what == 4:
                                pe.wait_ge(S("ml_rb_in"), 2 * g + d + 1)
                            mm(bank[6 + d][0:m, cols], row_ident[d][:, h:h + 1].to_broadcast([MH, m]),
                               rows[d][:, what, cols], start=True, stop=True).then_inc(S(name), 1)

                    def keys(kb):
                        kk = 4 * g + kb
                        if kb >= 2:
                            pe.wait_ge(S("ml_p"), kk - 1)
                        tc = cols if kb < 2 else LAT
                        mm(bank[4 + kb % 2][:, tc], qc[:, 4 + h, kb * P:(kb + 1) * P], qc[:, h, tc],
                           start=True, stop=True).then_inc(S("ml_s"), 1)

                    def values(kb):
                        kk = 4 * g + kb
                        pe.wait_ge(S("ml_p"), kk + 1)
                        tc = cols if kb < 2 else LAT
                        for d in range(2):
                            p = sq[:, (2 * (kb % 2) + d) * 512:(2 * (kb % 2) + d + 1) * 512]
                            mm(bank[mlb(l, 2 * d)][0:MD, tc], mv[:, kb, h * MD:(h + 1) * MD], p[:, tc],
                               start=(kb == 0), stop=(kb == 3), skip_group_check=True)
                            last = mm(bank[mlb(l, 2 * d + 1)][0:MD, tc], ones[:, 0:MD], p[:, tc],
                                      start=(kb == 0), stop=(kb == 3), skip_group_check=True)
                        last.then_inc(S("ml_v"), 1)

                    keys(0)
                    keys(1)
                    if h == 0:
                        for j in range(4):
                            claim(f"mlstm_{l}", j)
                    else:
                        pe.wait_ge(S("ml_sum"), g)
                    values(0)
                    keys(2)
                    values(1)
                    keys(3)
                    values(2)
                    values(3)
                    norm(f"head_{l}_{h}", MD, 1, n)
                pe.wait_ge(S("ml_out"), l * MH + MH)
                srcs = [(yf[:, j, cols], P) for j in range(2)] + [(ym[:, j, cols], MD) for j in range(MH)] \
                    + [(ya[:, j, cols], MD) for j in range(MH)]
                s = at + N_IN2
                held = None
                for m in range(KT):
                    b = claim(f"out_{l}", m)
                    for k, (src, nr) in enumerate(srcs):
                        t = m * len(srcs) + k
                        if t % 16 == 0:
                            landed(s + t // 16)
                        last = mm(b[:, 0:n], ring[0:nr, (s + t // 16) % RING, (t % 16) * P:(t % 16 + 1) * P], src,
                                  start=(k == 0), stop=(k == len(srcs) - 1))
                    finish(last)
                norm(f"n2_{l}", P, KT, n)
                pe.wait_ge(S("u_mod"), 2 * l + 2)
                s0 = at + N_IN2 + N_OUT2
                b0 = JOBS.number(f"up_{l}")
                e_dve, e_act = JOBS.emptied(b0 - 1)[1], JOBS.emptied(b0)[1]
                with pe.Fori(0, N_UP // RING) as i:
                    for s in range(RING):
                        pe.wait_ge(S(f"slot_in{(s0 + s) % RING}"), i * 16 + 16 * ((s0 + s) // RING + 1))
                        begun.append(s)
                        for m in range(2):
                            j = 2 * s + m
                            if j < 4:
                                pe.wait_ge(S("job_emptied_dve"), e_dve - 3 + j)
                            pe.wait_ge(S("job_emptied_act"), i * 8 + (e_act - 1 + j - 3 if j >= 3 else e_act - 4 + j))
                            for k in range(KT):
                                last = mm(bank[(b0 + j) % 4][:, 0:n], tile(s0 + s, m * KT + k), u[:, k, cols],
                                          start=(k == 0), stop=(k == KT - 1))
                            last.then_inc(S("job_full"), 1)
                s0 += N_UP
                b0 = JOBS.number(f"dn_{l}")
                e_dve = JOBS.emptied(b0)[1]
                pe.wait_ge(S("hidden"), 32 * (l + 1))
                with pe.Fori(0, N_DN // RING // 1) as i:
                    for m in range(2):
                        for half in range(2):
                            s = 2 * m + half
                            pe.wait_ge(S(f"slot_in{(s0 + s) % RING}"), i * 16 + 16 * ((s0 + s) // RING + 1))
                            begun.append(s)
                            if half == 0:
                                pe.wait_ge(S("job_emptied_dve"), i * 2 + (e_dve - 2 + m))
                            for k in range(16):
                                last = mm(bank[(b0 + m) % 4][:, 0:n], tile(s0 + s, k), hidden[:, half * 16 + k, 0:n],
                                          start=(half == 0 and k == 0), stop=(half == 1 and k == 15))
                        last.then_inc(S("job_full"), 1)
            norm("fin2", P, KT, T)

        @block.vector
        def _(dve):
            ch = Chain(dve, "dve_step")
            tt, ts, stt = dve.tensor_tensor, dve.tensor_scalar, dve.scalar_tensor_tensor

            def norm(name, parts, after=None):
                dve.wait_ge(S("norm_rstd"), NORM[name] + 1)
                for o, src, g, r in parts:
                    last = stt(o, src, g, r, ALU.mult, ALU.mult)
                last.then_inc(S("norm_out"), 1)

            def tiles(dst, src, gain, k, dcols, scols):
                g = tab(gain)
                return [(dst[:, j, dcols], src[:, j, scols], g[:, j:j + 1], rstd[:, 0:T]) for j in range(k)]

            def smv(i, what, k, w=1):
                a = (i % 2) * 8 + what * 2 + k
                return small[:, a:a + w]

            def neg_max(i):
                g = 1 if UNITS[i][2] is not None else 2
                dve.wait_ge(S("sm_s"), i + 1)
                b = bank[4 + i % 2][:, :].rearrange("p (g w) -> p g w", g=g)
                dve.tensor_reduce(smv(i, 0, 0, g), b, AX_X, ALU.max, negate=True).then_inc(S("sm_max"), 1)

            def divide(i):
                g = 1 if UNITS[i][2] is not None else 2
                w = 512 // g
                dve.wait_ge(S("sm_exp"), i + 1)
                ch.link(dve.reciprocal(smv(i, 1, 0, g), smv(i, 2, 0, g)))
                for k in range(g):
                    p = prob[i % 2][:, k * w:(k + 1) * w]
                    last = ts(p, p, smv(i, 1, k), None, ALU.mult)
                last.then_inc(S("sm_p"), 1)

            def out_of(i):
                kind, h, q = UNITS[i]
                dve.wait_ge(S("sm_o"), i + 1)
                if kind == "fox":
                    r = slice((h % 2) * HD, (h % 2) * HD + HD)
                    last = dve.tensor_copy(heads[r, h // 2, :], bank[7][r, 0:T])
                elif kind == "xat":
                    last = dve.tensor_copy(heads[:, 2 * h:2 * h + 2, :],
                                           bank[7][:, :].rearrange("p (a t) -> p a t", a=2))
                elif q is None:
                    last = dve.tensor_copy(ya[:, h, CTX], bank[7][0:MD, 0:T])
                else:
                    last = dve.tensor_copy(ya[:, h, T + q * P:T + (q + 1) * P], bank[7][0:MD, 0:P])
                last.then_inc(S("sm_out"), 1)

            def softmax_units(first, count):
                for i in range(first, first + count + 2):
                    if i < first + count:
                        neg_max(i)
                    if i < first + count:
                        divide(i)
                    if i >= first + 2:
                        out_of(i - 2)

            dve.wait_ge(S("c_exp"), 1)
            ch.link(ts(small[:, 64:80], small[:, 64:80], 1.0, None, ALU.add))
            ch.link(dve.reciprocal(small[:, 64:80], small[:, 64:80]))
            tt(silu_c[:, :, :].rearrange("p k c -> p (k c)"), small[:, 64:80], tab("c"),
               ALU.mult).then_inc(S("silu_c"), 1)
            norm("mix", tiles(u, res, "g_mix", KT, LAT, LAT))
            norm("mem", tiles(u, res, "g_mem", KT, CTX, CTX))
            dve.wait_ge(S("fox_f_full"), 1)
            ts(crow[:, 0, :], bank[6][0:NF, 0:T], tab("b_forget", NF), None, ALU.add).then_inc(S("fox_f"), 1)
            dve.wait_ge(S("fox_ln"), 1)
            ch.link(stt(crow[:, 2, :], crow[:, 0, :], 0.0, crow[:, 1, :], ALU.min, ALU.subtract))
            ch.link(dve.tensor_tensor_scan(out=crow[:, 3, :], data0=crow[:, 2, :], data1=crow[:, 2, :], initial=0.0,
                                           op0=ALU.add, op1=ALU.bypass))
            ts(crow[:, 4, :], crow[:, 3, :], -1.0, None, ALU.mult).then_inc(S("fox_c"), 1)
            softmax_units(0, NF)

            for h in range(NF + 2):
                if h < NF:
                    t = sbt[h % 2]
                    dve.wait_ge(S("sb_ln"), h + 1)
                    stt(t[:, 1, :], bank[4 + h % 2][:, :], 0.0, t[:, 0, :], ALU.max,
                        ALU.add).then_inc(S("sb_softplus"), 1)
                if 1 <= h <= NF:
                    g = h - 1
                    dve.wait_ge(S("sb_t"), g + 1)
                    tt(sbt[g % 2][:, 2, :], bank[6][:, :], tab("m_gt"), ALU.add).then_inc(S("sb_arg"), 1)
                if h >= 2:
                    g = h - 2
                    r = slice((g % 2) * HD, (g % 2) * HD + HD)
                    dve.wait_ge(S("sb_o"), g + 1)
                    dve.tensor_copy(heads[r, 4 + g // 2, :], bank[7][r, 0:T]).then_inc(S("sb_out"), 1)
            g = tab("g_fox")
            norm("fox", [(u[:, j, LAT], heads[:, j, :], g[:, j:j + 1], rstd[:, 0:T]) for j in range(4)])
            g2 = tab("g_sb")
            norm("sb", [(u[:, 4 + j, LAT], heads[:, 4 + j, :], g2[:, j:j + 1], rstd[:, 0:T]) for j in range(4)])

            def add_to_res(phase):
                for s in range(4):
                    b = full(dve, phase, s)
                    r = res[:, 2 * s:2 * s + 2, LAT]
                    emptied(tt(r, b[:, :].rearrange("p (a t) -> p a t", a=2), r, ALU.add), "dve")

            add_to_res("out1")
            norm("xattn", tiles(u, res, "g_xattn", KT, LAT, LAT))
            softmax_units(UNIT0["xat"], NX)
            add_to_res("xo")
            norm("ffn", tiles(u, res, "g_ffn", KT, LAT, LAT))

            def first_of(dst, src, best, tmp):
                ch.link(ts(tmp, src, best, None, ALU.is_ge))
                ch.link(tt(tmp, tmp, tab("w4"), ALU.mult))
                ch.link(dve.tensor_reduce(tmp1, tmp, AX_X, ALU.max))
                ch.link(ts(dst, tmp, tmp1, None, ALU.is_equal))

            for b in range(TB):
                r = small[:, 96 + 64 * b:160 + 64 * b]
                tmp1 = r[:, 28:29]
                ones_g, in_g, best, oh1, oh2 = r[:, 32:36], r[:, 36:40], r[:, 29:30], r[:, 40:44], r[:, 60:64]
                tmp = small[:, 80:84]
                dve.wait_ge(S("rt_full"), TB)
                ch.link(dve.tensor_copy(r[:, 0:20], bank[6][:, b * 32:b * 32 + 20]))
                ch.link(dve.tensor_reduce(best, r[:, 0:4], AX_X, ALU.max))
                ts(r[:, 20:21], best, -1.0, None, ALU.mult).then_inc(S("rt_max"), 1)
                first_of(ones_g, r[:, 0:4], best, tmp)
                ch.link(ts(in_g, r[:, 4:8], ones_g[:, 0:1], None, ALU.mult))
                for g in range(1, 4):
                    ch.link(stt(in_g, r[:, 4 + 4 * g:8 + 4 * g], ones_g[:, g:g + 1], in_g, ALU.mult, ALU.add))
                m1, m2 = small[:, 84:85], small[:, 85:86]
                ch.link(dve.tensor_reduce(m1, in_g, AX_X, ALU.max))
                first_of(oh1, in_g, m1, tmp)
                ch.link(stt(in_g, oh1, BIG, in_g, ALU.mult, ALU.add))
                ch.link(dve.tensor_reduce(m2, in_g, AX_X, ALU.max))
                tt(r[:, 23:24], m2, m1, ALU.subtract).then_inc(S("rt_diff"), 1)
                first_of(small[:, 88:92], in_g, m2, tmp)
                dve.wait_ge(S("rt_exp2"), b + 1)
                wa, wb = small[:, 92:93], small[:, 93:94]
                ch.link(ts(wa, r[:, 22:23], 1.0, r[:, 21:22], ALU.add, ALU.mult))
                ch.link(dve.reciprocal(wa, wa))
                ch.link(tt(wb, wa, r[:, 22:23], ALU.mult))
                ch.link(ts(tmp, small[:, 88:92], wb, None, ALU.mult))
                ch.link(stt(tmp, oh1, wa, tmp, ALU.mult, ALU.add))
                for g in range(4):
                    last = ts(r[:, 44 + 4 * g:48 + 4 * g], tmp, ones_g[:, g:g + 1], None, ALU.mult)
                last.then_inc(S("rt_gate"), 1)

            bmod = tab("b_mod")
            dve.wait_ge(S("gate_in"), NE // 2)
            dve.memset(hid[:, :, :], 0.0).then_inc(S("moe_hid"), 1)
            dve.memset(modv[:, 0:12], 0.0).then_inc(S("mod_in"), 1)
            with dve.Fori(0, NE) as e:
                ch.loop(e, 4)
                dve.wait_ge(S("moe_exp"), e + 1)
                ch.link(ts(eg, eg, 1.0, None, ALU.add))
                ch.link(dve.reciprocal(eg, eg))
                ch.link(tt(eg, bank[4][:, :], eg, ALU.mult))
                for k in range(2):
                    e_k = eg[:, k * T:(k + 1) * T]
                    last = tt(e_k, e_k, gates[:, bass.ds(e, 1), :].rearrange("p a t -> p (a t)"), ALU.mult)
                ch.link(last)
                dve.wait_ge(S("moe_up"), e + 1)
                tt(hid[:, :, :].rearrange("p a t -> p (a t)"), bank[5][:, :], eg, ALU.mult).then_inc(S("moe_hid"), 1)
                dve.wait_ge(S("mod_full"), e + 1)
                tt(modv[:, bass.ds(e * 12, 12)], bank[6][:, 0:12], bmod[:, bass.ds(e * 12, 12)],
                   ALU.add).then_inc(S("mod_in"), 1)
            ch.end(NE)
            for s in range(4):
                if s == 0:
                    dve.wait_ge(S("moe_down"), NE)
                b = bank[JOBS.number("moe_y", s) % 4]
                r = res[:, 2 * s:2 * s + 2, LAT]
                last = tt(r, b[:, :].rearrange("p (a t) -> p a t", a=2), r, ALU.add)
                emptied(last, "dve")
            dve.wait_ge(S("mod_in"), NE + 1)
            for l in range(NL):
                for k2 in range(2):
                    at = 2 * (l * 48 + 8 + 24 * k2)
                    ch.link(stt(gmod[:, 2 * l + k2, :], modv[:, at:at + 16], 1.0, tab(f"g{k2 + 1}_{l}"),
                                ALU.add, ALU.mult))
            norm("fin1", tiles(res, res, "g_fin1", KT, LAT, LAT))

            def norm_mod(l, k2):
                g = gmod[:, 2 * l + k2, :]
                parts = []
                off = 0 if (k2 == 0 or l == 0) else T
                for k in range(KT):
                    for which, cols in ((0, LAT), (1, CTX)):
                        if off and which:
                            continue
                        parts.append((u[:, k, cols], res[:, k, cols], g[:, 2 * k + which:2 * k + which + 1],
                                      rstd[:, cols.start - off:cols.stop - off]))
                norm(f"n{k2 + 1}_{l}", parts)

            def gated_add(phase, l, m, b, chunk):
                for which, cols in ((1, CTX), (0, LAT)):
                    if l and which:
                        continue
                    at = 2 * (l * 48 + 8 * chunk + m) + which
                    src = b[:, cols] if l == 0 else b[:, 0:T]
                    last = stt(res[:, m, cols], src, modv[:, at:at + 1], res[:, m, cols], ALU.mult, ALU.add)
                return last

            dve.wait_ge(S("norm_out"), NORM["fin1"] + 1)
            for l in range(NL):
                cols = lin_cols(l)
                n = cols.stop - cols.start
                norm_mod(l, 0)
                bg = tab(f"b_g_{l}")
                for d in range(2):
                    dve.wait_ge(S("ml_g_full"), 2 * l + d + 1)
                    rr = rows[d]
                    if l:
                        dve.wait_ge(S("ml_em"), 2 * MH * l)
                    ts(rr[:, 0, :], bank[4 + 2 * d][32 * d:32 * d + MH, :], bg[32 * d:32 * d + MH, 2 * d:2 * d + 1], None, ALU.add)
                    ts(rr[:, 1, :], bank[5 + 2 * d][32 * d:32 * d + MH, :], bg[32 * d:32 * d + MH, 2 * d + 1:2 * d + 2], None,
                       ALU.add).then_inc(S("ml_f"), 1)
                    dve.wait_ge(S("ml_f"), 2 * l + d + 1)
                if l == 0:
                    dve.memset(qkp[:, :, :, 0:2], 0.0)
                    ch.link(dve.memset(qkp[:, :, :, 258:260], 0.0))
                else:
                    ch.link(dve.memset(qkp[:, :, :, 0:2], 0.0))
                    ch.link(dve.memset(qkp[:, :, :, 258:260], 0.0))
                for d in range(2):
                    rr = rows[d]
                    dve.wait_ge(S("ml_ln"), 2 * l + d + 1)
                    ch.link(stt(rr[:, 1, :], rr[:, 1, :], 0.0, rr[:, 2, :], ALU.min, ALU.subtract))
                    if d == 0:
                        runs = [(slice(0, 512), 0.0)]
                    else:
                        runs = [(slice(255, None, -1), None), (slice(511, 255, -1), 0)]

                    def scan(dst, src, op):
                        for r, init in runs:
                            init = rr[:, dst, 0:1] if init == 0 and d else 0.0
                            ch.link(dve.tensor_tensor_scan(out=rr[:, dst, r], data0=rr[:, src, r],
                                                           data1=rr[:, src, r], initial=init, op0=op,
                                                           op1=ALU.bypass))

                    scan(2, 1, ALU.add)
                    ch.link(tt(rr[:, 0, :], rr[:, 0, :], rr[:, 2, :], ALU.subtract))
                    scan(3, 0, ALU.max)
                    ch.link(stt(rr[:, 4, :], rr[:, 2, :], -1.0, rr[:, 3, :], ALU.mult, ALU.subtract))
                    ts(rr[:, 3, :], rr[:, 3, :], -1.0, None, ALU.mult).then_inc(S("ml_rows"), 1)
                taps = tab(f"conv_{l}", MD).rearrange("p (h t) -> p h t", h=8)
                for j in range(8):
                    wait_emptied(dve, f"mqk_{l}", j)
                    segs = slice(0, 2) if (l == 0 or j >= 4) else slice(1, 2)
                    cc = cols if j < 4 else ALL
                    o = qc[:, j, cc].rearrange("p (s t) -> p s t", t=T)
                    ch.link(ts(o, qkp[:, j, segs, 0:T], taps[:, j, 0:1], None, ALU.mult))
                    for t in range(1, 5):
                        last = stt(o, qkp[:, j, segs, t:t + T], taps[:, j, t:t + 1], o, ALU.mult, ALU.add)
                        if t < 4:
                            ch.link(last)
                    last.then_inc(S("conv_sum"), 1)
                for j in range(8):
                    cc = cols if j < 4 else ALL
                    e = sq[0:MD, j * 512 + cc.start:j * 512 + cc.stop]
                    dve.wait_ge(S("conv_exp"), 8 * l + j + 1)
                    ch.link(ts(e, e, 1.0, None, ALU.add))
                    ch.link(dve.reciprocal(e, e))
                    last = stt(qc[:, j, cc], qc[:, j, cc], MD ** -0.5 if j < 4 else 1.0, e, ALU.mult, ALU.mult)
                last.then_inc(S("conv_done"), 1)
                wait_emptied(dve, f"mo_{l}", 3)
                ch.link(ts(mo[:, :, cols], mo[:, :, cols], 1.0, None, ALU.add))
                ch.link(dve.reciprocal(mo[:, :, cols], mo[:, :, cols]))
                g = tab(f"g_qn_{l}")
                norm(f"cq_{l}", [(cq[:, j, cols], cq[:, j, cols], g[:, j:j + 1], rstd[:, 0:n]) for j in range(2)])
                norm(f"ckv_{l}", [(ckv, ckv, tab(f"g_kvn_{l}"), rstd[:, :])])
                for h in range(MH + 1):
                    b = full(dve, f"rot_{l}", h)
                    o = qa[:, h, LAT] if h < MH else kr[:, LAT]
                    t1 = scratch[0:MD, h * 256:(h + 1) * 256]
                    ch.link(tt(t1, b[0:MD, 0:T], tab("sin", MD), ALU.mult))
                    ch.link(tt(o, o, tab("cos", MD), ALU.mult))
                    last = tt(o, o, t1, ALU.add)
                    emptied(last, "dve")
                dve.wait_ge(S("job_emptied_dve"), JOBS.emptied(JOBS.number(f"rot_{l}", MH))[1])
                for h in range(MH):
                    last = dve.tensor_copy(ka[64:96, h, :], kr[64:96, :])
                last.then_inc(S("mla_keys"), 1)
                units = range(UNIT0["mctx0"], UNIT0["mlat1"]) if l == 0 else range(UNIT0["mlat1"], len(UNITS))
                softmax_units(units.start, len(units))

                rb = [scratch[:, d * 512:(d + 1) * 512] for d in range(2)]
                em = [scratch[0:MD, (2 + d) * 512:(3 + d) * 512] for d in range(2)]
                arg = [scratch[:, (4 + d) * 512:(5 + d) * 512] for d in range(2)]
                den = [scratch[0:MD, (6 + d) * 512:(7 + d) * 512] for d in range(2)]
                masks = [tab("m_ge"), tab("m_le")]
                gm = tab(f"g_ml_{l}", MD)
                for h in range(MH):
                    g = l * MH + h

                    def args(kb):
                        for d in range(2):
                            kk = 2 * (4 * g + kb) + d
                            if kk >= 2:
                                dve.wait_ge(S("ml_e"), kk - 1)
                            tc = CTX if kb < 2 else LAT
                            if kb < 2 and l:
                                continue
                            m = masks[d][:, (kb % 2) * T:(kb % 2 + 1) * T]
                            tt(arg[d][:, tc], rb[d][:, tc], m, ALU.add).then_inc(S("ml_arg"), 1)

                    dve.wait_ge(S("ml_rb_in"), 2 * g + 2)
                    args(0)
                    for kb in range(4):
                        kk = 4 * g + kb
                        tc = cols if kb < 2 else LAT
                        dve.wait_ge(S("ml_s"), kk + 1)
                        for d in range(2):
                            e = sq[:, (2 * (kb % 2) + d) * 512:(2 * (kb % 2) + d + 1) * 512]
                            dve.wait_ge(S("ml_e"), 2 * kk + d + 1)
                            last = tt(e[:, tc], e[:, tc], bank[4 + kb % 2][:, tc], ALU.mult)
                        last.then_inc(S("ml_p"), 1)
                        if kb == 0:
                            args(1)
                        elif kb < 3:
                            dve.wait_ge(S("ml_v"), kk)
                            args(kb + 1)
                    dve.wait_ge(S("ml_den"), 2 * g + 2)
                    dve.wait_ge(S("ml_em_in"), 2 * g + 2)
                    for d in range(2):
                        ch.link(tt(den[d][:, cols], den[d][:, cols], em[d][:, cols], ALU.max))
                        ch.link(dve.reciprocal(den[d][:, cols], den[d][:, cols]))
                        ch.link(tt(den[d][:, cols], bank[mlb(l, 2 * d)][0:MD, cols], den[d][:, cols], ALU.mult))
                    tt(ym[:, h, cols], den[0][:, cols], den[1][:, cols], ALU.add).then_inc(S("ml_sum"), 1)
                    norm(f"head_{l}_{h}", [(ym[:, h, cols], ym[:, h, cols], gm[:, h:h + 1], rstd[0:MD, 0:n])])
                    dve.wait_ge(S("norm_out"), NORM[f"head_{l}_{h}"] + 1)
                    tt(ym[:, h, cols], ym[:, h, cols], mo[:, h, cols], ALU.mult).then_inc(S("ml_out"), 1)
                for m in range(KT):
                    b = full(dve, f"out_{l}", m)
                    emptied(gated_add("out", l, m, b, 2), "dve")
                norm_mod(l, 1)
                b0 = JOBS.emptied(JOBS.number(f"up_{l}"))[1]
                with dve.Fori(0, MT) as i:
                    dve.wait_ge(S("job_emptied_act"), i + b0)
                    hrow = hidden[:, bass.ds(i, 1), 0:n].rearrange("p a b -> p (a b)")
                    tt(hrow, hrow, hrow, ALU.mult).then_inc(S("hidden"), 1)
                b0, f0 = JOBS.number(f"dn_{l}"), JOBS.full(JOBS.number(f"dn_{l}"))
                with dve.Fori(0, KT // 2) as i:
                    for j in range(2):
                        dve.wait_ge(S("job_full"), i * 2 + (f0 + j))
                        for which, cc in ((1, CTX), (0, LAT)):
                            if l and which:
                                continue
                            at = 2 * (l * 48 + 40 + j) + which
                            src = bank[(b0 + j) % 4][:, cc] if l == 0 else bank[(b0 + j) % 4][:, 0:T]
                            r = res[:, bass.ds(i * 2 + j, 1), cc].rearrange("p a b -> p (a b)")
                            last = stt(r, src, modv[:, bass.ds(i * 4 + at, 1)], r, ALU.mult, ALU.add)
                        last.then_inc(S("job_emptied_dve"), 1)
            norm("fin2", tiles(res, res, "g_fin2", KT, LAT, LAT))


def pack(inputs):
    f = {k: np.asarray(v) for k, v in inputs.items()}

    def tiles_fm(w, cols):
        k = w.shape[0] // P
        out = []
        for group in cols:
            t = np.zeros((P, 16, P), np.float32)
            for m, c in enumerate(group):
                width = len(c)
                t[:, m * k:(m + 1) * k, 0:width] = w[:, c].reshape(k, P, width).transpose(1, 0, 2)
            out.append(t.reshape(P, SLOT))
        return out

    def fm(w, c0, c1, width=P):
        starts = list(range(c0, c1, width))
        return tiles_fm(w, [[list(range(a, a + width)) for a in starts[i:i + 2]] for i in range(0, len(starts), 2)])

    def tm(w, c0, c1):
        return [w[:, c:c + T].reshape(KT, P, T).transpose(1, 0, 2).reshape(P, SLOT) for c in range(c0, c1, T)]

    w = f["w_in"][0]
    slots = fm(w, 0, 1024) + fm(w, 1536, 2560) + tm(w, 1024, 1536) + tm(w, 2560, 3072)
    slots += fm(f["w_xkv"][0], 0, 1024) + tm(f["w_xkv"][0], 1024, 2048)
    slots += fm(f["w_out"][0], 0, 1024) + fm(f["w_xq"][0], 0, 1024) + fm(f["w_xo"][0], 0, 1024)
    mods = [s for l in range(NL) for s in fm(f["w_mod_2"][l], 0, 6 * D)]
    for e in range(NE):
        slots += fm(f["w_exp_gate"][0, e], 0, 256) + fm(f["w_exp_up"][0, e], 0, 256) + mods[3 * e:3 * e + 3]
        slots.append(f["w_exp_down"][0, e].reshape(2, P, D).transpose(1, 0, 2).reshape(P, SLOT))
    for l in range(NL):
        w = f["w_in_2"][l]
        slots += fm(w, 256, 256 + 768, MD)
        wv = w[:, 1024:1408].reshape(2, 4, P, 384).transpose(0, 2, 1, 3).reshape(2, P, 1536)
        for s in range(2):
            t = np.zeros((P, SLOT), np.float32)
            t[:, 0:1536] = wv[s]
            slots.append(t)
        slots += fm(w, 1408, 1792, MD) + fm(w, 1808, 2064)
        t = np.zeros((P, 16, P), np.float32)
        t[:, 0:8, :] = w[:, 2064:2192].reshape(KT, P, P).transpose(1, 0, 2)
        t[:, 8:16, 64:96] = w[:, 2192:2224].reshape(KT, P, RD).transpose(1, 0, 2)
        slots.append(t.reshape(P, SLOT))
        slots += fm(w, 0, 256)
        wo = f["w_out_2"][l]
        t = np.zeros((P, 80, P), np.float32)
        rows = [(0, P), (P, P)] + [(256 + MD * j, MD) for j in range(8)]
        for m in range(KT):
            for k, (r0, nr) in enumerate(rows):
                t[0:nr, m * 10 + k, :] = wo[r0:r0 + nr, m * P:(m + 1) * P]
        slots += [t[:, 16 * s:16 * s + 16].reshape(P, SLOT) for s in range(5)]
        slots += fm(f["w_up_2"][l], 0, FF)
        wd = f["w_down_2"][l].reshape(2, 16, P, KT, P).transpose(3, 0, 2, 1, 4).reshape(16, P, SLOT)
        slots += list(wd)
    stream = np.stack(slots)
    assert stream.shape == (N_SLOTS, P, SLOT), stream.shape

    table = np.zeros((P, N_COLS), np.float32)

    def put(name, a, rows=P):
        c, n = COL[name]
        table[0:rows, c:c + n] = a.reshape(rows, n)

    def cols_of(g, k=KT):
        return g.reshape(k, P).transpose(1, 0)

    p = np.arange(P)
    t = np.arange(T)
    key = (p[:, None] + P * np.arange(2)[None, :])[:, :, None]
    put("ident", np.eye(P, dtype=np.float32))
    put("ones", np.ones((P, P), np.float32))
    put("tri", (p[:, None] >= p[None, :]).astype(np.float32))
    put("m_le", np.where(t <= key, 0.0, BIG))
    put("m_ge", np.where(t >= key, 0.0, BIG))
    put("m_gt", np.where(t > key, 0.0, BIG))
    put("neg01", np.where(t > key, -1.0, 0.0))
    a64 = 2 * np.pi * ((np.arange(64)[:, None] * np.arange(64)[None, :]) % 64) / 64
    cd = np.kron(np.eye(2), np.cos(a64))
    sd = np.kron(np.eye(2), np.sin(a64))
    put("cdsd", np.concatenate([cd, sd], 1) / 128.0)
    a256 = 2 * np.pi * ((t[:, None] * t[None, :]) % T) / T
    put("cn", np.cos(a256).reshape(2, P, T).transpose(1, 0, 2))
    put("sn", (-np.sin(a256)).reshape(2, P, T).transpose(1, 0, 2))
    nf = RD // 4
    freqs = (np.float32(10000.0) ** (-np.arange(nf, dtype=np.float32) / np.float32(nf))).astype(np.float32)
    ang = np.zeros((RD, T), np.float32)
    rot = np.zeros((MD, MD), np.float32)
    for axis in range(2):
        pos = (t // 64 if axis == 0 else t % 64).astype(np.float32)
        for half in range(2):
            for i in range(nf):
                r = axis * 16 + half * 8 + i
                ang[r] = pos * freqs[i]
                other = axis * 16 + (1 - half) * 8 + i
                rot[64 + other, 64 + r] = -1.0 if half == 0 else 1.0
    cos, sin = np.ones((MD, T)), np.zeros((MD, T))
    cos[64:], sin[64:] = np.cos(ang.astype(np.float64)), np.sin(ang.astype(np.float64))
    put("cos", cos, MD)
    put("sin", sin, MD)
    put("rot", rot, MD)
    put("w4", np.tile(np.arange(4, 0, -1), (P, 1)))
    put("eps", np.full((P, 1), EPS))
    for name, key_ in (("g_mix", "norm_mix"), ("g_xattn", "norm_xattn"), ("g_mem", "norm_mem"), ("g_ffn", "norm_ffn")):
        put(name, cols_of(f[key_][0]))
    put("g_fin1", cols_of(f["norm_final"]))
    put("g_fin2", cols_of(f["g_final_2"]))
    put("g_fox", cols_of(f["norm_fox_out"][0], 4))
    put("g_sb", cols_of(f["norm_sb_out"][0], 4))
    put("b_forget", f["b_forget"][0], 8)
    put("b_route", np.concatenate([f["b_router_group"][0], f["b_router_expert"][0]]), 1)
    put("w_f", f["w_in"][0][:, 3072:].reshape(KT, P, 8).transpose(1, 0, 2))
    wr = np.concatenate([f["w_router_group"][0], f["w_router_expert"][0]], 1)
    put("w_route", wr.reshape(KT, P, 20).transpose(1, 0, 2))
    put("c", np.stack([cols_of(f["c_2"][0]), cols_of(f["c_ctx_2"])], 2))
    bm = f["b_mod_2"].reshape(NL * 48, P).transpose(1, 0)
    put("b_mod", np.stack([bm, bm], 2))
    for l in range(NL):
        for k2 in (1, 2):
            g = cols_of(f[f"g_norm{k2}_2"][l])
            put(f"g{k2}_{l}", np.stack([g, g], 2))
        put(f"g_ml_{l}", f["g_mlstm_2"][l].reshape(MH, MD).transpose(1, 0), MD)
        put(f"g_qn_{l}", cols_of(f["g_q_norm_2"][l], 2))
        put(f"g_kvn_{l}", f["g_kv_norm_2"][l])
        put(f"conv_{l}", f["conv_qk_2"][l].reshape(5, 8, MD).transpose(2, 1, 0), MD)
        bg = np.zeros((P, 4), np.float32)
        bg[0:MH] = bg[32:32 + MH] = f["b_gates_2"][l].reshape(4, MH).transpose(1, 0)
        put(f"b_g_{l}", bg)
        put(f"w_g_{l}", f["w_in_2"][l][:, 1792:1808].reshape(KT, P, 16).transpose(1, 0, 2))
        put(f"uq_{l}", f["w_uq_2"][l].reshape(2, P, 384).transpose(1, 0, 2))
        kv = f["w_ukv_2"][l].reshape(P, MH, 160)
        put(f"ukv_{l}", np.concatenate([kv[:, :, 0:64].reshape(P, 256), kv[:, :, 64:].reshape(P, 384)], 1))

    def act_fm(x):
        return np.ascontiguousarray(x.reshape(T, KT, P).transpose(2, 1, 0))

    return {"w_stream": stream, "table": table, "x": act_fm(f["x"]), "mem": act_fm(f["mem"]), "ctx": act_fm(f["ctx_2"])}


def kernel(**inputs):
    import concourse.bacc as bacc
    from concourse.bass_utils import run_bass_kernel_spmd

    arrays = pack(inputs)
    nc = bacc.Bacc("TRN2", target_bir_lowering=False, num_devices=1)
    args = [nc.dram_tensor(f"in_{n}", a.shape, F32, kind="ExternalInput").ap() for n, a in arrays.items()]
    out = nc.dram_tensor("out_dram", (P, KT, T), F32, kind="ExternalOutput").ap()
    build(nc, *args, out)
    r = run_bass_kernel_spmd(nc, [{f"in_{n}": a for n, a in arrays.items()}], core_ids=[0])
    got = r.results[0]["out_dram"]
    return np.ascontiguousarray(got.transpose(2, 1, 0).reshape(1, T, D))
```

```python
from contextlib import ExitStack

import numpy as np

import concourse.bass as bass
from concourse import mybir

F32 = mybir.dt.float32
F32R = mybir.dt.float32r
ALU = mybir.AluOpType
ACT = mybir.ActivationFunctionType
AX_X = mybir.AxisListType.X

P = 128
D = 1024
KT = D // P
T = 256
TB = T // P
NF = 8
HD = 64
NX = 4
NE = 16
NL = 2
MH = 4
MD = 96
RD = 32
FF = 4096
MT = FF // P
EPS = 1e-6
BIG = -1e30
RING = 4
PIECE = 1024
AHEAD = 3
CTX, LAT, ALL = slice(0, T), slice(T, 2 * T), slice(0, 2 * T)

N_QK, N_V, N_XKV, N_SQ = 16, 8, 16, 8
N_MOE = 12 * NE
N_IN2, N_OUT2, N_UPDN = 8 + 4 + 4 + 2 + 2 + 2, 10, 64
LAYER_PIECES = N_IN2 + N_OUT2 + N_UPDN
S_QK = 0
S_V = S_QK + N_QK
S_XKV = S_V + N_V
S_OUT = S_XKV + N_XKV
S_XQ = S_OUT + N_SQ
S_XO = S_XQ + N_SQ
S_MOE = S_XO + N_SQ
S_L = S_MOE + N_MOE
N_PIECES = S_L + NL * LAYER_PIECES
MC = MT // 2

_COLS = [("ones", 128), ("g_mix", 8), ("g_mem", 8), ("eps", 1), ("tiny", 1), ("c", 16), ("w_f", 64), ("b_forget", 1), ("ident", 128),
         ("nones", 128), ("ntri", 128), ("m_le", 512), ("m_ge", 514), ("cdsd", 256), ("cn", 512), ("sn", 512),
         ("cos", 256), ("sin", 256), ("rot", 96), ("w4", 4), ("g_xattn", 8), ("g_ffn", 8), ("g_fin1", 8), ("g_fox", 4),
         ("g_sb", 4), ("b_route", 20), ("w_route", 160), ("b_mod", 192), ("g_fin2", 8)]
EARLY = 8
for _l in range(NL):
    _COLS += [(f"g1_{_l}", 16), (f"g2_{_l}", 16), (f"g_ml_{_l}", 4), (f"g_qn_{_l}", 2), (f"g_kvn_{_l}", 1),
              (f"conv_{_l}", 40), (f"b_g_{_l}", 4)]
COL = {}
_at = 0
for _name, _n in _COLS:
    COL[_name] = (_at, _n)
    _at += _n
N_COLS = _at
N_EARLY = COL[_COLS[EARLY][0]][0]
LCOL = {"w_g": (0, 128), "uq": (128, 768), "ukv": (896, 640)}
N_LCOLS = 1536
MOD_PIECES = (4, 8)

NORM_LIST = [("mix", 4, 2), ("mem", 4, 2), ("fox", 2, 2), ("sb", 2, 2), ("xattn", 4, 2), ("ffn", 4, 2), ("fin1", 4, 2)]
for _l in range(NL):
    NORM_LIST += [(f"n1_{_l}", 8, 1), (f"cq_{_l}", 2, 1) if _l == 0 else (f"cq_{_l}", 1, 2), (f"ckv_{_l}", 1, 1)]
    NORM_LIST += [(f"head_{_l}_{_h}", 1, 1) for _h in range(MH)] + [(f"n2_{_l}", 8, 1)]
NORM_LIST += [("fin2", 8, 1)]
LOOPED = ("n1_1", "fin2")
NORM, SQ_AT, ADD_AT, STEPS, HALVES = {}, {}, {}, {}, {}
_sq = _add = 0
for _i, (_name, _steps, _halves) in enumerate(NORM_LIST):
    NORM[_name], STEPS[_name], HALVES[_name] = _i, _steps, _halves
    SQ_AT[_name], ADD_AT[_name] = _sq, _add
    _sq += _steps
    _add += _steps if _name in LOOPED else _steps - 1

U_STEPS = [("mix", 8), ("mem", 8), ("fox", 4), ("sb", 4), ("xattn", 8), ("xo", 4), ("ffn", 8)]
for _l in range(NL):
    U_STEPS += [(f"n1_{_l}", 8), (f"y_{_l}", 10), (f"n2_{_l}", 8)]
U_AT = {}
_at = 0
for _name, _n in U_STEPS:
    U_AT[_name] = _at
    _at += _n

_HEAD_STEPS = (4, 5, 6, 9)
V_AT, V_N = {}, {}
_at = 0
for _name, _n in U_STEPS:
    V_AT[_name] = _at
    V_N[_name] = 0 if _name == "xo" else len(_HEAD_STEPS) if _name.startswith("y_") else _n
    _at += V_N[_name]
OUT_NORMS = [_name for _name, _, _ in NORM_LIST if _name not in V_N]


def value_count(name, step):
    return V_AT[name] + (_HEAD_STEPS.index(step) if name.startswith("y_") else step) + 1


def normed(name):
    if name in V_N:
        return "u_v", V_AT[name] + V_N[name]
    return "norm_out", OUT_NORMS.index(name) + 1


UNITS = [("fox", h, None) for h in range(NF)] + [("xat", h, None) for h in range(NX)]
for _l in range(NL):
    if _l == 0:
        UNITS += [(f"mctx{_l}", h, None) for h in range(MH)]
    UNITS += [(f"mlat{_l}", h, q) for h in range(MH) for q in range(TB)]
UNIT0 = {}
for _i, _u in enumerate(UNITS):
    UNIT0.setdefault(_u[0], _i)


class Jobs:

    def __init__(self):
        self.first, self.engines, self.counted = {}, [], []

    def add(self, phase, count, engine, counted=True):
        self.first[phase] = len(self.engines)
        self.engines += [engine] * count
        self.counted += [counted] * count

    def number(self, phase, j=0):
        return self.first[phase] + j

    def full(self, n):
        return self.counted[: n + 1].count(True)

    def emptied(self, n):
        engine = self.engines[n]
        if engine.startswith("mlstm"):
            return "ml_sum", MH * (int(engine[-1]) + 1)
        return f"job_emptied_{engine}", self.engines[: n + 1].count(engine)


JOBS = Jobs()
for _phase, _count, _engine in [("qk", 8, "act"), ("v", 4, "act"), ("xkv", 8, "act"), ("out1", 4, "dve"),
                                ("xq", 4, "act"), ("xo", 4, "dve")]:
    JOBS.add(_phase, _count, _engine)
JOBS.add("moe_y", 4, "dve", False)
for _l in range(NL):
    _w = 2 if _l == 0 else 1
    for _phase, _count, _engine in [("mqk", 8, "act"), ("mv", 4, "act"), ("mo", 4, "act"), ("cq", 2, "act"),
                                    ("ckv", 2, "act"), ("pf", 2, "act"), ("uq", 4, "act"), ("rot", 5, "dve"),
                                    ("kn", 4, "act"), ("va", 4, "act"),
                                    ("fa0", 2, "act"), ("fy0", 2, "act"), ("fa1", 2 * (_w - 1), "act"), ("fy1", 2 * (_w - 1), "act"),
                                    ("mlstm", 4, f"mlstm{_l}"),
                                    ("out", 8, "dve"), ("upa", MC, "act"), ("dna", 8, "dve"), ("upb", MC, "act"), ("dnb", 8, "dve")]:
        JOBS.add(f"{_phase}_{_l}", _count, _engine, _phase != "mlstm")


def build(nc, w_stream, table_in, small_in, x_in, mem_in, ctx_in, out):
    with ExitStack() as stack:
        sems = {}

        def S(name):
            if name not in sems:
                sems[name] = stack.enter_context(nc.semaphore(name))
            return sems[name]

        base = (nc.sbuf_base + 31) // 32 * 32
        top = [0]

        def at(name, shape, off, dtype=F32):
            n = int(np.prod(shape[1:]))
            return nc.alloc_sbuf_tensor_at(name, list(shape), dtype, offset=base + 4 * off)

        def take(n):
            top[0] += n
            return top[0] - n

        table = at("table", [P, N_COLS], take((N_COLS + 7) // 8 * 8))
        lw = at("lw", [P, N_LCOLS], take(N_LCOLS))
        res = at("res", [P, KT, 2 * T], take(KT * 2 * T))
        uh = at("uh", [P, KT, 2 * T], take(KT * 2 * T), F32R)
        ul_at = take(KT * 2 * T)
        ul = at("ul", [P, KT, 2 * T], ul_at, F32R)
        uv = at("uv", [P, KT, 2 * T], ul_at)
        sq_at = take(5 * 512)
        sq = at("sq", [P, 5, 512], sq_at)
        rows_at = take(5 * 512)
        rows_buf = at("rows_buf", [32 + MH, 5, 512], rows_at)
        yfl = at("yfl", [P, 2, 512], rows_at, F32R)
        crow = at("crow", [NF, 5, T], rows_at)
        turned = at("turned", [32, 16, 32], rows_at)
        rstd = at("rstd", [P, 2 * T], take(2 * T))
        small = at("small", [P, 256], take(256))
        modv = at("modv", [P, 192], take(192))
        gmod = at("gmod", [P, 2 * NL, 16], take(64))
        cparts = at("cparts", [P, 100], take(104), F32R)
        gcol = at("gcol", [P, 2, 4, MH], take(32))
        ring = at("ring", [P, RING, PIECE], take(RING * PIECE))
        wh = at("wh", [P, RING, PIECE], take(RING * PIECE), F32R)
        wl = at("wl", [P, RING, PIECE], take(RING * PIECE), F32R)
        w0 = take(16448)
        assert base + 4 * top[0] <= nc.sbuf_top, (base + 4 * top[0], nc.sbuf_top)
        qk = at("qk", [P, 16, T], w0)
        v1 = at("v1", [P, TB, D], w0 + 4096)
        heads = at("heads", [P, KT, T], w0 + 6144)
        kx = at("kx", [P, KT, T], w0 + 8192)
        vx = at("vx", [P, TB, D], w0 + 10240)
        sbt = [at(f"sbt{i}", [P, 4, 512], w0 + 12288 + i * 2048) for i in range(2)]
        qx = at("qx", [P, KT, T], w0)
        gates = at("gates", [P, NE, T], w0)
        eg = at("eg", [P, 512], w0 + 4096)
        hidh = at("hidh", [P, 2, T], w0 + 4608, F32R)
        hidl = at("hidl", [P, 2, T], w0 + 5120, F32R)
        qkp = at("qkp", [MD, 8, TB, 260], w0)
        qa = at("qa", [MD, MH, 512], w0)
        ka = at("ka", [MD, MH, 512], w0 + 2048)
        ml = at("ml", [P, 8, 512], w0)
        qc = at("qc", [MD, 8, 512], w0 + 4160)
        mv = at("mv", [P, 4, 384], w0 + 8256)
        mo = at("mo", [MD, MH, 512], w0 + 9792)
        va = at("va", [P, 4, 384], w0 + 11840)
        yfh = at("yfh", [P, 2, 512], w0 + 11840, F32R)
        pf = at("pf", [P, 2, 512], w0 + 13376)
        yf = pf
        cq = at("cq", [P, 2, 512], w0 + 14400)
        ckv = at("ckv", [P, 512], w0 + 15424)
        kr = at("kr", [MD, 512], w0 + 15936)
        ya = at("ya", [MD, MH, 512], w0 + 14400)
        hh = at("hh", [P, MC, 512], w0, F32R)
        hl = at("hl", [P, MC, 512], w0 + 8192, F32R)
        prob = [sq[:, i, :] for i in range(2)]
        probT = [sq[:, 2 + i, :] for i in range(2)]
        fa = sq[:, 0:2, :].rearrange("p a (b c) -> p a b c", b=TB)
        rows = [rows_buf[32 * d:32 * d + MH] for d in range(2)]
        bank = [stack.enter_context(nc.psum_tensor(f"bank{i}", [P, 512], F32)) for i in range(8)]

        def tab(name, rows=P):
            a, n = COL[name]
            return table[0:rows, a:a + n]

        def ltab(name):
            a, n = LCOL[name]
            return lw[:, a:a + n]

        ident, ones = tab("ident"), tab("ones")
        row_ident = [ident[32 * d:32 * d + MH, 32 * d:32 * d + MH] for d in range(2)]
        m_ge = tab("m_ge").rearrange("p (k t) -> p k t", k=2)

        class Chain:

            def __init__(self, eng, name):
                self.eng, self.sem, self.n, self.more = eng, S(name), 0, None

            def link(self, ins):
                ins.then_inc(self.sem, 1)
                self.n += 1
                self.eng.wait_ge(self.sem, self.n if self.more is None else self.more + self.n)

            def loop(self, i, per):
                self.start, self.per, self.more = self.n, per, i * per

            def end(self, turns):
                assert self.n - self.start == self.per, (self.n - self.start, self.per)
                self.n, self.more = self.start + self.per * turns, None

        def full(eng, phase, j=0):
            n = JOBS.number(phase, j)
            eng.wait_ge(S("job_full"), JOBS.full(n))
            return bank[n % 4]

        def emptied(ins, engine):
            ins.then_inc(S(f"job_emptied_{engine}"), 1)

        def wait_emptied(eng, phase, j):
            sem, count = JOBS.emptied(JOBS.number(phase, j))
            eng.wait_ge(S(sem), count)

        def lin_cols(l):
            return ALL if l == 0 else LAT

        def mlb(l, i):
            return JOBS.number(f"mlstm_{l}", i) % 4

        def ml_args(l, h, kb, d):
            if l == 0:
                return 2 * (4 * h + kb) + d + 1
            return 2 * 4 * MH + 2 * (2 * h + kb - 2) + d + 1

        def out_piece(m):
            return (10 * m + 9) // 8

        block = stack.enter_context(nc.Block())

        @block.sync
        def _(sp):
            sp.dma_start(table[:, 0:N_EARLY], table_in[:, 0:N_EARLY]).then_inc(S("early_in"), 16)
            sp.dma_start(res[:, :, LAT], x_in).then_inc(S("x_in"), 16)
            for s in range(RING):
                sp.dma_start(ring[:, s, :], w_stream[s]).then_inc(S(f"piece_in{s}"), 16)
            sp.dma_start(table[:, N_EARLY:], table_in[:, N_EARLY:]).then_inc(S("table_in"), 16)
            sp.dma_start(res[:, :, CTX], mem_in).then_inc(S("mem_in"), 16)
            sp.dma_start(lw[:, :], small_in[0]).then_inc(S("lw_in0"), 16)
            with sp.Fori(1, N_PIECES // RING) as i:
                for s in range(RING):
                    sp.wait_ge(S("w_lo"), i * RING + (s + 1 - RING))
                    sp.dma_start(ring[:, s, :], w_stream[i * RING + s]).then_inc(S(f"piece_in{s}"), 16)
            sp.wait_ge(S("norm_out"), normed("fin2")[1])
            sp.dma_start(out, res[:, :, LAT]).then_inc(S("stored"), 16)
            sp.wait_ge(S("stored"), 16)

        @block.gpsimd
        def _(pool):
            pool.wait_ge(S("u_v"), normed("mem")[1])
            pool.dma_start(res[:, :, CTX], ctx_in).then_inc(S("ctx_in"), 16)
            for l in range(1, NL):
                pool.wait_ge(S("job_full"), JOBS.full(JOBS.number(f"va_{l - 1}", 3)))
                pool.dma_start(lw[:, :], small_in[l]).then_inc(S(f"lw_in{l}"), 16)

        @block.scalar
        def _(act):
            ch = Chain(act, "act_step")
            hi_at = [0]

            def hi_part(s, landed, used):
                act.wait_ge(S(f"piece_in{s}"), landed)
                if used is not None:
                    act.wait_ge(S("piece_used"), used)
                act.activation(wh[:, s, :], ring[:, s, :], ACT.Copy).then_inc(S("w_hi"), 1)

            def split(to):
                while hi_at[0] <= min(to, N_PIECES - 1):
                    n = hi_at[0]
                    hi_part(n % RING, 16 * (n // RING + 1), n - 3 if n >= RING else None)
                    hi_at[0] += 1

            def split_turn(i, per, base, lo, hi):
                for j in range(lo, hi + 1):
                    n = base + j
                    hi_part(n % RING, i * (4 * per) + 16 * (n // RING + 1), i * per + (n - 3))

            def square(name, t, src, p, n, after=True):
                if name.startswith("head"):
                    dst = sq[0:p, 4, 0:n]
                elif t == 0 and name not in LOOPED:
                    dst = sq[0:p, 3, 0:n]
                else:
                    dst = sq[0:p, t % 2, 0:n]
                    if t >= 3:
                        act.wait_ge(S("norm_add"), ADD_AT[name] + t - 2)
                if len(src.shape) == 3:
                    dst = dst.rearrange("p (a t) -> p a t", a=src.shape[1])
                act.activation(dst, src, ACT.Square).then_inc(S("norm_sq"), 1)

            def root(name, p, n, width):
                i = NORM[name]
                act.wait_ge(S("norm_ms"), i + 1)
                if i:
                    sem, count = normed(NORM_LIST[i - 1][0])
                    act.wait_ge(S(sem), count)
                ch.link(act.activation(rstd[0:p, 0:n], bank[7][0:p, 0:n], ACT.Ln, bias=tab("eps")[0:p],
                                       scale=1.0 / width))
                act.activation(rstd[0:p, 0:n], rstd[0:p, 0:n], ACT.Exp, scale=-0.5).then_inc(S("norm_rstd"), 1)

            def pairs(name, src, cols, width, steps=4):
                for t in range(steps):
                    square(name, t, src[:, 2 * t:2 * t + 2, cols], P, 512)
                root(name, P, T, width)

            def round_u(name, i, parts, ready=None):
                sem, count = ready or ("u_v", value_count(name, i))
                act.wait_ge(S(sem), count)
                for hi, v, bias in parts:
                    if bias is None:
                        last = act.activation(hi, v, ACT.Copy)
                    else:
                        last = act.activation(hi, v, ACT.Identity, bias=bias)
                last.then_inc(S("u_h"), 1)

            def round_tiles(name, cols, steps=8):
                for k in range(steps):
                    j = k + (4 if name == "sb" else 0)
                    round_u(name, k, [(uh[:, j, cols], uv[:, j, cols], None)])

            def smv(i, what, k):
                a = (i % 2) * 8 + what * 2 + k
                return small[:, a:a + 1]

            def softmax(i):
                g, w = (1, 512) if UNITS[i][2] is not None else (2, 256)
                act.wait_ge(S("sm_max"), i + 1)
                if i >= 2:
                    act.wait_ge(S("sm_tr"), i - 1)
                for k in range(g):
                    last = act.activation(prob[i % 2][:, k * w:(k + 1) * w], bank[4 + i % 2][:, k * w:(k + 1) * w],
                                          ACT.Exp, bias=smv(i, 0, k), accum_out=smv(i, 2, k))
                last.then_inc(S("sm_exp"), 1)

            def transposed(i):
                act.wait_ge(S("sm_tr"), i + 1)
                if i >= 2:
                    act.wait_ge(S("sm_o"), i - 1)
                act.activation(probT[i % 2], bank[6][:, :], ACT.Copy).then_inc(S("sm_pt"), 1)

            def log1p_rows(src, dst, sem_in, count, sem_out):
                act.wait_ge(S(sem_in), count)
                ch.link(act.activation(dst, src, ACT.Abs))
                ch.link(act.activation(dst, dst, ACT.Exp, scale=-1.0))
                act.activation(dst, dst, ACT.Ln, bias=1.0).then_inc(S(sem_out), 1)

            act.wait_ge(S("early_in"), 16)
            act.activation(small[:, 64:80], tab("c"), ACT.Exp, scale=-1.0).then_inc(S("c_exp"), 1)
            act.wait_ge(S("x_in"), 16)
            pairs("mix", res, LAT, D)
            round_tiles("mix", LAT)
            split(2)
            for s in range(8):
                split(S_QK + 2 * s + 1 + AHEAD)
                b = full(act, "qk", s)
                scale = HD ** -0.5 if s in (0, 1, 4, 5) else 1.0
                emptied(act.activation(qk[:, 2 * s:2 * s + 2, :], b[:, :].rearrange("p (a t) -> p a t", a=2), ACT.Copy,
                                       scale=scale), "act")
                if s == 0:
                    act.wait_ge(S("mem_in"), 16)
                    for t in range(4):
                        square("mem", t, res[:, 2 * t:2 * t + 2, CTX], P, 512)
                if s == 2:
                    root("mem", P, T, D)
                    round_tiles("mem", CTX)
                if s == 3:
                    log1p_rows(crow[:, 0, :], crow[:, 1, :], "fox_f", 1, "fox_ln")
            for s in range(4):
                split(S_V + 2 * s + 1 + AHEAD)
                b = full(act, "v", s)
                emptied(act.activation(v1[:, :, s * T:(s + 1) * T], b[:, :].rearrange("p (a t) -> p a t", a=2),
                                       ACT.Copy), "act")

            for i in range(NF + 1):
                if i < NF:
                    softmax(i)
                    split(S_XKV + 2 * i + 1 + AHEAD)
                    b = full(act, "xkv", i)
                    dst = kx[:, 2 * i:2 * i + 2, :] if i < 4 else vx[:, :, (i - 4) * T:(i - 3) * T]
                    emptied(act.activation(dst, b[:, :].rearrange("p (a t) -> p a t", a=2), ACT.Copy), "act")
                if i >= 1:
                    transposed(i - 1)

            for h in range(NF + 1):
                if h < NF:
                    t = sbt[h % 2]
                    act.wait_ge(S("sb_z"), h + 1)
                    if h >= 2:
                        act.wait_ge(S("sb_softplus"), h - 1)
                    ch.link(act.activation(t[:, 0, :], bank[4 + h % 2][:, :], ACT.Abs))
                    ch.link(act.activation(t[:, 0, :], t[:, 0, :], ACT.Exp, scale=-1.0))
                    act.activation(t[:, 0, :], t[:, 0, :], ACT.Ln, bias=1.0).then_inc(S("sb_ln"), 1)
                if h >= 1:
                    g = h - 1
                    act.wait_ge(S("sb_arg"), g + 1)
                    act.activation(sbt[g % 2][:, 3, :], sbt[g % 2][:, 2, :], ACT.Exp).then_inc(S("sb_w"), 1)
                if h == 2:
                    for t in range(2):
                        square("fox", t, heads[:, 2 * t:2 * t + 2, :], P, 512)
                    root("fox", P, T, 512)
            for t in range(2):
                act.wait_ge(S("sb_out"), 4 * t + 4)
                square("sb", t, heads[:, 4 + 2 * t:6 + 2 * t, :], P, 512)
            root("sb", P, T, 512)
            round_tiles("fox", LAT, 4)
            round_tiles("sb", LAT, 4)

            def added_squares(name, phase, first):
                for t in range(4):
                    split(first + 2 * t + 1 + AHEAD)
                    wait_emptied(act, phase, t)
                    square(name, t, res[:, 2 * t:2 * t + 2, LAT], P, 512)
                root(name, P, T, D)

            added_squares("xattn", "out1", S_OUT)
            round_tiles("xattn", LAT)
            for s in range(4):
                split(S_XQ + 2 * s + 1 + AHEAD)
                b = full(act, "xq", s)
                emptied(act.activation(qx[:, 2 * s:2 * s + 2, :], b[:, :].rearrange("p (a t) -> p a t", a=2), ACT.Copy,
                                       scale=256 ** -0.5), "act")
            for i in range(NX + 2):
                if i < NX:
                    softmax(UNIT0["xat"] + i)
                if 1 <= i <= NX:
                    transposed(UNIT0["xat"] + i - 1)
                if i >= 2:
                    j = 2 * (i - 2)
                    round_u("xo", i - 2, [(uh[:, j:j + 2, LAT], uv[:, j:j + 2, LAT], None)],
                            ("sm_out", UNIT0["xat"] + i - 1))
            added_squares("ffn", "xo", S_XO)
            round_tiles("ffn", LAT)

            for b in range(TB):
                act.wait_ge(S("rt_max"), b + 1)
                r = small[:, 96 + 64 * b:160 + 64 * b]
                act.activation(r[:, 24:28], r[:, 0:4], ACT.Exp, bias=r[:, 20:21],
                               accum_out=r[:, 21:22]).then_inc(S("rt_exp"), 1)
                act.wait_ge(S("rt_diff"), b + 1)
                act.activation(r[:, 22:23], r[:, 23:24], ACT.Exp).then_inc(S("rt_exp2"), 1)
            for e in range(NE // 2):
                act.wait_ge(S("gate_full"), e + 1)
                act.activation(gates[:, 2 * e:2 * e + 2, :], bank[4 + e % 2][:, :].rearrange("p (a t) -> p a t", a=2),
                               ACT.Copy).then_inc(S("gate_in"), 1)
            split(S_MOE + 2)
            with act.Fori(0, NE // 2) as i:
                done = AHEAD
                for e, (gate_end, up_end) in enumerate(((1, 3), (11, 13))):
                    split_turn(i, 24, S_MOE, done, gate_end + AHEAD)
                    act.wait_ge(S("moe_gate"), i * 2 + (e + 1))
                    act.wait_ge(S("moe_lo"), i * 2 + (e + 1))
                    act.activation(eg[:, :], bank[4][:, :], ACT.Silu).then_inc(S("moe_silu"), 1)
                    split_turn(i, 24, S_MOE, gate_end + AHEAD + 1, up_end + AHEAD)
                    act.wait_ge(S("moe_v"), i * 2 + (e + 1))
                    act.activation(hidh[:, :, :].rearrange("p a t -> p (a t)"), eg[:, :],
                                   ACT.Copy).then_inc(S("moe_hi"), 1)
                    done = up_end + AHEAD + 1
                split_turn(i, 24, S_MOE, done, 23 + AHEAD)
            hi_at[0] = S_L + AHEAD
            for t in range(4):
                wait_emptied(act, "moe_y", t)
                square("fin1", t, res[:, 2 * t:2 * t + 2, LAT], P, 512)
            root("fin1", P, T, D)

            def round_mod(l, k2):
                first = l * 48 + (0 if k2 == 0 else 24)
                name = f"n{k2 + 1}_{l}"
                for k in range(KT):
                    parts = []
                    for which, cols in ((0, LAT), (1, CTX)):
                        if k2 == 1 and l == NL - 1 and which == 1:
                            continue
                        c = 2 * (first + k) + which
                        parts.append((uh[:, k, cols], uv[:, k, cols], modv[:, c:c + 1]))
                    round_u(name, k, parts)

            for l in range(NL):
                cols = lin_cols(l)
                n = cols.stop - cols.start
                p0 = S_L + l * LAYER_PIECES
                if l == 0:
                    act.wait_ge(S("ctx_in"), 16)
                    act.wait_ge(S("norm_out"), normed("fin1")[1])
                    for k in range(KT):
                        square("n1_0", k, res[:, k, :], P, 512)
                root(f"n1_{l}", P, 2 * T, D)
                round_mod(l, 0)
                for d in range(2):
                    log1p_rows(rows[d][:, 1, :], rows[d][:, 2, :], "ml_f", 2 * l + d + 1, "ml_ln")
                for j in range(8):
                    split(p0 + j + AHEAD)
                    b = full(act, f"mqk_{l}", j)
                    if j < 4 and l:
                        last = act.activation(qkp[:, j, 1, 2:258], b[0:MD, 0:T], ACT.Copy)
                    else:
                        last = act.activation(qkp[:, j, :, 2:258],
                                              b[0:MD, :].rearrange("p (s t) -> p s t", s=2), ACT.Copy)
                    emptied(last, "act")
                split(p0 + 11 + AHEAD)
                for j in range(4):
                    b = full(act, f"mv_{l}", j)
                    emptied(act.activation(mv[:, j, :], b[:, 0:384], ACT.Copy), "act")
                for j in range(4):
                    split(p0 + 12 + j + AHEAD)
                    b = full(act, f"mo_{l}", j)
                    emptied(act.activation(mo[:, j, cols], b[0:MD, 0:n], ACT.Sigmoid), "act")
                for j in range(8):
                    cc = cols if j < 4 else ALL
                    act.wait_ge(S("conv_sum"), 8 * l + j + 1)
                    act.activation(qc[:, j, cc], qc[:, j, cc], ACT.Silu).then_inc(S("conv_done"), 1)
                for j in range(2):
                    split(p0 + 16 + j + AHEAD)
                    b = full(act, f"cq_{l}", j)
                    emptied(act.activation(cq[:, j, cols], b[:, 0:n], ACT.Copy), "act")
                split(p0 + 18 + AHEAD)
                b = full(act, f"ckv_{l}", 0)
                emptied(act.activation(ckv[:, :], b[:, :], ACT.Copy), "act")
                split(p0 + 19 + AHEAD)
                b = full(act, f"ckv_{l}", 1)
                emptied(act.activation(kr[:, :], b[0:MD, :], ACT.Copy), "act")
                wait_emptied(act, f"ckv_{l}", 0)
                if l == 0:
                    for j in range(2):
                        square("cq_0", j, cq[:, j, :], P, 512)
                else:
                    square("cq_1", 0, cq[:, :, LAT], P, 512)
                for j in range(2):
                    split(p0 + 20 + j + AHEAD)
                    b = full(act, f"pf_{l}", j)
                    emptied(act.activation(pf[:, j, cols], b[:, 0:n], ACT.Copy), "act")
                for d in range(2):
                    act.wait_ge(S("gcol_full"), 2 * l + d + 1)
                    act.activation(gcol[:, d, :, :], bank[4 + d][:, 0:16].rearrange("p (a b) -> p a b", a=4),
                                   ACT.Copy).then_inc(S("gcol_in"), 1)
                root(f"cq_{l}", P, n, 256)
                square(f"ckv_{l}", 0, ckv[:, :], P, 512)
                root(f"ckv_{l}", P, 512, 128)
                for h in range(MH):
                    b = full(act, f"uq_{l}", h)
                    emptied(act.activation(qa[:, h, cols], b[0:MD, 0:n], ACT.Copy, scale=MD ** -0.5), "act")
                for h in range(MH):
                    b = full(act, f"kn_{l}", h)
                    emptied(act.activation(ka[0:64, h, :], b[0:64, :], ACT.Copy), "act")
                for j in range(4):
                    b = full(act, f"va_{l}", j)
                    emptied(act.activation(va[:, j, :], b[:, 0:384], ACT.Copy), "act")
                for s in range(n // T):
                    sc = slice(cols.start + s * T, cols.start + (s + 1) * T)
                    for ft in range(2):
                        b = full(act, f"fa{s}_{l}", ft)
                        emptied(act.activation(fa[:, ft, :, :], b[:, :].rearrange("p (a t) -> p a t", a=2),
                                               ACT.Copy), "act")
                    for ft in range(2):
                        b = full(act, f"fy{s}_{l}", ft)
                        emptied(act.activation(yf[:, ft, sc], b[:, 0:T], ACT.Copy), "act")
                units = range(UNIT0["mctx0"], UNIT0["mlat1"]) if l == 0 else range(UNIT0["mlat1"], len(UNITS))
                for i in range(units.start, units.stop + 1):
                    if i < units.stop:
                        softmax(i)
                    if i > units.start:
                        transposed(i - 1)
                for h in range(MH):
                    round_u(f"y_{l}", h, [(uh[0:MD, h, cols], ya[:, h, cols], None)],
                            ("sm_out", UNIT0[f"mlat{l}"] + TB * (h + 1)))

                rb, em = [ml[:, d, :] for d in range(2)], [ml[0:MD, 2 + d, :] for d in range(2)]
                arg, den = [ml[:, 4 + d, :] for d in range(2)], [ml[0:MD, 6 + d, :] for d in range(2)]

                def head_root(h):
                    root(f"head_{l}_{h}", MD, n, MD)

                def head_round(h):
                    round_u(f"y_{l}", MH + h if h < MH - 1 else 9, [(uh[0:MD, MH + h, cols], mo[:, h, cols], None)])

                for h in range(MH):
                    g = l * MH + h
                    for d in range(2):
                        act.wait_ge(S("ml_b"), 4 * g + d + 1)
                        act.activation(rb[d][:, cols], bank[6][:, cols], ACT.Copy).then_inc(S("ml_b_in"), 1)
                    for d in range(2):
                        act.wait_ge(S("ml_b"), 4 * g + 2 + d + 1)
                        act.activation(em[d][:, cols], bank[6][0:MD, cols], ACT.Copy).then_inc(S("ml_b_in"), 1)
                    if h:
                        act.wait_ge(S("ml_sum"), g)
                        square(f"head_{l}_{h - 1}", 0, den[0][:, cols], MD, n)
                    for kb in range(4):
                        for d in range(2):
                            if kb >= 2 or l == 0:
                                act.wait_ge(S("ml_arg"), ml_args(l, h, kb, d))
                            if kb >= 2:
                                act.wait_ge(S("ml_v"), 4 * g + kb - 1)
                            bias = gcol[:, d, kb, h:h + 1]
                            e = sq[:, 2 * (kb % 2) + d, :]
                            if kb < 2:
                                if l == 0:
                                    act.activation(e[:, CTX], arg[d][:, CTX], ACT.Exp, bias=bias)
                                last = act.activation(e[:, LAT], rb[d][:, LAT], ACT.Exp, bias=bias)
                            else:
                                last = act.activation(e[:, LAT], arg[d][:, LAT], ACT.Exp, bias=bias)
                            last.then_inc(S("ml_e"), 1)
                        if h and kb == 1:
                            head_root(h - 1)
                        if h and kb == 2:
                            head_round(h - 1)
                    act.wait_ge(S("ml_v"), 4 * (g + 1))
                    for d in range(2):
                        last = act.activation(den[d][:, cols], bank[mlb(l, 2 * d + 1)][0:MD, cols], ACT.Abs)
                    ch.link(last)
                    for d in range(2):
                        act.activation(den[d][:, cols], den[d][:, cols], ACT.Ln,
                                       bias=tab("tiny", MD)).then_inc(S("ml_ln2"), 1)
                    for d in range(2):
                        act.wait_ge(S("ml_min"), 2 * g + d + 1)
                        act.activation(den[d][:, cols], den[d][:, cols], ACT.Exp).then_inc(S("ml_rden"), 1)
                act.wait_ge(S("ml_sum"), (l + 1) * MH)
                square(f"head_{l}_{MH - 1}", 0, den[0][:, cols], MD, n)
                head_root(MH - 1)
                for j in range(2):
                    round_u(f"y_{l}", 7 + j, [(yfh[:, j, cols], yf[:, j, cols], None)],
                            JOBS.emptied(JOBS.number(f"fy1_{l}" if l == 0 else f"fy0_{l}", j)))
                head_round(MH - 1)
                for m in range(KT):
                    split(p0 + N_IN2 + out_piece(m) + AHEAD)
                    wait_emptied(act, f"out_{l}", m)
                    square(f"n2_{l}", m, res[:, m, cols], P, n)
                root(f"n2_{l}", P, n, D)
                round_mod(l, 1)
                for half, name in enumerate("ab"):
                    pu = p0 + N_IN2 + N_OUT2 + half * 32
                    b0, f0 = JOBS.number(f"up{name}_{l}"), JOBS.full(JOBS.number(f"up{name}_{l}"))
                    h0 = (2 * l + half) * MC
                    split(pu + AHEAD - 1)
                    with act.Fori(0, MC // 4) as i:
                        for j in range(4):
                            split_turn(i, 4, pu, j + AHEAD, j + AHEAD)
                            act.wait_ge(S("job_full"), i * 4 + (f0 + j))
                            r = sq[:, j % 2, 0:n]
                            v = sq[:, 2 + j % 2, 0:n]
                            act.wait_ge(S("hid_lo"), i * 4 + (h0 + j + 1))
                            act.activation(r, bank[(b0 + j) % 4][:, 0:n], ACT.Relu).then_inc(
                                S("job_emptied_act"), 1)
                            act.wait_ge(S("job_emptied_act"),
                                        i * 4 + (JOBS.emptied(b0)[1] + j))
                            act.activation(v, r, ACT.Square)
                            act.activation(hh[:, bass.ds(i * 4 + j, 1), 0:n].rearrange("p a b -> p (a b)"), r,
                                           ACT.Square).then_inc(S("hid_hi"), 1)
                    hi_at[0] = pu + MC + AHEAD
                    pd = pu + MC
                    if half == 0:
                        with act.Fori(0, 4) as i:
                            split_turn(i, 4, pd, AHEAD, AHEAD + 3)
                    else:
                        nxt = "n1_1" if l == 0 else "fin2"
                        turns = 4 if l < NL - 1 else 3
                        b1 = JOBS.emptied(JOBS.number(f"dnb_{l}"))[1]

                        def down_squares(i, fixed=None):
                            for j in range(2):
                                act.wait_ge(S("job_emptied_dve"), i * 2 + (b1 + j))
                                act.wait_ge(S("norm_add"), i * 2 + ADD_AT[nxt] + j - 1)
                                c = ALL if l == 0 else LAT
                                src = res[:, bass.ds(i * 2 + j, 1), c] if fixed is None else res[:, 2 * fixed + j, c]
                                if fixed is None:
                                    src = src.rearrange("p a b -> p (a b)")
                                act.activation(sq[:, j, 0:n], src, ACT.Square).then_inc(S("norm_sq"), 1)

                        with act.Fori(0, turns) as i:
                            split_turn(i, 4, pd, AHEAD, AHEAD + 3)
                            down_squares(i)
                        if turns == 3:
                            hi_at[0] = pd + 12 + AHEAD
                            split(pd + 15)
                            down_squares(3, 3)
                    hi_at[0] = pd + MC + AHEAD
            root("fin2", P, T, D)

        @block.tensor
        def _(pe):
            begun = []

            def mm(*operands, **flags):
                ins = pe.matmul(*operands, **flags)
                if begun:
                    begun.clear()
                    ins.then_inc(S("piece_used"), 1)
                return ins

            def claim(phase, j=0):
                n = JOBS.number(phase, j)
                if n >= 4:
                    sem, count = JOBS.emptied(n - 4)
                    pe.wait_ge(S(sem), count)
                return bank[n % 4]

            def parts(n):
                pe.wait_ge(S("w_lo"), n + 1)
                if n:
                    begun.append(n)

            def parts_turn(i, per, n):
                pe.wait_ge(S("w_lo"), i * per + (n + 1))
                begun.append(n)

            def prod(o, n, j, xh, xl, start, stop, m=P, nr=P, **flags):
                h, lo = (w[0:nr, n % RING, j * P:j * P + m] for w in (wh, wl))
                mm(o, h, xh, start=start, stop=False, **flags)
                mm(o, h, xl, start=False, stop=False, **flags)
                return mm(o, lo, xh, start=False, stop=stop, **flags)

            def prod_t(o, n, c0, w, xh, xl, start, stop, **flags):
                h, lo = (x[:, n % RING, c0:c0 + w] for x in (wh, wl))
                mm(o, xh, h, start=start, stop=False, **flags)
                mm(o, xh, lo, start=False, stop=False, **flags)
                return mm(o, xl, h, start=False, stop=stop, **flags)

            def finish(ins):
                ins.then_inc(S("job_full"), 1)

            def norm(name, p, n):
                if STEPS[name] > 1:
                    end = ADD_AT[name] + STEPS[name] - (0 if name in LOOPED else 1)
                    pe.wait_ge(S("norm_add"), end)
                else:
                    pe.wait_ge(S("norm_sq"), SQ_AT[name] + 1)
                s = 4 if name.startswith("head") else 3
                for j in range(HALVES[name]):
                    last = mm(bank[7][0:p, 0:n], ones[0:p, 0:p], sq[0:p, s, j * n:(j + 1) * n],
                              start=(j == 0), stop=(j == HALVES[name] - 1))
                last.then_inc(S("norm_ms"), 1)

            def linear(phase, j, n, cols, ready=None):
                b = claim(phase, j)
                for m in range(2):
                    parts(n + m)
                    for k in range(KT):
                        if ready and j == 0 and m == 0:
                            pe.wait_ge(S("u_l"), U_AT[ready] + (k // 2 if ready == "xo" else k) + 1)
                        last = prod(b[:, m * T:(m + 1) * T], n + m, k, uh[:, k, cols], ul[:, k, cols],
                                    k == 0, k == KT - 1)
                finish(last)

            def token_major(phase, j, n, c0):
                b = claim(phase, j)
                for p in range(2):
                    parts(n + p)
                    for tb in range(TB):
                        for k in range(4):
                            t = slice(c0 + tb * P, c0 + (tb + 1) * P)
                            last = prod_t(b[:, tb * T:(tb + 1) * T], n + p, k * T, T, uh[:, 4 * p + k, t],
                                          ul[:, 4 * p + k, t], p + tb + k == 0, p == 1 and k == 3,
                                          skip_group_check=True)
                finish(last)

            pe.wait_ge(S("early_in"), 16)
            norm("mix", P, T)
            linear("qk", 0, S_QK, LAT, "mix")
            wf = tab("w_f").rearrange("p (k f) -> p k f", k=KT)
            for k in range(KT):
                mm(bank[6][0:NF, 0:T], wf[:, k, :], uh[:, k, LAT].bitcast(F32), start=(k == 0), stop=False)
                last = mm(bank[6][0:NF, 0:T], wf[:, k, :], ul[:, k, LAT].bitcast(F32), start=False,
                          stop=(k == KT - 1))
            last.then_inc(S("fox_f_full"), 1)
            for s in range(1, 8):
                linear("qk", s, S_QK + 2 * s, LAT)
                if s == 1:
                    norm("mem", P, T)
            for s in range(4):
                token_major("v", s, S_V + 2 * s, T)

            def scores(i):
                kind, h, q = UNITS[i]
                b = bank[4 + i % 2]
                if i >= 2:
                    pe.wait_ge(S("sm_exp"), i - 1)
                if kind == "fox":
                    r = slice((h % 2) * HD, (h % 2) * HD + HD)
                    for qb in range(TB):
                        o = b[:, qb * T:(qb + 1) * T]
                        mm(o, qk[r, h // 2, qb * P:(qb + 1) * P], qk[r, 4 + h // 2, :], start=True, stop=False)
                        mm(o, ident[0:NF, h:h + 1].to_broadcast([NF, P]), crow[:, 4, :], start=False, stop=False)
                        last = mm(o, ident, tab("m_le")[:, qb * T:(qb + 1) * T], start=False, stop=True)
                elif kind == "xat":
                    for qb in range(TB):
                        for k in range(2):
                            last = mm(b[:, qb * T:(qb + 1) * T], qx[:, 2 * h + k, qb * P:(qb + 1) * P],
                                      kx[:, 2 * h + k, :], start=(k == 0), stop=(k == 1))
                elif q is None:
                    for qb in range(TB):
                        last = mm(b[:, qb * T:(qb + 1) * T], qa[:, h, qb * P:(qb + 1) * P], ka[:, h, CTX],
                                  start=True, stop=True)
                else:
                    last = mm(b[:, :], qa[:, h, T + q * P:T + (q + 1) * P], ka[:, h, :], start=True, stop=True)
                last.then_inc(S("sm_s"), 1)

            def transposes(i):
                q = UNITS[i][2]
                pe.wait_ge(S("sm_p"), i + 1)
                if i:
                    pe.wait_ge(S("sm_pt"), i)
                for j in range(4):
                    to = j if q is not None else (j % 2) * 2 + j // 2
                    last = pe.transpose(bank[6][:, to * P:(to + 1) * P], prob[i % 2][:, j * P:(j + 1) * P], ident)
                last.then_inc(S("sm_tr"), 1)

            def weighted(i):
                kind, h, q = UNITS[i]
                pe.wait_ge(S("sm_pt"), i + 1)
                if i:
                    pe.wait_ge(S("sm_out"), i)
                pt = probT[i % 2].rearrange("p (k q) -> p k q", k=2 if q is None else 4)
                if kind == "fox":
                    r = slice((h % 2) * HD, (h % 2) * HD + HD)
                    for kb in range(TB):
                        last = mm(bank[7][r, 0:T], v1[:, kb, h * HD:(h + 1) * HD], pt[:, kb, :],
                                  start=(kb == 0), stop=(kb == TB - 1))
                elif kind == "xat":
                    for m in range(2):
                        for kb in range(TB):
                            c = h * 256 + m * P
                            last = mm(bank[7][:, m * T:(m + 1) * T], vx[:, kb, c:c + P], pt[:, kb, :],
                                      start=(kb == 0), stop=(kb == TB - 1))
                else:
                    nk, nq = (2, T) if q is None else (4, P)
                    for kb in range(nk):
                        last = mm(bank[7][0:MD, 0:nq], va[:, kb, h * MD:(h + 1) * MD], pt[:, kb, :],
                                  start=(kb == 0), stop=(kb == nk - 1))
                last.then_inc(S("sm_o"), 1)

            wait_emptied(pe, "v", 3)
            pe.wait_ge(S("table_in"), 16)
            pe.wait_ge(S("fox_c"), 1)
            pe.wait_ge(S("u_l"), U_AT["mem"] + 8)
            for i in range(NF + 2):
                if i < NF:
                    scores(i)
                    if i < 4:
                        linear("xkv", i, S_XKV + 2 * i, CTX)
                    else:
                        token_major("xkv", i, S_XKV + 2 * i, 0)
                if 1 <= i <= NF:
                    transposes(i - 1)
                if i >= 2:
                    weighted(i - 2)

            def sb_z(h, b):
                r = slice((h % 2) * HD, (h % 2) * HD + HD)
                return [(b[:, kb * T:(kb + 1) * T], qk[r, 12 + h // 2, kb * P:(kb + 1) * P], qk[r, 8 + h // 2, :])
                        for kb in range(TB)]

            for h in range(NF + 2):
                if h < NF:
                    if h >= 2:
                        pe.wait_ge(S("sb_softplus"), h - 1)
                    else:
                        pe.wait_ge(S("sm_exp"), NF)
                    for o, a, b in sb_z(h, bank[4 + h % 2]):
                        last = mm(o, a, b, start=True, stop=True)
                    last.then_inc(S("sb_z"), 1)
                if 1 <= h <= NF:
                    g = h - 1
                    pe.wait_ge(S("sb_log"), g + 1)
                    if g:
                        pe.wait_ge(S("sb_arg"), g)
                    else:
                        pe.wait_ge(S("sm_pt"), NF)
                    logs = sbt[g % 2][:, 1, :].rearrange("p (k t) -> p k t", k=2)
                    for kb, (o, a, b) in enumerate(sb_z(g, bank[6])):
                        mm(o, a, b, start=True, stop=False)
                        last = mm(o, tab("ntri"), logs[:, kb, :], start=False, stop=(kb == 1))
                        if kb == 0:
                            last = mm(o, tab("nones"), logs[:, 1, :], start=False, stop=True)
                    last.then_inc(S("sb_t"), 1)
                if h == 2:
                    pe.wait_ge(S("sm_out"), NF)
                    norm("fox", P, T)
                    pe.wait_ge(S("norm_rstd"), NORM["fox"] + 1)
                if h >= 2:
                    g = h - 2
                    pe.wait_ge(S("sb_w"), g + 1)
                    if g:
                        pe.wait_ge(S("sb_out"), g)
                    r = slice((g % 2) * HD, (g % 2) * HD + HD)
                    wts = sbt[g % 2][:, 3, :].rearrange("p (k t) -> p k t", k=2)
                    for kb in range(TB):
                        last = mm(bank[7][r, 0:T], v1[:, kb, 512 + g * HD:512 + (g + 1) * HD], wts[:, kb, :],
                                  start=(kb == 0), stop=(kb == TB - 1))
                    last.then_inc(S("sb_o"), 1)
            norm("sb", P, T)
            for s in range(4):
                linear("out1", s, S_OUT + 2 * s, LAT, "fox")
            norm("xattn", P, T)
            for s in range(4):
                linear("xq", s, S_XQ + 2 * s, LAT, "xattn")
            wait_emptied(pe, "xq", 3)
            a = UNIT0["xat"]
            for i in range(NX + 2):
                if i < NX:
                    scores(a + i)
                if 1 <= i <= NX:
                    transposes(a + i - 1)
                if i >= 2:
                    weighted(a + i - 2)
            for s in range(4):
                linear("xo", s, S_XO + 2 * s, LAT, "xo")
            norm("ffn", P, T)
            pe.wait_ge(S("u_l"), U_AT["ffn"] + 8)
            wr = tab("w_route").rearrange("p (k f) -> p k f", k=KT)
            for b in range(TB):
                o = bank[6][:, b * 32:b * 32 + 20]
                mm(o, ones[0:1, :], tab("b_route", 1), start=True, stop=False)
                for k in range(KT):
                    t = slice(T + b * P, T + (b + 1) * P)
                    mm(o, uh[:, k, t].bitcast(F32), wr[:, k, :], start=False, stop=False)
                    last = mm(o, ul[:, k, t].bitcast(F32), wr[:, k, :], start=False, stop=(k == KT - 1))
                last.then_inc(S("rt_full"), 1)
            pe.wait_ge(S("rt_gate"), TB)
            for e in range(NE // 2):
                if e >= 2:
                    pe.wait_ge(S("gate_in"), e - 1)
                for j in range(2):
                    for b in range(TB):
                        w = 96 + 64 * b + 44 + 2 * e + j
                        last = mm(bank[4 + e % 2][:, j * T + b * P:j * T + (b + 1) * P],
                                  small[:, w:w + 1].to_broadcast([P, P]), ident, start=True, stop=True)
                last.then_inc(S("gate_full"), 1)
            pe.wait_ge(S("moe_lo"), 1)
            for j in range(4):
                b = claim("moe_y", j)
                mm(b[:, :], hidl[:, 0, 0:P], uh[:, 0, :], start=True, stop=False, skip_group_check=True)
            y0 = JOBS.number("moe_y")
            pe.wait_ge(S("gate_in"), NE // 2)
            pe.wait_ge(S("c_parts"), 1)
            with pe.Fori(0, NE // 2) as i:
                group = 0
                for e in range(2):
                    n = S_MOE + 10 * e
                    pe.wait_ge(S("moe_lo"), i * 2 + (e + 1))
                    for b, name in ((4, "moe_gate"), (5, "moe_up")):
                        for m in range(2):
                            parts_turn(i, 24, n)
                            for k in range(KT):
                                last = prod(bank[b][:, m * T:(m + 1) * T], n, k, uh[:, k, LAT], ul[:, k, LAT],
                                            k == 0, k == KT - 1)
                            n += 1
                        last.then_inc(S(name), 1)
                    for g in range(MOD_PIECES[e] // 4):
                        b = bank[6 + group % 2]
                        pe.wait_ge(S("mod_in"), i * 3 + (2 if group == 2 else 1))
                        for p in range(4):
                            parts_turn(i, 24, n)
                            for k in range(2):
                                c = cparts[:, 4 * (2 * p + k):4 * (2 * p + k) + 68]
                                s = n % RING
                                mm(b[0:68, :], c, wh[:, s, k * 512:(k + 1) * 512], start=(p + k == 0), stop=False)
                                last = mm(b[0:68, :], c, wl[:, s, k * 512:(k + 1) * 512], start=False,
                                          stop=(p == 3 and k == 1))
                            n += 1
                        last.then_inc(S("mod_full"), 1)
                        group += 1
                    pe.wait_ge(S("moe_lo"), i * 2 + (e + 2))
                    for k in range(2):
                        parts_turn(i, 24, n)
                        for m in range(KT):
                            last = prod(bank[(y0 + m // 2) % 4][:, (m % 2) * T:(m % 2 + 1) * T], n, m, hidh[:, k, :],
                                        hidl[:, k, :], False, False, skip_group_check=True)
                        n += 1
                    last.then_inc(S("moe_down"), 1)
            norm("fin1", P, T)

            for l in range(NL):
                cols = lin_cols(l)
                n = cols.stop - cols.start
                p0 = S_L + l * LAYER_PIECES
                norm(f"n1_{l}", P, 2 * T)

                def tiles_of(phase, j, p, width, cc, ready=None):
                    b = claim(phase, j)
                    w = cc.stop - cc.start
                    parts(p)
                    for k in range(KT):
                        if ready:
                            pe.wait_ge(S("u_l"), U_AT[ready] + k + 1)
                        last = prod(b[0:width, 0:w], p, k, uh[:, k, cc], ul[:, k, cc], k == 0, k == KT - 1, m=width)
                    finish(last)

                for j in range(8):
                    tiles_of(f"mqk_{l}", j, p0 + j, MD, cols if j < 4 else ALL, f"n1_{l}" if j == 0 else None)
                    if j == 0:
                        pe.wait_ge(S(f"lw_in{l}"), 16)
                        wg = ltab("w_g").rearrange("p (k g) -> p k g", k=KT)
                        for d in range(2):
                            if d == 1:
                                pe.wait_ge(S("norm_rstd"), NORM[f"n1_{l}"] + 1)
                            for g in range(2):
                                b = bank[4 + 2 * d + g]
                                for k in range(KT):
                                    c = 4 * (2 * d + g)
                                    o = b[32 * d:32 * d + MH, :]
                                    mm(o, wg[:, k, c:c + 4], uh[:, k, :].bitcast(F32), start=(k == 0), stop=False)
                                    last = mm(o, wg[:, k, c:c + 4], ul[:, k, :].bitcast(F32), start=False,
                                              stop=(k == KT - 1))
                            last.then_inc(S("ml_g_full"), 1)
                banks = [claim(f"mv_{l}", j) for j in range(4)]
                for s in range(4):
                    parts(p0 + 8 + s)
                    for tb in range(4):
                        for k in range(2):
                            t = slice(tb * P, (tb + 1) * P)
                            last = prod_t(banks[tb][:, 0:384], p0 + 8 + s, k * 384, 384, uh[:, 2 * s + k, t],
                                          ul[:, 2 * s + k, t], s + k == 0, s == 3 and k == 1)
                        if s == 3:
                            finish(last)
                for j in range(4):
                    tiles_of(f"mo_{l}", j, p0 + 12 + j, MD, cols)
                for j in range(2):
                    tiles_of(f"cq_{l}", j, p0 + 16 + j, P, cols)
                tiles_of(f"ckv_{l}", 0, p0 + 18, P, ALL)
                tiles_of(f"ckv_{l}", 1, p0 + 19, MD, ALL)
                for j in range(2):
                    tiles_of(f"pf_{l}", j, p0 + 20 + j, P, cols)
                for d in range(2):
                    pe.wait_ge(S("ml_rows"), 2 * l + d + 1)
                    for kb in range(4):
                        last = mm(bank[4 + d][:, kb * MH:(kb + 1) * MH], rows[d][:, 0, kb * P:(kb + 1) * P],
                                  row_ident[d], start=True, stop=True)
                    last.then_inc(S("gcol_full"), 1)
                norm(f"cq_{l}", P, n)
                norm_ckv = f"ckv_{l}"
                pe.wait_ge(S("norm_rstd"), NORM[f"cq_{l}"] + 1)
                norm(norm_ckv, P, 512)
                pe.wait_ge(S("norm_out"), normed(f"cq_{l}")[1])
                uq = ltab("uq").rearrange("p (k c) -> p k c", k=2)
                for h in range(MH):
                    b = claim(f"uq_{l}", h)
                    for k in range(2):
                        last = mm(b[0:MD, 0:n], uq[:, k, h * MD:(h + 1) * MD], cq[:, k, cols],
                                  start=(k == 0), stop=(k == 1))
                    finish(last)
                for h in range(MH + 1):
                    b = claim(f"rot_{l}", h)
                    if h < MH:
                        wait_emptied(pe, f"uq_{l}", h)
                    src = qa[:, h, LAT] if h < MH else kr[:, LAT]
                    finish(mm(b[0:MD, 0:T], tab("rot", MD), src, start=True, stop=True))
                pe.wait_ge(S("norm_out"), normed(f"ckv_{l}")[1])
                ukv = ltab("ukv")
                for h in range(MH):
                    b = claim(f"kn_{l}", h)
                    finish(mm(b[0:64, :], ukv[:, h * 64:(h + 1) * 64], ckv[:, :], start=True, stop=True))
                for j in range(4):
                    b = claim(f"va_{l}", j)
                    finish(mm(b[:, 0:384], ckv[:, j * P:(j + 1) * P], ukv[:, 256:640], start=True, stop=True))
                cn = tab("cn").rearrange("p (b n) -> p b n", b=2)
                sn = tab("sn").rearrange("p (b n) -> p b n", b=2)
                for s in range(n // T):
                    c0 = cols.start + s * T
                    for ft in range(2):
                        b = claim(f"fa{s}_{l}", ft)
                        wait_emptied(pe, f"pf_{l}", ft)
                        for nb in range(TB):
                            last = mm(b[:, nb * T:(nb + 1) * T], pf[:, ft, c0 + nb * P:c0 + (nb + 1) * P],
                                      tab("cdsd"), start=True, stop=True)
                        finish(last)
                    for ft in range(2):
                        b = claim(f"fy{s}_{l}", ft)
                        wait_emptied(pe, f"fa{s}_{l}", ft)
                        for nb in range(TB):
                            mm(b[:, 0:T], fa[:, ft, nb, 0:P], cn[:, nb, :], start=(nb == 0), stop=False)
                            last = mm(b[:, 0:T], fa[:, ft, nb, P:2 * P], sn[:, nb, :], start=False, stop=(nb == 1))
                        finish(last)
                pe.wait_ge(S("mla_keys"), l + 1)
                wait_emptied(pe, f"va_{l}", 3)
                units = range(UNIT0["mctx0"], UNIT0["mlat1"]) if l == 0 else range(UNIT0["mlat1"], len(UNITS))
                for i in range(units.start, units.stop + 2):
                    if i < units.stop:
                        scores(i)
                    if units.start < i <= units.stop:
                        transposes(i - 1)
                    if i >= units.start + 2:
                        weighted(i - 2)
                pe.wait_ge(S("sm_out"), units.stop)
                pe.wait_ge(S("conv_done"), 8 * l + 8)
                for h in range(MH):
                    g = l * MH + h

                    def spread(what, d):
                        c = 4 * g + 2 * (what - 3) + d
                        if c:
                            pe.wait_ge(S("ml_b_in"), c)
                        m = P if what == 3 else MD
                        mm(bank[6][0:m, cols], row_ident[d][:, h:h + 1].to_broadcast([MH, m]),
                           rows[d][:, what, cols], start=True, stop=True).then_inc(S("ml_b"), 1)

                    def keys(kb):
                        kk = 4 * g + kb
                        if kk >= 2:
                            pe.wait_ge(S("ml_p"), kk - 1)
                        tc = cols if kb < 2 else LAT
                        mm(bank[4 + kb % 2][:, tc], qc[:, 4 + h, kb * P:(kb + 1) * P], qc[:, h, tc],
                           start=True, stop=True).then_inc(S("ml_s"), 1)

                    def values(kb):
                        kk = 4 * g + kb
                        pe.wait_ge(S("ml_p"), kk + 1)
                        tc = cols if kb < 2 else LAT
                        for d in range(2):
                            p = sq[:, 2 * (kb % 2) + d, :]
                            mm(bank[mlb(l, 2 * d)][0:MD, tc], mv[:, kb, h * MD:(h + 1) * MD], p[:, tc],
                               start=(kb == 0), stop=(kb == 3), skip_group_check=True)
                            last = mm(bank[mlb(l, 2 * d + 1)][0:MD, tc], ones[:, 0:MD], p[:, tc],
                                      start=(kb == 0), stop=(kb == 3), skip_group_check=True)
                        last.then_inc(S("ml_v"), 1)

                    spread(3, 0)
                    keys(0)
                    spread(3, 1)
                    keys(1)
                    spread(4, 0)
                    spread(4, 1)
                    if h == 0:
                        for j in range(4):
                            claim(f"mlstm_{l}", j)
                    else:
                        pe.wait_ge(S("ml_sum"), g)
                    values(0)
                    if h:
                        norm(f"head_{l}_{h - 1}", MD, n)
                    keys(2)
                    values(1)
                    keys(3)
                    values(2)
                    values(3)
                norm(f"head_{l}_{MH - 1}", MD, n)
                srcs = [(uh[0:MD, j, cols], ul[0:MD, j, cols], MD) for j in range(8)] \
                    + [(yfh[:, j, cols], yfl[:, j, cols], P) for j in range(2)]
                s = p0 + N_IN2
                for m in range(KT):
                    b = claim(f"out_{l}", m)
                    for k, (xh, xl, nr) in enumerate(srcs):
                        if m == 0:
                            step = {7: 9, 8: 7, 9: 8}.get(k, k)
                            pe.wait_ge(S("u_l"), U_AT[f"y_{l}"] + (10 if k == 7 else step + 1))
                        t = m * len(srcs) + k
                        if t % 8 == 0:
                            parts(s + t // 8)
                        last = prod(b[:, 0:n], s + t // 8, t % 8, xh, xl, k == 0, k == len(srcs) - 1, nr=nr)
                    finish(last)
                norm(f"n2_{l}", P, n)
                for half, name in enumerate("ab"):
                    pu = p0 + N_IN2 + N_OUT2 + half * 32
                    b0 = JOBS.number(f"up{name}_{l}")
                    if half == 0:
                        pe.wait_ge(S("u_l"), U_AT[f"n2_{l}"] + 8)
                    e_dve, e_act = JOBS.emptied(b0 - 1)[1], JOBS.emptied(b0)[1]
                    with pe.Fori(0, MC // 4) as i:
                        for j in range(4):
                            parts_turn(i, 4, pu + j)
                            pe.wait_ge(S("job_emptied_dve"), e_dve - (j == 0))
                            pe.wait_ge(S("job_emptied_act"), i * 4 + (e_act - 4 + j))
                            for k in range(KT):
                                last = prod(bank[(b0 + j) % 4][:, 0:n], pu + j, k, uh[:, k, cols], ul[:, k, cols],
                                            k == 0, k == KT - 1)
                            last.then_inc(S("job_full"), 1)
                    pd = pu + MC
                    b0 = JOBS.number(f"dn{name}_{l}")
                    e_dve, e_act = JOBS.emptied(b0)[1], JOBS.emptied(b0 - 1)[1]
                    pe.wait_ge(S("hid_lo"), 2 + MC * (2 * l + half + 1))
                    with pe.Fori(0, 4) as i:
                        for m in range(2):
                            pe.wait_ge(S("job_emptied_dve"), i * 2 + (e_dve - 2 + m))
                            for part in range(2):
                                parts_turn(i, 4, pd + 2 * m + part)
                                for k in range(8):
                                    last = prod(bank[(b0 + m) % 4][:, 0:n],
                                                pd + 2 * m + part, k, hh[:, part * 8 + k, 0:n],
                                                hl[:, part * 8 + k, 0:n], part + k == 0, part == 1 and k == 7)
                            last.then_inc(S("job_full"), 1)
            norm("fin2", P, T)

        @block.vector
        def _(dve):
            ch = Chain(dve, "dve_step")
            tt, ts, stt = dve.tensor_tensor, dve.tensor_scalar, dve.scalar_tensor_tensor
            lo_at = [0]

            def lo_part(s, count):
                dve.wait_ge(S("w_hi"), count)
                tt(wl[:, s, :], ring[:, s, :], wh[:, s, :].bitcast(F32), ALU.subtract).then_inc(S("w_lo"), 1)

            def split(to):
                while lo_at[0] <= min(to, N_PIECES - 1):
                    lo_part(lo_at[0] % RING, lo_at[0] + 1)
                    lo_at[0] += 1

            def split_turn(i, per, base, lo, hi):
                for j in range(lo, hi + 1):
                    lo_part((base + j) % RING, i * per + (base + j + 1))

            def add_square(name, t, p, n):
                first = 0 if name in LOOPED else 1
                dve.wait_ge(S("norm_sq"), SQ_AT[name] + t + 1)
                if t > first:
                    dve.wait_ge(S("norm_add"), ADD_AT[name] + t - first)
                tt(sq[0:p, 3, 0:n], sq[0:p, 3, 0:n], sq[0:p, t % 2, 0:n], ALU.add).then_inc(S("norm_add"), 1)

            def add_squares(name, n):
                for t in range(1, STEPS[name]):
                    add_square(name, t, P, n)

            def rest(name, i, parts):
                dve.wait_ge(S("u_h"), U_AT[name] + i + 1)
                for lo, v, hi, shift in parts:
                    if shift is None:
                        last = tt(lo, v, hi.bitcast(F32), ALU.subtract)
                    else:
                        last = stt(lo, v, shift, hi.bitcast(F32), ALU.add, ALU.subtract)
                last.then_inc(S("u_l"), 1)

            def norm(name, steps):
                dve.wait_ge(S("norm_rstd"), NORM[name] + 1)
                done = []
                for i, (parts, lows) in enumerate(steps):
                    for o, src, g, r in parts:
                        last = stt(o, src, g, r, ALU.mult, ALU.mult)
                    last.then_inc(S("u_v"), 1)
                    done.append(lows)
                    if i >= 2:
                        rest(name, i - 2, done[i - 2])
                for i in range(max(0, len(done) - 2), len(done)):
                    rest(name, i, done[i])
                return last

            def norm_tiles(name, src, gain, cols, scols, first=0, k=KT):
                g = tab(gain)
                steps = []
                for j in range(k):
                    t = first + j
                    steps.append(([(uv[:, t, cols], src[:, t, scols], g[:, j:j + 1], rstd[:, 0:T])],
                                  [(ul[:, t, cols], uv[:, t, cols], uh[:, t, cols], None)]))
                norm(name, steps)

            def smv(i, what, k, w=1):
                a = (i % 2) * 8 + what * 2 + k
                return small[:, a:a + w]

            def neg_max(i):
                g = 1 if UNITS[i][2] is not None else 2
                dve.wait_ge(S("sm_s"), i + 1)
                b = bank[4 + i % 2][:, :].rearrange("p (g w) -> p g w", g=g)
                dve.tensor_reduce(smv(i, 0, 0, g), b, AX_X, ALU.max, negate=True).then_inc(S("sm_max"), 1)

            def divide(i):
                g = 1 if UNITS[i][2] is not None else 2
                w = 512 // g
                dve.wait_ge(S("sm_exp"), i + 1)
                ch.link(dve.reciprocal(smv(i, 1, 0, g), smv(i, 2, 0, g)))
                for k in range(g):
                    p = prob[i % 2][:, k * w:(k + 1) * w]
                    last = ts(p, p, smv(i, 1, k), None, ALU.mult)
                last.then_inc(S("sm_p"), 1)

            def out_of(i):
                kind, h, q = UNITS[i]
                dve.wait_ge(S("sm_o"), i + 1)
                if kind == "fox":
                    r = slice((h % 2) * HD, (h % 2) * HD + HD)
                    last = dve.tensor_copy(heads[r, h // 2, :], bank[7][r, 0:T])
                elif kind == "xat":
                    last = dve.tensor_copy(uv[:, 2 * h:2 * h + 2, LAT],
                                           bank[7][:, :].rearrange("p (a t) -> p a t", a=2))
                elif q is None:
                    last = dve.tensor_copy(ya[:, h, CTX], bank[7][0:MD, 0:T])
                else:
                    last = dve.tensor_copy(ya[:, h, T + q * P:T + (q + 1) * P], bank[7][0:MD, 0:P])
                last.then_inc(S("sm_out"), 1)

            dve.wait_ge(S("c_exp"), 1)
            ch.link(ts(small[:, 64:80], small[:, 64:80], 1.0, None, ALU.add))
            ch.link(dve.reciprocal(small[:, 64:80], small[:, 64:80]))
            ch.link(tt(small[:, 64:80], small[:, 64:80], tab("c"), ALU.mult))
            ch.link(ts(cparts[:, :], ones[:, 0:100], 0.0, None, ALU.mult))
            silu_c = small[:, 64:80].rearrange("p (k c) -> p k c", k=KT)
            cp = cparts[:, 0:32].rearrange("p (k c) -> p k c", k=KT)
            ch.link(dve.tensor_copy(cp[:, :, 0:2], silu_c))
            tt(cp[:, :, 2:4], silu_c, cp[:, :, 0:2].bitcast(F32), ALU.subtract).then_inc(S("c_parts"), 1)

            add_squares("mix", 512)
            norm_tiles("mix", res, "g_mix", LAT, LAT)
            for s in range(8):
                split(S_QK + 2 * s + 1 + AHEAD)
                if s == 0:
                    add_squares("mem", 512)
                    dve.wait_ge(S("fox_f_full"), 1)
                    ts(crow[:, 0, :], bank[6][0:NF, 0:T], tab("b_forget", NF), None, ALU.add).then_inc(S("fox_f"), 1)
                if s == 2:
                    norm_tiles("mem", res, "g_mem", CTX, CTX)
                if s == 4:
                    dve.wait_ge(S("fox_ln"), 1)
                    ch.link(stt(crow[:, 2, :], crow[:, 0, :], 0.0, crow[:, 1, :], ALU.min, ALU.subtract))
                    ch.link(dve.tensor_tensor_scan(out=crow[:, 3, :], data0=crow[:, 2, :], data1=crow[:, 2, :],
                                                   initial=0.0, op0=ALU.add, op1=ALU.bypass))
                    ts(crow[:, 4, :], crow[:, 3, :], -1.0, None, ALU.mult).then_inc(S("fox_c"), 1)
            split(S_V + 7 + AHEAD)
            for i in range(NF + 2):
                if i < NF:
                    neg_max(i)
                    divide(i)
                    split(S_XKV + 2 * i + 1 + AHEAD)
                if i >= 2:
                    out_of(i - 2)

            for h in range(NF + 2):
                if h < NF:
                    t = sbt[h % 2]
                    dve.wait_ge(S("sb_ln"), h + 1)
                    stt(t[:, 1, :], bank[4 + h % 2][:, :], 0.0, t[:, 0, :], ALU.max,
                        ALU.add).then_inc(S("sb_softplus"), 1)
                    dve.wait_ge(S("sb_softplus"), h + 1)
                    logs = t[:, 1, :].rearrange("p (k t) -> p k t", k=2)
                    stt(logs, m_ge[:, :, 0:T], 0.0, logs, ALU.is_ge, ALU.mult).then_inc(S("sb_log"), 1)
                if 1 <= h <= NF:
                    g = h - 1
                    dve.wait_ge(S("sb_t"), g + 1)
                    tt(sbt[g % 2][:, 2, :].rearrange("p (k t) -> p k t", k=2),
                       bank[6][:, :].rearrange("p (k t) -> p k t", k=2), m_ge[:, :, 0:T],
                       ALU.add).then_inc(S("sb_arg"), 1)
                if h == 2:
                    add_squares("fox", 512)
                if h >= 2:
                    g = h - 2
                    r = slice((g % 2) * HD, (g % 2) * HD + HD)
                    dve.wait_ge(S("sb_o"), g + 1)
                    dve.tensor_copy(heads[r, 4 + g // 2, :], bank[7][r, 0:T]).then_inc(S("sb_out"), 1)
                if h == 4:
                    dve.wait_ge(S("norm_rstd"), NORM["fox"] + 1)
                    g = tab("g_fox")
                    for j in range(4):
                        stt(uv[:, j, LAT], heads[:, j, :], g[:, j:j + 1], rstd[:, 0:T], ALU.mult,
                            ALU.mult).then_inc(S("u_v"), 1)
            add_squares("sb", 512)
            for j in range(4):
                rest("fox", j, [(ul[:, j, LAT], uv[:, j, LAT], uh[:, j, LAT], None)])
            g = tab("g_sb")
            norm("sb", [([(uv[:, 4 + j, LAT], heads[:, 4 + j, :], g[:, j:j + 1], rstd[:, 0:T])],
                         [(ul[:, 4 + j, LAT], uv[:, 4 + j, LAT], uh[:, 4 + j, LAT], None)]) for j in range(4)])

            def add_to_res(phase, name, first):
                for s in range(4):
                    split(first + 2 * s + 1 + AHEAD)
                    b = full(dve, phase, s)
                    r = res[:, 2 * s:2 * s + 2, LAT]
                    emptied(tt(r, b[:, :].rearrange("p (a t) -> p a t", a=2), r, ALU.add), "dve")
                    if s >= 2:
                        add_square(name, s - 1, P, 512)
                add_square(name, 3, P, 512)

            add_to_res("out1", "xattn", S_OUT)
            norm_tiles("xattn", res, "g_xattn", LAT, LAT)
            split(S_XQ + 7 + AHEAD)
            a = UNIT0["xat"]
            for i in range(NX + 3):
                if i < NX:
                    neg_max(a + i)
                    divide(a + i)
                if 2 <= i < NX + 2:
                    out_of(a + i - 2)
                if i >= 3:
                    j = 2 * (i - 3)
                    rest("xo", i - 3, [(ul[:, j:j + 2, LAT], uv[:, j:j + 2, LAT], uh[:, j:j + 2, LAT], None)])
            add_to_res("xo", "ffn", S_XO)
            norm_tiles("ffn", res, "g_ffn", LAT, LAT)

            def first_of(dst, src, best, tmp):
                ch.link(ts(tmp, src, best, None, ALU.is_ge))
                ch.link(tt(tmp, tmp, tab("w4"), ALU.mult))
                ch.link(dve.tensor_reduce(tmp1, tmp, AX_X, ALU.max))
                ch.link(ts(dst, tmp, tmp1, None, ALU.is_equal))

            for b in range(TB):
                r = small[:, 96 + 64 * b:160 + 64 * b]
                tmp1 = r[:, 28:29]
                ones_g, in_g, best, oh1 = r[:, 32:36], r[:, 36:40], r[:, 29:30], r[:, 40:44]
                tmp = small[:, 80:84]
                dve.wait_ge(S("rt_full"), TB)
                ch.link(dve.tensor_copy(r[:, 0:20], bank[6][:, b * 32:b * 32 + 20]))
                ch.link(dve.tensor_reduce(best, r[:, 0:4], AX_X, ALU.max))
                ts(r[:, 20:21], best, -1.0, None, ALU.mult).then_inc(S("rt_max"), 1)
                first_of(ones_g, r[:, 0:4], best, tmp)
                ch.link(ts(in_g, r[:, 4:8], ones_g[:, 0:1], None, ALU.mult))
                for g in range(1, 4):
                    ch.link(stt(in_g, r[:, 4 + 4 * g:8 + 4 * g], ones_g[:, g:g + 1], in_g, ALU.mult, ALU.add))
                m1, m2 = small[:, 84:85], small[:, 85:86]
                ch.link(dve.tensor_reduce(m1, in_g, AX_X, ALU.max))
                first_of(oh1, in_g, m1, tmp)
                ch.link(stt(in_g, oh1, BIG, in_g, ALU.mult, ALU.add))
                ch.link(dve.tensor_reduce(m2, in_g, AX_X, ALU.max))
                tt(r[:, 23:24], m2, m1, ALU.subtract).then_inc(S("rt_diff"), 1)
                first_of(small[:, 88:92], in_g, m2, tmp)
                dve.wait_ge(S("rt_exp2"), b + 1)
                wa, wb = small[:, 92:93], small[:, 93:94]
                ch.link(ts(wa, r[:, 22:23], 1.0, r[:, 21:22], ALU.add, ALU.mult))
                ch.link(dve.reciprocal(wa, wa))
                ch.link(tt(wb, wa, r[:, 22:23], ALU.mult))
                ch.link(ts(tmp, small[:, 88:92], wb, None, ALU.mult))
                ch.link(stt(tmp, oh1, wa, tmp, ALU.mult, ALU.add))
                for g in range(4):
                    last = ts(r[:, 44 + 4 * g:48 + 4 * g], tmp, ones_g[:, g:g + 1], None, ALU.mult)
                last.then_inc(S("rt_gate"), 1)

            ts(hidl[:, 0, 0:P], ones, 0.0, None, ALU.mult).then_inc(S("moe_lo"), 1)
            dve.memset(modv[:, 0:8], 0.0).then_inc(S("mod_in"), 1)
            split(S_MOE + 2)
            dve.wait_ge(S("gate_in"), NE // 2)
            with dve.Fori(0, NE // 2) as i:
                ch.loop(i, 2 + 3)

                def turn_mod(q, b, end, done):
                    split_turn(i, 24, S_MOE, done, end + AHEAD)
                    dve.wait_ge(S("mod_full"), i * 3 + (q + 1))
                    ch.link(dve.transpose(turned[:, :, :].rearrange("p a b -> p (a b)"), b[0:32, :]))
                    for c in range(4):
                        o = modv[32 * c:32 * c + 32, bass.ds(i * 24 + 8 * q, 8)].rearrange("p (t w) -> p t w", w=2)
                        last = tt(o, turned[:, c:16:4, 0:2], turned[:, c:16:4, 2:4], ALU.add)
                    last.then_inc(S("mod_in"), 1)
                    dve.wait_ge(S("mod_in"), i * 3 + (q + 2))
                    return end + AHEAD + 1

                done = AHEAD
                for e, (gate_end, up_end) in enumerate(((1, 3), (11, 13))):
                    split_turn(i, 24, S_MOE, done, gate_end + AHEAD)
                    dve.wait_ge(S("moe_silu"), i * 2 + (e + 1))
                    for k in range(2):
                        e_k = eg[:, k * T:(k + 1) * T]
                        last = tt(e_k, e_k, gates[:, bass.ds(i * 2 + e, 1), :].rearrange("p a t -> p (a t)"), ALU.mult)
                    ch.link(last)
                    split_turn(i, 24, S_MOE, gate_end + AHEAD + 1, up_end + AHEAD)
                    dve.wait_ge(S("moe_up"), i * 2 + (e + 1))
                    tt(eg[:, :], bank[5][:, :], eg[:, :], ALU.mult).then_inc(S("moe_v"), 1)
                    dve.wait_ge(S("moe_hi"), i * 2 + (e + 1))
                    tt(hidl[:, :, :].rearrange("p a t -> p (a t)"), eg[:, :],
                       hidh[:, :, :].rearrange("p a t -> p (a t)").bitcast(F32), ALU.subtract).then_inc(S("moe_lo"), 1)
                    done = up_end + AHEAD + 1
                    if e == 0:
                        done = turn_mod(0, bank[6], 7, done)
                    else:
                        done = turn_mod(1, bank[7], 17, done)
                        done = turn_mod(2, bank[6], 21, done)
                split_turn(i, 24, S_MOE, done, 23 + AHEAD)
            ch.end(NE // 2)
            lo_at[0] = S_L + AHEAD
            for s in range(4):
                if s == 0:
                    dve.wait_ge(S("moe_down"), NE)
                b = bank[JOBS.number("moe_y", s) % 4]
                r = res[:, 2 * s:2 * s + 2, LAT]
                emptied(tt(r, b[:, :].rearrange("p (a t) -> p a t", a=2), r, ALU.add), "dve")
                if s >= 2:
                    add_square("fin1", s - 1, P, 512)
            add_square("fin1", 3, P, 512)
            ch.link(tt(modv[:, :], modv[:, :], tab("b_mod"), ALU.add))
            for l in range(NL):
                for k2 in range(2):
                    c = 2 * (l * 48 + 8 + 24 * k2)
                    ch.link(stt(gmod[:, 2 * l + k2, :], modv[:, c:c + 16], 1.0, tab(f"g{k2 + 1}_{l}"),
                                ALU.add, ALU.mult))
            dve.wait_ge(S("norm_rstd"), NORM["fin1"] + 1)
            g = tab("g_fin1")
            for j in range(KT):
                last = stt(res[:, j, LAT], res[:, j, LAT], g[:, j:j + 1], rstd[:, 0:T], ALU.mult, ALU.mult)
            last.then_inc(S("norm_out"), 1)

            def norm_mod(l, k2):
                g = gmod[:, 2 * l + k2, :]
                first = l * 48 + (0 if k2 == 0 else 24)
                off = 0 if (k2 == 0 or l == 0) else T
                steps = []
                for k in range(KT):
                    vals, lows = [], []
                    for which, cols in ((0, LAT), (1, CTX)):
                        if off and which:
                            continue
                        vals.append((uv[:, k, cols], res[:, k, cols], g[:, 2 * k + which:2 * k + which + 1],
                                     rstd[:, cols.start - off:cols.stop - off]))
                        c = 2 * (first + k) + which
                        lows.append((ul[:, k, cols], uv[:, k, cols], uh[:, k, cols], modv[:, c:c + 1]))
                    steps.append((vals, lows))
                norm(f"n{k2 + 1}_{l}", steps)
    
            for l in range(NL):
                cols = lin_cols(l)
                n = cols.stop - cols.start
                p0 = S_L + l * LAYER_PIECES
                if l == 0:
                    add_squares("n1_0", 512)
                norm_mod(l, 0)
                bg = tab(f"b_g_{l}")
                for d in range(2):
                    dve.wait_ge(S("ml_g_full"), 2 * l + d + 1)
                    rr, r = rows[d], slice(32 * d, 32 * d + MH)
                    ts(rr[:, 0, :], bank[4 + 2 * d][r, :], bg[r, 2 * d:2 * d + 1], None, ALU.add)
                    ts(rr[:, 1, :], bank[5 + 2 * d][r, :], bg[r, 2 * d + 1:2 * d + 2], None,
                       ALU.add).then_inc(S("ml_f"), 1)
                dve.wait_ge(S("ml_f"), 2 * l + 2)
                dve.memset(qkp[:, :, :, 0:2], 0.0)
                ch.link(dve.memset(qkp[:, :, :, 258:260], 0.0))

                def gate_rows(d):
                    rr = rows[d]
                    dve.wait_ge(S("ml_ln"), 2 * l + d + 1)
                    ch.link(stt(rr[:, 1, :], rr[:, 1, :], 0.0, rr[:, 2, :], ALU.min, ALU.subtract))
                    if d == 0:
                        runs = [(slice(0, 512), False)]
                    else:
                        runs = [(slice(255, None, -1), False), (slice(511, 255, -1), True)]

                    def scan(dst, src, op):
                        for r, goes_on in runs:
                            init = rr[:, dst, 0:1] if goes_on else 0.0
                            ch.link(dve.tensor_tensor_scan(out=rr[:, dst, r], data0=rr[:, src, r],
                                                           data1=rr[:, src, r], initial=init, op0=op,
                                                           op1=ALU.bypass))

                    scan(2, 1, ALU.add)
                    ch.link(tt(rr[:, 0, :], rr[:, 0, :], rr[:, 2, :], ALU.subtract))
                    scan(3, 0, ALU.max)
                    ch.link(tt(rr[:, 4, :], rr[:, 2, :], rr[:, 3, :], ALU.add))
                    ts(rr[:, 3, :], rr[:, 3, :], -1.0, None, ALU.mult).then_inc(S("ml_rows"), 1)

                taps = tab(f"conv_{l}", MD).rearrange("p (h t) -> p h t", h=8)

                def conv(j):
                    wait_emptied(dve, f"mqk_{l}", j)
                    segs = slice(0, 2) if (l == 0 or j >= 4) else slice(1, 2)
                    cc = cols if j < 4 else ALL
                    o = qc[:, j, cc].rearrange("p (s t) -> p s t", t=T)
                    ch.link(ts(o, qkp[:, j, segs, 0:T], taps[:, j, 0:1], None, ALU.mult))
                    for t in range(1, 5):
                        last = stt(o, qkp[:, j, segs, t:t + T], taps[:, j, t:t + 1], o, ALU.mult, ALU.add)
                        if t < 4:
                            ch.link(last)
                    last.then_inc(S("conv_sum"), 1)

                for j in range(16):
                    split(p0 + j + AHEAD)
                    if j in (1, 2):
                        gate_rows(j - 1)
                    if 2 <= j < 10:
                        conv(j - 2)
                split(p0 + 19 + AHEAD)
                if l == 0:
                    add_squares("cq_0", 512)
                split(p0 + 21 + AHEAD)
                g = tab(f"g_qn_{l}")
                dve.wait_ge(S("norm_rstd"), NORM[f"cq_{l}"] + 1)
                for j in range(2):
                    last = stt(cq[:, j, cols], cq[:, j, cols], g[:, j:j + 1], rstd[:, 0:n], ALU.mult, ALU.mult)
                last.then_inc(S("norm_out"), 1)
                dve.wait_ge(S("norm_rstd"), NORM[f"ckv_{l}"] + 1)
                stt(ckv[:, :], ckv[:, :], tab(f"g_kvn_{l}"), rstd[:, :], ALU.mult, ALU.mult).then_inc(S("norm_out"), 1)
                for h in range(MH + 1):
                    b = full(dve, f"rot_{l}", h)
                    o = qa[:, h, LAT] if h < MH else kr[:, LAT]
                    t1 = sq[0:MD, 2 + h // 2, (h % 2) * T:(h % 2 + 1) * T]
                    tt(t1, b[0:MD, 0:T], tab("sin", MD), ALU.mult)
                    ch.link(tt(o, o, tab("cos", MD), ALU.mult))
                    emptied(tt(o, o, t1, ALU.add), "dve")
                dve.wait_ge(S("job_emptied_dve"), JOBS.emptied(JOBS.number(f"rot_{l}", MH))[1])
                for h in range(MH):
                    last = dve.tensor_copy(ka[64:96, h, :], kr[64:96, :])
                last.then_inc(S("mla_keys"), 1)
                units = range(UNIT0["mctx0"], UNIT0["mlat1"]) if l == 0 else range(UNIT0["mlat1"], len(UNITS))
                for i in range(units.start, units.stop + 2):
                    if i < units.stop:
                        neg_max(i)
                        divide(i)
                    if i >= units.start + 2:
                        out_of(i - 2)
                dve.wait_ge(S("sm_out"), units.stop)
                for h in range(MH):
                    rest(f"y_{l}", h, [(ul[0:MD, h, cols], ya[:, h, cols], uh[0:MD, h, cols], None)])

                rb, em = [ml[:, d, :] for d in range(2)], [ml[0:MD, 2 + d, :] for d in range(2)]
                arg, den = [ml[:, 4 + d, :] for d in range(2)], [ml[0:MD, 6 + d, :] for d in range(2)]
                masks = [m_ge[:, :, 1:T + 1], tab("m_le").rearrange("p (k t) -> p k t", k=2)]
                gm = tab(f"g_ml_{l}", MD)

                def head_value(h):
                    dve.wait_ge(S("norm_rstd"), NORM[f"head_{l}_{h}"] + 1)
                    d0 = den[0][:, cols]
                    stt(d0, d0, gm[:, h:h + 1], rstd[0:MD, 0:n], ALU.mult, ALU.mult).then_inc(S("norm_out"), 1)
                    dve.wait_ge(S("norm_out"), normed(f"head_{l}_{h}")[1])
                    tt(mo[:, h, cols], d0, mo[:, h, cols], ALU.mult).then_inc(S("u_v"), 1)

                def head_rest(h):
                    rest(f"y_{l}", MH + h if h < MH - 1 else 9,
                         [(ul[0:MD, MH + h, cols], mo[:, h, cols], uh[0:MD, MH + h, cols], None)])

                for h in range(MH):
                    g = l * MH + h

                    def args(kb):
                        if kb < 2 and l:
                            return
                        for d in range(2):
                            c = ml_args(l, h, kb, d)
                            if kb:
                                dve.wait_ge(S("ml_e"), 2 * (4 * g + kb - 1) + d + 1)
                            tc = CTX if kb < 2 else LAT
                            tt(arg[d][:, tc], rb[d][:, tc], masks[d][:, kb % 2, :], ALU.add).then_inc(S("ml_arg"), 1)

                    dve.wait_ge(S("ml_b_in"), 4 * g + 2)
                    args(0)
                    for kb in range(4):
                        kk = 4 * g + kb
                        tc = cols if kb < 2 else LAT
                        dve.wait_ge(S("ml_s"), kk + 1)
                        for d in range(2):
                            e = sq[:, 2 * (kb % 2) + d, :]
                            dve.wait_ge(S("ml_e"), 2 * kk + d + 1)
                            last = stt(e[:, tc], bank[4 + kb % 2][:, tc], MD ** -0.5, e[:, tc], ALU.mult, ALU.mult)
                        last.then_inc(S("ml_p"), 1)
                        if kb < 3:
                            args(kb + 1)
                        if h and kb == 2:
                            head_value(h - 1)
                        if h and kb == 3:
                            head_rest(h - 1)
                    dve.wait_ge(S("ml_v"), 4 * (g + 1))
                    dve.wait_ge(S("ml_b_in"), 4 * g + 4)
                    for d in range(2):
                        dve.wait_ge(S("ml_ln2"), 2 * g + d + 1)
                        stt(den[d][:, cols], den[d][:, cols], -1.0, em[d][:, cols], ALU.mult,
                            ALU.min).then_inc(S("ml_min"), 1)
                    for d in range(2):
                        dve.wait_ge(S("ml_rden"), 2 * g + d + 1)
                        last = tt(den[d][:, cols], bank[mlb(l, 2 * d)][0:MD, cols], den[d][:, cols], ALU.mult)
                    ch.link(last)
                    tt(den[0][:, cols], den[0][:, cols], den[1][:, cols], ALU.add).then_inc(S("ml_sum"), 1)
                for j in range(2):
                    rest(f"y_{l}", 7 + j, [(yfl[:, j, cols], yf[:, j, cols], yfh[:, j, cols], None)])
                head_value(MH - 1)
                head_rest(MH - 1)

                def gated(l, m, b, chunk):
                    for which, cc in ((1, CTX), (0, LAT)):
                        if l and which:
                            continue
                        c = 2 * (l * 48 + 8 * chunk + m) + which
                        src = b[:, cc] if l == 0 else b[:, 0:T]
                        last = stt(res[:, m, cc], src, modv[:, c:c + 1], res[:, m, cc], ALU.mult, ALU.add)
                    return last

                for m in range(KT):
                    split(p0 + N_IN2 + out_piece(m) + AHEAD)
                    b = full(dve, f"out_{l}", m)
                    emptied(gated(l, m, b, 2), "dve")
                    if m >= 2:
                        add_square(f"n2_{l}", m - 1, P, n)
                add_square(f"n2_{l}", KT - 1, P, n)
                norm_mod(l, 1)
                if l == 0:
                    for j in range(2):
                        dve.memset(small[:, 94 + j:95 + j], 0.0).then_inc(S("hid_lo"), 1)
                for half, name in enumerate("ab"):
                    pu = p0 + N_IN2 + N_OUT2 + half * 32
                    h0 = (2 * l + half) * MC
                    split(pu + AHEAD - 1)
                    with dve.Fori(0, MC // 4) as i:
                        for j in range(4):
                            split_turn(i, 4, pu, j + AHEAD, j + AHEAD)
                            dve.wait_ge(S("hid_hi"), i * 4 + (h0 + j + 1))
                            d = bass.ds(i * 4 + j, 1)
                            tt(hl[:, d, 0:n].rearrange("p a b -> p (a b)"), sq[:, 2 + j % 2, 0:n],
                               hh[:, d, 0:n].rearrange("p a b -> p (a b)").bitcast(F32),
                               ALU.subtract).then_inc(S("hid_lo"), 1)
                    lo_at[0] = pu + MC + AHEAD
                    pd = pu + MC
                    nxt = ("n1_1" if l == 0 else "fin2") if half else None
                    b0, f0 = JOBS.number(f"dn{name}_{l}"), JOBS.full(JOBS.number(f"dn{name}_{l}"))
                    if nxt:
                        dve.wait_ge(S("hid_lo"), 2 + MC * (2 * l + half + 1))
                        ch.link(dve.memset(sq[:, 3, :], 0.0))
                    ends = nxt and l == NL - 1

                    def down_turn(i, fixed=None):
                        for j in range(2):
                            dve.wait_ge(S("job_full"), i * 2 + (f0 + j))
                            for which, cc in ((1, CTX), (0, LAT)):
                                if l and which:
                                    continue
                                c = 2 * (l * 48 + 40 + j) + which
                                b = bank[(b0 + j) % 4]
                                src = b[:, cc] if l == 0 else b[:, 0:T]
                                if fixed is None:
                                    r = res[:, bass.ds(i * 2 + j, 1), cc].rearrange("p a b -> p (a b)")
                                    gate = modv[:, bass.ds(i * 4 + c, 1)]
                                else:
                                    r = res[:, 2 * fixed + j, cc]
                                    gate = modv[:, 4 * fixed + c:4 * fixed + c + 1]
                                last = stt(r, src, gate, r, ALU.mult, ALU.add)
                            last.then_inc(S("job_emptied_dve"), 1)
                        if nxt:
                            for j in range(2):
                                dve.wait_ge(S("norm_sq"), i * 2 + (SQ_AT[nxt] + j + 1))
                                dve.wait_ge(S("norm_add"), i * 2 + (ADD_AT[nxt] + j))
                                tt(sq[:, 3, 0:n], sq[:, 3, 0:n], sq[:, j, 0:n], ALU.add).then_inc(S("norm_add"), 1)

                    turns = 3 if ends else 4
                    with dve.Fori(0, turns) as i:
                        split_turn(i, 4, pd, AHEAD, AHEAD + 3)
                        down_turn(i)
                    if ends:
                        lo_at[0] = pd + 12 + AHEAD
                        split(pd + 15)
                        down_turn(3, 3)
                    lo_at[0] = pd + MC + AHEAD
            dve.wait_ge(S("norm_rstd"), NORM["fin2"] + 1)
            g = tab("g_fin2")
            for j in range(KT):
                last = stt(res[:, j, LAT], res[:, j, LAT], g[:, j:j + 1], rstd[:, 0:T], ALU.mult, ALU.mult)
            last.then_inc(S("norm_out"), 1)


def pack(inputs):
    f = {k: np.asarray(v) for k, v in inputs.items()}

    def fm(w, c0, c1, width=P, at=0):
        out = []
        for c in range(c0, c1, width):
            t = np.zeros((P, KT, P), np.float32)
            t[:, :, at:at + width] = w[:, c:c + width].reshape(KT, P, width).transpose(1, 0, 2)
            out.append(t.reshape(P, PIECE))
        return out

    def moving(w, c0, c1, k, width):
        out = []
        for c in range(c0, c1, width):
            for g in range(KT // k):
                t = np.zeros((P, PIECE), np.float32)
                part = w[g * k * P:(g + 1) * k * P, c:c + width].reshape(k, P, width).transpose(1, 0, 2)
                t[:, 0:k * width] = part.reshape(P, k * width)
                out.append(t)
        return out

    w = f["w_in"][0]
    slots = fm(w, 0, 1024) + fm(w, 1536, 2560) + moving(w, 1024, 1536, 4, T) + moving(w, 2560, 3072, 4, T)
    slots += fm(f["w_xkv"][0], 0, 1024) + moving(f["w_xkv"][0], 1024, 2048, 4, T)
    slots += fm(f["w_out"][0], 0, 1024) + fm(f["w_xq"][0], 0, 1024) + fm(f["w_xo"][0], 0, 1024)
    mods = [s for l in range(NL) for s in moving(f["w_mod_2"][l], 0, 6 * D, 2, 512)]
    for e in range(NE):
        n_mod = MOD_PIECES[e % 2]
        slots += fm(f["w_exp_gate"][0, e], 0, 256) + fm(f["w_exp_up"][0, e], 0, 256) + mods[0:n_mod]
        mods = mods[n_mod:]
        slots += list(f["w_exp_down"][0, e].reshape(2, P, D))
    assert not mods
    for l in range(NL):
        w = f["w_in_2"][l]
        slots += fm(w, 256, 256 + 768, MD) + moving(w, 1024, 1408, 2, 384) + fm(w, 1408, 1792, MD)
        slots += fm(w, 1808, 2064) + fm(w, 2064, 2192) + fm(w, 2192, 2224, RD, 64) + fm(w, 0, 256)
        wo = f["w_out_2"][l]
        t = np.zeros((P, 80, P), np.float32)
        rows = [(640 + MD * j, MD) for j in range(4)] + [(256 + MD * j, MD) for j in range(4)] + [(0, P), (P, P)]
        for m in range(KT):
            for k, (r0, nr) in enumerate(rows):
                t[0:nr, m * 10 + k, :] = wo[r0:r0 + nr, m * P:(m + 1) * P]
        slots += [t[:, 8 * s:8 * s + 8].reshape(P, PIECE) for s in range(10)]
        wd = f["w_down_2"][l].reshape(2, 2, 8, P, KT, P).transpose(0, 4, 1, 3, 2, 5).reshape(2, 16, P, PIECE)
        for half in range(2):
            slots += fm(f["w_up_2"][l], half * FF // 2, (half + 1) * FF // 2) + list(wd[half])
    stream = np.stack(slots)
    assert stream.shape == (N_PIECES, P, PIECE), stream.shape

    table = np.zeros((P, N_COLS), np.float32)

    def put(name, a, rows=P):
        c, n = COL[name]
        table[0:rows, c:c + n] = a.reshape(rows, n)

    def cols_of(g, k=KT):
        return g.reshape(k, P).transpose(1, 0)

    p = np.arange(P)
    t = np.arange(T)
    key = (p[:, None] + P * np.arange(2)[None, :])[:, :, None]
    put("ident", np.eye(P, dtype=np.float32))
    put("ones", np.ones((P, P), np.float32))
    put("nones", -np.ones((P, P), np.float32))
    put("ntri", -(p[:, None] >= p[None, :]).astype(np.float32))
    put("m_le", np.where(t <= key, 0.0, BIG))
    put("m_ge", np.concatenate([np.full((P, 2, 1), BIG), np.where(t >= key, 0.0, BIG)], 2))
    a64 = 2 * np.pi * ((np.arange(64)[:, None] * np.arange(64)[None, :]) % 64) / 64
    cd = np.kron(np.eye(2), np.cos(a64))
    sd = np.kron(np.eye(2), np.sin(a64))
    put("cdsd", np.concatenate([cd, sd], 1) / 128.0)
    a256 = 2 * np.pi * ((t[:, None] * t[None, :]) % T) / T
    put("cn", np.cos(a256).reshape(2, P, T).transpose(1, 0, 2))
    put("sn", (-np.sin(a256)).reshape(2, P, T).transpose(1, 0, 2))
    nf = RD // 4
    freqs = (np.float32(10000.0) ** (-np.arange(nf, dtype=np.float32) / np.float32(nf))).astype(np.float32)
    ang = np.zeros((RD, T), np.float32)
    rot = np.zeros((MD, MD), np.float32)
    for axis in range(2):
        pos = (t // 64 if axis == 0 else t % 64).astype(np.float32)
        for half in range(2):
            for i in range(nf):
                r = axis * 16 + half * 8 + i
                ang[r] = pos * freqs[i]
                other = axis * 16 + (1 - half) * 8 + i
                rot[64 + other, 64 + r] = -1.0 if half == 0 else 1.0
    cos, sin = np.ones((MD, T)), np.zeros((MD, T))
    cos[64:], sin[64:] = np.cos(ang.astype(np.float64)), np.sin(ang.astype(np.float64))
    put("cos", cos, MD)
    put("sin", sin, MD)
    put("rot", rot, MD)
    put("w4", np.tile(np.arange(4, 0, -1), (P, 1)))
    put("eps", np.full((P, 1), EPS))
    put("tiny", np.full((P, 1), 1e-37))
    for name, key_ in (("g_mix", "norm_mix"), ("g_xattn", "norm_xattn"), ("g_mem", "norm_mem"), ("g_ffn", "norm_ffn")):
        put(name, cols_of(f[key_][0]))
    put("g_fin1", cols_of(f["norm_final"]))
    put("g_fin2", cols_of(f["g_final_2"]))
    put("g_fox", cols_of(f["norm_fox_out"][0], 4))
    put("g_sb", cols_of(f["norm_sb_out"][0], 4))
    put("b_forget", f["b_forget"][0], 8)
    put("b_route", np.concatenate([f["b_router_group"][0], f["b_router_expert"][0]]), 1)
    put("w_f", f["w_in"][0][:, 3072:].reshape(KT, P, 8).transpose(1, 0, 2))
    wr = np.concatenate([f["w_router_group"][0], f["w_router_expert"][0]], 1)
    put("w_route", wr.reshape(KT, P, 20).transpose(1, 0, 2))
    put("c", np.stack([cols_of(f["c_2"][0]), cols_of(f["c_ctx_2"])], 2))
    small = np.zeros((NL, P, N_LCOLS), np.float32)
    bm = f["b_mod_2"].reshape(NL * 48, P).transpose(1, 0)
    put("b_mod", np.stack([bm, bm], 2))
    for l in range(NL):
        for k2 in (1, 2):
            g = cols_of(f[f"g_norm{k2}_2"][l])
            put(f"g{k2}_{l}", np.stack([g, g], 2))
        put(f"g_ml_{l}", f["g_mlstm_2"][l].reshape(MH, MD).transpose(1, 0), MD)
        put(f"g_qn_{l}", cols_of(f["g_q_norm_2"][l], 2))
        put(f"g_kvn_{l}", f["g_kv_norm_2"][l])
        put(f"conv_{l}", f["conv_qk_2"][l].reshape(5, 8, MD).transpose(2, 1, 0), MD)
        bg = np.zeros((P, 4), np.float32)
        bg[0:MH] = bg[32:32 + MH] = f["b_gates_2"][l].reshape(4, MH).transpose(1, 0)
        put(f"b_g_{l}", bg)
        kv = f["w_ukv_2"][l].reshape(P, MH, 160)
        small[l, :, 0:128] = f["w_in_2"][l][:, 1792:1808].reshape(KT, P, 16).transpose(1, 0, 2).reshape(P, 128)
        small[l, :, 128:896] = f["w_uq_2"][l].reshape(2, P, 384).transpose(1, 0, 2).reshape(P, 768)
        small[l, :, 896:1152] = kv[:, :, 0:64].reshape(P, 256)
        small[l, :, 1152:1536] = kv[:, :, 64:].reshape(P, 384)

    def act_fm(x):
        return np.ascontiguousarray(x.reshape(T, KT, P).transpose(2, 1, 0))

    return {"w_stream": stream, "table": table, "small": small, "x": act_fm(f["x"]), "mem": act_fm(f["mem"]), "ctx": act_fm(f["ctx_2"])}


def kernel(**inputs):
    import concourse.bacc as bacc
    from concourse.bass_utils import run_bass_kernel_spmd

    arrays = pack(inputs)
    nc = bacc.Bacc("TRN2", target_bir_lowering=False, num_devices=1)
    args = [nc.dram_tensor(f"in_{n}", a.shape, F32, kind="ExternalInput").ap() for n, a in arrays.items()]
    out = nc.dram_tensor("out_dram", (P, KT, T), F32, kind="ExternalOutput").ap()
    build(nc, *args, out)
    r = run_bass_kernel_spmd(nc, [{f"in_{n}": a for n, a in arrays.items()}], core_ids=[0])
    got = r.results[0]["out_dram"]
    return np.ascontiguousarray(got.transpose(2, 1, 0).reshape(1, T, D))
```

```python
from contextlib import ExitStack

import numpy as np

import concourse.bass as bass
from concourse import mybir

F32 = mybir.dt.float32
F32R = mybir.dt.float32r
ALU = mybir.AluOpType
ACT = mybir.ActivationFunctionType
AX_X = mybir.AxisListType.X

P = 128
D = 1024
KT = D // P
T = 256
TB = T // P
NF = 8
HD = 64
NX = 4
NE = 16
NL = 2
MH = 4
MD = 96
RD = 32
FF = 4096
MT = FF // P
EPS = 1e-6
BIG = -1e30
RING = 4
PIECE = 1024
AHEAD = 3
CTX, LAT, ALL = slice(0, T), slice(T, 2 * T), slice(0, 2 * T)

N_QK, N_V, N_XKV, N_SQ = 16, 8, 16, 8
N_MOE = 12 * NE
N_IN2, N_OUT2, N_UPDN = 8 + 4 + 4 + 2 + 1 + 2, 8, 64
LAYER_PIECES = 1 + N_IN2 + N_OUT2 + N_UPDN
S_QK = 0
S_F = S_QK + N_QK
S_V = S_F + 1
S_XKV = S_V + N_V
S_OUT = S_XKV + N_XKV
S_XQ = S_OUT + N_SQ
S_XO = S_XQ + N_SQ
S_RT = S_XO + N_SQ
S_MOE = S_RT + 1
S_L = S_MOE + N_MOE
N_PIECES = S_L + NL * LAYER_PIECES
MC = MT // 2

_COLS = [("ones", 128), ("g_mix", 8), ("g_mem", 8), ("eps", 1), ("tiny", 1), ("c", 16), ("b_forget", 1), ("ident", 128),
         ("nones", 128), ("ntri", 128), ("m_le", 512), ("m_ge", 514), ("cdsd", 256), ("cn", 512), ("sn", 512),
         ("cos", 256), ("sin", 256), ("rot", 96), ("w4", 8), ("g_xattn", 8), ("g_ffn", 8), ("g_fin1", 8), ("g_fox", 4),
         ("g_sb", 4), ("b_route", 1), ("b_mod", 192), ("g_fin2", 8)]
EARLY = 7
for _l in range(NL):
    _COLS += [(f"g1_{_l}", 16), (f"g2_{_l}", 16), (f"g_ml_{_l}", 4), (f"g_qn_{_l}", 2), (f"g_kvn_{_l}", 1),
              (f"conv_{_l}", 40), (f"b_g_{_l}", 1)]
COL = {}
_at = 0
for _name, _n in _COLS:
    COL[_name] = (_at, _n)
    _at += _n
N_COLS = _at
N_EARLY = COL[_COLS[EARLY][0]][0]
LCOL = {"uq": (0, 768), "ukv": (768, 640)}
N_LCOLS = 1408

NORM_LIST = [("mix", 4, 2), ("mem", 4, 2), ("fox", 2, 2), ("sb", 2, 2), ("xattn", 4, 2), ("ffn", 4, 2), ("fin1", 4, 2)]
for _l in range(NL):
    NORM_LIST += [(f"n1_{_l}", 8, 1), (f"cq_{_l}", 2, 1) if _l == 0 else (f"cq_{_l}", 1, 2), (f"ckv_{_l}", 1, 1)]
    NORM_LIST += [(f"head_{_l}_{_h}", 1, 1) for _h in range(MH)] + [(f"n2_{_l}", 8, 1)]
NORM_LIST += [("fin2", 8, 1)]
LOOPED = ("n1_1", "fin2")
NORM, SQ_AT, ADD_AT, STEPS, HALVES = {}, {}, {}, {}, {}
_sq = _add = 0
for _i, (_name, _steps, _halves) in enumerate(NORM_LIST):
    NORM[_name], STEPS[_name], HALVES[_name] = _i, _steps, _halves
    SQ_AT[_name], ADD_AT[_name] = _sq, _add
    _sq += _steps
    _add += _steps if _name in LOOPED else _steps - 1

U_STEPS = [("mix", 8), ("mem", 8), ("fox", 4), ("sb", 4), ("xattn", 8), ("xo", 4), ("ffn", 8)]
for _l in range(NL):
    U_STEPS += [(f"n1_{_l}", 8), (f"y_{_l}", 10), (f"n2_{_l}", 8)]
U_AT = {}
_at = 0
for _name, _n in U_STEPS:
    U_AT[_name] = _at
    _at += _n

_HEAD_STEPS = (6, 7, 8, 9)
V_AT, V_N = {}, {}
_at = 0
for _name, _n in U_STEPS:
    V_AT[_name] = _at
    V_N[_name] = 0 if _name == "xo" else len(_HEAD_STEPS) if _name.startswith("y_") else _n
    _at += V_N[_name]
OUT_NORMS = [_name for _name, _, _ in NORM_LIST if _name not in V_N and _name != "fin1"]


def value_count(name, step):
    return V_AT[name] + (_HEAD_STEPS.index(step) if name.startswith("y_") else step) + 1


def normed(name):
    if name in V_N:
        return "u_v", V_AT[name] + V_N[name]
    if name == "fin1":
        return "fin1_tile", KT
    return "norm_out", OUT_NORMS.index(name) + 1


TURN = []
for _e in range(2):
    for _what in ("gate0", "mod", "gate1", "mod", "up0", "mod", "up1", "mod", "mod", "down0", "mod", "down1"):
        if _what == "mod":
            _n = [w for w, _, _ in TURN].count("mod")
            TURN.append(("mod", _n // 4, _n % 4))
        else:
            TURN.append((_what[:-1], _e, int(_what[-1])))
N_TURN = len(TURN)
MOD_STEPS = (8, 19, 23)

UNITS = [("fox", h, None) for h in range(NF)] + [("xat", h, None) for h in range(NX)]
for _l in range(NL):
    if _l == 0:
        UNITS += [(f"mctx{_l}", h, None) for h in range(MH)]
    UNITS += [(f"mlat{_l}", h, q) for h in range(MH) for q in range(TB)]
UNIT0 = {}
for _i, _u in enumerate(UNITS):
    UNIT0.setdefault(_u[0], _i)


class Jobs:

    def __init__(self):
        self.first, self.engines, self.counted = {}, [], []

    def add(self, phase, count, engine, counted=True):
        self.first[phase] = len(self.engines)
        self.engines += [engine] * count
        self.counted += [counted] * count

    def number(self, phase, j=0):
        return self.first[phase] + j

    def full(self, n):
        return self.counted[: n + 1].count(True)

    def emptied(self, n):
        engine = self.engines[n]
        if engine.startswith("mlstm"):
            return "ml_sum", MH * (int(engine[-1]) + 1)
        return f"job_emptied_{engine}", self.engines[: n + 1].count(engine)


JOBS = Jobs()
for _phase, _count, _engine in [("qk", 8, "act"), ("v", 4, "act"), ("xkv", 8, "act"), ("out1", 4, "dve"),
                                ("xq", 4, "act"), ("xo", 4, "dve")]:
    JOBS.add(_phase, _count, _engine)
JOBS.add("moe_y", 4, "dve", False)
for _l in range(NL):
    _w = 2 if _l == 0 else 1
    for _phase, _count, _engine in [("mqk", 8, "act"), ("mv", 4, "act"), ("mo", 4, "act"), ("cq", 2, "act"),
                                    ("ckv", 1, "act"), ("pf", 2, "act"), ("uq", 4, "act"), ("rot", 5, "dve"),
                                    ("kn", 4, "act"), ("va", 4, "act"),
                                    ("fa0", 2, "act"), ("fy0", 2, "act"), ("fa1", 2 * (_w - 1), "act"), ("fy1", 2 * (_w - 1), "act"),
                                    ("mlstm", 4, f"mlstm{_l}"),
                                    ("out", 8, "dve"), ("upa", MC, "act"), ("dna", 8, "dve"), ("upb", MC, "act"), ("dnb", 8, "dve")]:
        JOBS.add(f"{_phase}_{_l}", _count, _engine, _phase != "mlstm")


def build(nc, w_stream, table_in, small_in, x_in, mem_in, ctx_in, out):
    with ExitStack() as stack:
        sems = {}

        def S(name):
            if name not in sems:
                sems[name] = stack.enter_context(nc.semaphore(name))
            return sems[name]

        base = (nc.sbuf_base + 31) // 32 * 32
        top = [0]

        def at(name, shape, off, dtype=F32):
            n = int(np.prod(shape[1:]))
            return nc.alloc_sbuf_tensor_at(name, list(shape), dtype, offset=base + 4 * off)

        def take(n):
            top[0] += n
            return top[0] - n

        table = at("table", [P, N_COLS], take((N_COLS + 7) // 8 * 8))
        lw = at("lw", [P, N_LCOLS], take(N_LCOLS))
        res = at("res", [P, KT, 2 * T], take(KT * 2 * T))
        uh = at("uh", [P, KT, 2 * T], take(KT * 2 * T), F32R)
        ul_at = take(KT * 2 * T)
        ul = at("ul", [P, KT, 2 * T], ul_at, F32R)
        uv = at("uv", [P, KT, 2 * T], ul_at)
        sq_at = take(5 * 512)
        sq = at("sq", [P, 5, 512], sq_at)
        rows_at = take(5 * 512)
        rows_buf = at("rows_buf", [32 + MH, 5, 512], rows_at)
        crow = at("crow", [NF, 5, T], rows_at)
        logit_rows = at("logit_rows", [32, T], rows_at)
        turned = at("turned", [32, 16, 32], rows_at)
        rstd = at("rstd", [P, 2 * T], take(2 * T))
        small = at("small", [P, 256], take(256))
        modv = at("modv", [P, 192], take(192))
        gmod = at("gmod", [P, 2 * NL, 16], take(64))
        cparts = at("cparts", [P, 100], take(104), F32R)
        gcol = at("gcol", [P, 2, 4, MH], take(32))
        ring = at("ring", [P, RING, PIECE], take(RING * PIECE))
        wh = at("wh", [P, RING, PIECE], take(RING * PIECE), F32R)
        wl = at("wl", [P, RING, PIECE], take(RING * PIECE), F32R)
        w0 = take(16464)
        assert base + 4 * top[0] <= nc.sbuf_top, (base + 4 * top[0], nc.sbuf_top)
        qk = at("qk", [P, 16, T], w0)
        v1 = at("v1", [P, TB, D], w0 + 4096)
        heads = at("heads", [P, KT, T], w0 + 6144)
        kx = at("kx", [P, KT, T], w0 + 8192)
        vx = at("vx", [P, TB, D], w0 + 10240)
        sbt = [at(f"sbt{i}", [P, 4, 512], w0 + 12288 + i * 2048) for i in range(2)]
        qx = at("qx", [P, KT, T], w0)
        gates = at("gates", [P, NE, T], w0)
        eg = at("eg", [P, 512], w0 + 4096)
        hidh = at("hidh", [P, 2, T], w0 + 4608, F32R)
        hidl = at("hidl", [P, 2, T], w0 + 5120, F32R)
        qkp = at("qkp", [MD, 8, TB, 260], w0)
        qa = at("qa", [MD, MH, 512], w0)
        ka = at("ka", [MD, MH, 512], w0 + 2048)
        ml = at("ml", [P, 8, 512], w0)
        qc = at("qc", [MD, 8, 512], w0 + 4160)
        mv = at("mv", [P, 4, MH, MD + 1], w0 + 8256)
        mo = at("mo", [MD, MH, 512], w0 + 9808)
        va = at("va", [P, 4, 384], w0 + 11856)
        yfh = at("yfh", [P, 2, 512], w0 + 11856, F32R)
        pf = at("pf", [P, 2, 512], w0 + 13392)
        yf = pf
        yfl = at("yfl", [P, 2, 512], w0 + 13392, F32R)
        cq = at("cq", [P, 2, 512], w0 + 14416)
        ckv = at("ckv", [P, 512], w0 + 15440)
        kr = at("kr", [MD, 512], w0 + 15952)
        ya = at("ya", [MD, MH, 512], w0 + 14416)
        hh = at("hh", [P, MC, 512], w0, F32R)
        hl = at("hl", [P, MC, 512], w0 + 8192, F32R)
        rt = small[:, 96:224].rearrange("p (b c) -> p b c", b=TB)
        prob = [sq[:, i, :] for i in range(2)]
        probT = [sq[:, 2 + i, :] for i in range(2)]
        fa = sq[:, 0:2, :].rearrange("p a (b c) -> p a b c", b=TB)
        rows = [rows_buf[32 * d:32 * d + MH] for d in range(2)]
        bank = [stack.enter_context(nc.psum_tensor(f"bank{i}", [P, 512], F32)) for i in range(8)]

        def tab(name, rows=P):
            a, n = COL[name]
            return table[0:rows, a:a + n]

        def ltab(name):
            a, n = LCOL[name]
            return lw[:, a:a + n]

        ident, ones = tab("ident"), tab("ones")
        row_ident = [ident[32 * d:32 * d + MH, 32 * d:32 * d + MH] for d in range(2)]
        m_ge = tab("m_ge").rearrange("p (k t) -> p k t", k=2)

        class Chain:

            def __init__(self, eng, name):
                self.eng, self.sem, self.n, self.more = eng, S(name), 0, None

            def link(self, ins):
                ins.then_inc(self.sem, 1)
                self.n += 1
                self.eng.wait_ge(self.sem, self.n if self.more is None else self.more + self.n)

            def loop(self, i, per):
                self.start, self.per, self.more = self.n, per, i * per

            def end(self, turns):
                assert self.n - self.start == self.per, (self.n - self.start, self.per)
                self.n, self.more = self.start + self.per * turns, None

        def full(eng, phase, j=0):
            n = JOBS.number(phase, j)
            eng.wait_ge(S("job_full"), JOBS.full(n))
            return bank[n % 4]

        def emptied(ins, engine):
            ins.then_inc(S(f"job_emptied_{engine}"), 1)

        def wait_emptied(eng, phase, j):
            sem, count = JOBS.emptied(JOBS.number(phase, j))
            eng.wait_ge(S(sem), count)

        def lin_cols(l):
            return ALL if l == 0 else LAT

        def mlb(l, i):
            return JOBS.number(f"mlstm_{l}", i) % 4

        def ml_args(l, h, kb, d):
            if l == 0:
                return 2 * (4 * h + kb) + d + 1
            return 2 * 4 * MH + 2 * (2 * h + kb - 2) + d + 1

        rb, arg = [ml[:, d, :] for d in range(2)], [ml[:, 4 + d, :] for d in range(2)]
        den, quot = [ml[MD:MD + 1, 2 + d, :] for d in range(2)], [ml[0:MD, 6 + d, :] for d in range(2)]

        block = stack.enter_context(nc.Block())

        @block.sync
        def _(sp):
            for t in range(4):
                sp.dma_start(res[:, 2 * t:2 * t + 2, LAT], x_in[:, 2 * t:2 * t + 2, :]).then_inc(S(f"x_in{t}"), 16)
            sp.dma_start(table[:, 0:N_EARLY], table_in[:, 0:N_EARLY]).then_inc(S("early_in"), 16)
            for s in range(RING):
                sp.dma_start(ring[:, s, :], w_stream[s]).then_inc(S(f"piece_in{s}"), 16)
            sp.dma_start(table[:, N_EARLY:], table_in[:, N_EARLY:]).then_inc(S("table_in"), 16)
            sp.dma_start(res[:, :, CTX], mem_in).then_inc(S("mem_in"), 16)
            sp.dma_start(lw[:, :], small_in[0]).then_inc(S("lw_in0"), 16)
            with sp.Fori(1, N_PIECES // RING) as i:
                for s in range(RING):
                    sp.wait_ge(S("w_lo"), i * RING + (s + 1 - RING))
                    sp.dma_start(ring[:, s, :], w_stream[i * RING + s]).then_inc(S(f"piece_in{s}"), 16)
            for s in range(N_PIECES % RING):
                n = N_PIECES // RING * RING + s
                sp.wait_ge(S("w_lo"), n + 1 - RING)
                sp.dma_start(ring[:, s, :], w_stream[n]).then_inc(S(f"piece_in{s}"), 16)
            sp.wait_ge(S("norm_out"), normed("fin2")[1])
            sp.dma_start(out, res[:, :, LAT]).then_inc(S("stored"), 16)
            sp.wait_ge(S("stored"), 16)

        @block.gpsimd
        def _(pool):
            pool.wait_ge(S("u_v"), normed("mem")[1])
            pool.dma_start(res[:, :, CTX], ctx_in).then_inc(S("ctx_in"), 16)
            for l in range(1, NL):
                pool.wait_ge(S("job_full"), JOBS.full(JOBS.number(f"va_{l - 1}", 3)))
                pool.dma_start(lw[:, :], small_in[l]).then_inc(S(f"lw_in{l}"), 16)
            for l in range(NL):
                cols = lin_cols(l)
                for j in range(2):
                    pool.wait_ge(S("u_l"), U_AT[f"y_{l}"] + MH + j + 1)
                    for q in range(4):
                        for dst, src in ((uh, yfh), (ul, yfl)):
                            pool.tensor_copy(dst[MD:P, 4 * j + q, cols],
                                             src[32 * q:32 * q + 32, j, cols]).then_inc(S("y_moved"), 1)

        @block.scalar
        def _(act):
            ch = Chain(act, "act_step")
            hi_at = [0]

            def hi_part(s, landed, used):
                act.wait_ge(S(f"piece_in{s}"), landed)
                if used is not None:
                    act.wait_ge(S("piece_used"), used)
                act.activation(wh[:, s, :], ring[:, s, :], ACT.Copy).then_inc(S("w_hi"), 1)

            def split(to):
                while hi_at[0] <= min(to, N_PIECES - 1):
                    n = hi_at[0]
                    hi_part(n % RING, 16 * (n // RING + 1), n - 3 if n >= RING else None)
                    hi_at[0] += 1

            def split_turn(i, per, base, lo, hi):
                for j in range(lo, hi + 1):
                    n = base + j
                    hi_part(n % RING, i * (4 * per) + 16 * (n // RING + 1), i * per + (n - 3))

            def square(name, t, src, p, n, after=True):
                if name.startswith("head"):
                    dst = sq[0:p, 4, 0:n]
                elif t == 0 and name not in LOOPED:
                    dst = sq[0:p, 3, 0:n]
                else:
                    dst = sq[0:p, t % 2, 0:n]
                    if t >= 3:
                        act.wait_ge(S("norm_add"), ADD_AT[name] + t - 2)
                if len(src.shape) == 3:
                    dst = dst.rearrange("p (a t) -> p a t", a=src.shape[1])
                act.activation(dst, src, ACT.Square).then_inc(S("norm_sq"), 1)

            def root(name, p, n, width):
                i = NORM[name]
                act.wait_ge(S("norm_ms"), i + 1)
                if i:
                    sem, count = normed(NORM_LIST[i - 1][0])
                    act.wait_ge(S(sem), count)
                ch.link(act.activation(rstd[0:p, 0:n], bank[7][0:p, 0:n], ACT.Ln, bias=tab("eps")[0:p],
                                       scale=1.0 / width))
                act.activation(rstd[0:p, 0:n], rstd[0:p, 0:n], ACT.Exp, scale=-0.5).then_inc(S("norm_rstd"), 1)

            def round_u(name, i, parts, ready=None):
                sem, count = ready or ("u_v", value_count(name, i))
                act.wait_ge(S(sem), count)
                for hi, v, bias in parts:
                    if bias is None:
                        last = act.activation(hi, v, ACT.Copy)
                    else:
                        last = act.activation(hi, v, ACT.Identity, bias=bias)
                last.then_inc(S("u_h"), 1)

            def round_tiles(name, cols, steps=8):
                for k in range(steps):
                    j = k + (4 if name == "sb" else 0)
                    round_u(name, k, [(uh[:, j, cols], uv[:, j, cols], None)])

            def smv(i, what, k):
                a = (i % 2) * 8 + what * 2 + k
                return small[:, a:a + 1]

            def softmax(i):
                g, w = (1, 512) if UNITS[i][2] is not None else (2, 256)
                act.wait_ge(S("sm_max"), i + 1)
                if i >= 2:
                    act.wait_ge(S("sm_tr"), i - 1)
                for k in range(g):
                    last = act.activation(prob[i % 2][:, k * w:(k + 1) * w], bank[4 + i % 2][:, k * w:(k + 1) * w],
                                          ACT.Exp, bias=smv(i, 0, k), accum_out=smv(i, 2, k))
                last.then_inc(S("sm_exp"), 1)

            def transposed(i):
                act.wait_ge(S("sm_tr"), i + 1)
                if i >= 2:
                    act.wait_ge(S("sm_o"), i - 1)
                act.activation(probT[i % 2], bank[6][:, :], ACT.Copy).then_inc(S("sm_pt"), 1)

            def log1p_rows(src, dst, sem_in, count, sem_out):
                act.wait_ge(S(sem_in), count)
                ch.link(act.activation(dst, src, ACT.Abs))
                ch.link(act.activation(dst, dst, ACT.Exp, scale=-1.0))
                act.activation(dst, dst, ACT.Ln, bias=1.0).then_inc(S(sem_out), 1)

            act.preload_act_table_set("natural_log_exp_and_others")
            for t in range(4):
                act.wait_ge(S(f"x_in{t}"), 16)
                square("mix", t, res[:, 2 * t:2 * t + 2, LAT], P, 512)
            act.wait_ge(S("early_in"), 16)
            root("mix", P, T, D)
            split(2)
            round_tiles("mix", LAT)
            act.activation(small[:, 64:80], tab("c"), ACT.Exp, scale=-1.0).then_inc(S("c_exp"), 1)
            for s in range(8):
                split(S_QK + 2 * s + 1 + AHEAD)
                b = full(act, "qk", s)
                scale = HD ** -0.5 if s in (0, 1, 4, 5) else 1.0
                emptied(act.activation(qk[:, 2 * s:2 * s + 2, :], b[:, :].rearrange("p (a t) -> p a t", a=2), ACT.Copy,
                                       scale=scale), "act")
                if s == 0:
                    act.wait_ge(S("mem_in"), 16)
                    for t in range(4):
                        square("mem", t, res[:, 2 * t:2 * t + 2, CTX], P, 512)
                if s == 4:
                    root("mem", P, T, D)
                    round_tiles("mem", CTX)
            for s in range(4):
                split(S_V + 2 * s + 1 + AHEAD)
                if s == 1:
                    log1p_rows(crow[:, 0, :], crow[:, 1, :], "fox_f", 1, "fox_ln")
                b = full(act, "v", s)
                emptied(act.activation(v1[:, :, s * T:(s + 1) * T], b[:, :].rearrange("p (a t) -> p a t", a=2),
                                       ACT.Copy), "act")

            for i in range(NF + 1):
                if i < NF:
                    softmax(i)
                    split(S_XKV + 2 * i + 1 + AHEAD)
                    b = full(act, "xkv", i)
                    dst = kx[:, 2 * i:2 * i + 2, :] if i < 4 else vx[:, :, (i - 4) * T:(i - 3) * T]
                    emptied(act.activation(dst, b[:, :].rearrange("p (a t) -> p a t", a=2), ACT.Copy), "act")
                if i >= 1:
                    transposed(i - 1)

            for h in range(NF + 1):
                if h < NF:
                    t = sbt[h % 2]
                    act.wait_ge(S("sb_z"), h + 1)
                    if h >= 2:
                        act.wait_ge(S("sb_softplus"), h - 1)
                    ch.link(act.activation(t[:, 0, :], bank[4 + h % 2][:, :], ACT.Abs))
                    ch.link(act.activation(t[:, 0, :], t[:, 0, :], ACT.Exp, scale=-1.0))
                    act.activation(t[:, 0, :], t[:, 0, :], ACT.Ln, bias=1.0).then_inc(S("sb_ln"), 1)
                if h >= 1:
                    g = h - 1
                    act.wait_ge(S("sb_arg"), g + 1)
                    act.activation(sbt[g % 2][:, 3, :], sbt[g % 2][:, 2, :], ACT.Exp).then_inc(S("sb_w"), 1)
                if h == 2:
                    for t in range(2):
                        square("fox", t, heads[:, 2 * t:2 * t + 2, :], P, 512)
                    root("fox", P, T, 512)
            for t in range(2):
                act.wait_ge(S("sb_out"), 4 * t + 4)
                square("sb", t, heads[:, 4 + 2 * t:6 + 2 * t, :], P, 512)
            root("sb", P, T, 512)
            round_tiles("fox", LAT, 4)
            round_tiles("sb", LAT, 4)

            def added_squares(name, phase, first):
                for t in range(4):
                    split(first + 2 * t + 1 + AHEAD - (t == 3))
                    wait_emptied(act, phase, t)
                    square(name, t, res[:, 2 * t:2 * t + 2, LAT], P, 512)
                split(first + 7 + AHEAD)
                root(name, P, T, D)

            added_squares("xattn", "out1", S_OUT)
            round_tiles("xattn", LAT)
            for s in range(4):
                split(S_XQ + 2 * s + 1 + AHEAD)
                b = full(act, "xq", s)
                emptied(act.activation(qx[:, 2 * s:2 * s + 2, :], b[:, :].rearrange("p (a t) -> p a t", a=2), ACT.Copy,
                                       scale=256 ** -0.5), "act")
            for i in range(NX + 2):
                if i < NX:
                    softmax(UNIT0["xat"] + i)
                if 1 <= i <= NX:
                    transposed(UNIT0["xat"] + i - 1)
                if i >= 2:
                    j = 2 * (i - 2)
                    round_u("xo", i - 2, [(uh[:, j:j + 2, LAT], uv[:, j:j + 2, LAT], None)],
                            ("sm_out", UNIT0["xat"] + i - 1))
            added_squares("ffn", "xo", S_XO)
            round_tiles("ffn", LAT)

            split(S_RT + AHEAD)
            act.wait_ge(S("rt_logits"), 1)
            act.activation(logit_rows[0:20, :], bank[6][0:20, 0:T], ACT.Identity,
                           bias=tab("b_route", 20)).then_inc(S("rt_rows"), 1)
            act.wait_ge(S("rt_max"), 1)
            for b in range(TB):
                act.activation(rt[:, b, 24:28], rt[:, b, 0:4], ACT.Exp, bias=rt[:, b, 20:21],
                               accum_out=rt[:, b, 21:22])
            act.wait_ge(S("rt_diff"), 1)
            act.activation(rt[:, :, 22:23], rt[:, :, 23:24], ACT.Exp).then_inc(S("rt_exp"), 1)
            for e in range(NE // 2):
                act.wait_ge(S("gate_full"), e + 1)
                act.activation(gates[:, 2 * e:2 * e + 2, :], bank[4 + e % 2][:, :].rearrange("p (a t) -> p a t", a=2),
                               ACT.Copy).then_inc(S("gate_in"), 1)
            split(S_MOE + 2)
            with act.Fori(0, NE // 2) as i:
                for step, (what, e, m) in enumerate(TURN):
                    split_turn(i, N_TURN, S_MOE, step + AHEAD, step + AHEAD)
                    if (what, m) == ("gate", 1):
                        act.wait_ge(S("moe_gate"), i * 2 + (e + 1))
                        act.wait_ge(S("moe_lo"), i * 2 + (e + 1))
                        act.activation(eg[:, :], bank[4][:, :], ACT.Silu).then_inc(S("moe_silu"), 1)
                    elif (what, m) == ("up", 1):
                        act.wait_ge(S("moe_v"), i * 2 + (e + 1))
                        act.activation(hidh[:, :, :].rearrange("p a t -> p (a t)"), eg[:, :],
                                       ACT.Copy).then_inc(S("moe_hi"), 1)
            act.preload_act_table_set("natural_log_exp_and_others")
            hi_at[0] = S_L + AHEAD
            for t in range(4):
                wait_emptied(act, "moe_y", t)
                square("fin1", t, res[:, 2 * t:2 * t + 2, LAT], P, 512)
            root("fin1", P, T, D)

            def round_mod(l, k2):
                first = l * 48 + (0 if k2 == 0 else 24)
                name = f"n{k2 + 1}_{l}"
                for k in range(KT):
                    parts = []
                    for which, cols in ((0, LAT), (1, CTX)):
                        if k2 == 1 and l == NL - 1 and which == 1:
                            continue
                        c = 2 * (first + k) + which
                        parts.append((uh[:, k, cols], uv[:, k, cols], modv[:, c:c + 1]))
                    round_u(name, k, parts)

            for l in range(NL):
                cols = lin_cols(l)
                n = cols.stop - cols.start
                p0 = S_L + l * LAYER_PIECES + 1
                if l == 0:
                    act.wait_ge(S("ctx_in"), 16)
                    for k in range(KT):
                        act.wait_ge(S("fin1_tile"), k + 1)
                        square("n1_0", k, res[:, k, :], P, 512)
                root(f"n1_{l}", P, 2 * T, D)
                round_mod(l, 0)
                for j in range(8):
                    split(p0 + j + AHEAD)
                    if j in (1, 2):
                        log1p_rows(rows[j - 1][:, 1, :], rows[j - 1][:, 2, :], "ml_f", 2 * l + j, "ml_ln")
                    b = full(act, f"mqk_{l}", j)
                    if j == 7:
                        act.activation(kr[64:64 + RD, :], b[MD:MD + RD, :], ACT.Copy)
                    if j < 4 and l:
                        last = act.activation(qkp[:, j, 1, 2:258], b[0:MD, 0:T], ACT.Copy)
                    else:
                        last = act.activation(qkp[:, j, :, 2:258],
                                              b[0:MD, :].rearrange("p (s t) -> p s t", s=2), ACT.Copy)
                    emptied(last, "act")
                split(p0 + 11 + AHEAD)
                for j in range(4):
                    b = full(act, f"mv_{l}", j)
                    emptied(act.activation(mv[:, j, :, 0:MD], b[:, 0:384].rearrange("p (h d) -> p h d", h=MH), ACT.Copy),
                            "act")
                for j in range(4):
                    split(p0 + 12 + j + AHEAD)
                    b = full(act, f"mo_{l}", j)
                    emptied(act.activation(mo[:, j, cols], b[0:MD, 0:n], ACT.Sigmoid), "act")
                for j in range(8):
                    cc = cols if j < 4 else ALL
                    act.wait_ge(S("conv_sum"), 8 * l + j + 1)
                    act.activation(qc[:, j, cc], qc[:, j, cc], ACT.Silu).then_inc(S("conv_done"), 1)
                act.preload_act_table_set("natural_log_exp_and_others")
                for j in range(2):
                    split(p0 + 16 + j + AHEAD)
                    b = full(act, f"cq_{l}", j)
                    emptied(act.activation(cq[:, j, cols], b[:, 0:n], ACT.Copy), "act")
                split(p0 + 18 + AHEAD)
                b = full(act, f"ckv_{l}", 0)
                emptied(act.activation(ckv[:, :], b[:, :], ACT.Copy), "act")
                wait_emptied(act, f"ckv_{l}", 0)
                if l == 0:
                    for j in range(2):
                        square("cq_0", j, cq[:, j, :], P, 512)
                else:
                    square("cq_1", 0, cq[:, :, LAT], P, 512)
                for j in range(2):
                    split(p0 + 19 + j + AHEAD)
                    b = full(act, f"pf_{l}", j)
                    emptied(act.activation(pf[:, j, cols], b[:, 0:n], ACT.Copy), "act")
                for d in range(2):
                    act.wait_ge(S("gcol_full"), 2 * l + d + 1)
                    act.activation(gcol[:, d, :, :], bank[4 + d][:, 0:16].rearrange("p (a b) -> p a b", a=4),
                                   ACT.Copy).then_inc(S("gcol_in"), 1)
                root(f"cq_{l}", P, n, 256)
                square(f"ckv_{l}", 0, ckv[:, :], P, 512)
                root(f"ckv_{l}", P, 512, 128)
                for h in range(MH):
                    b = full(act, f"uq_{l}", h)
                    emptied(act.activation(qa[:, h, cols], b[0:MD, 0:n], ACT.Copy, scale=MD ** -0.5), "act")
                for h in range(MH):
                    b = full(act, f"kn_{l}", h)
                    emptied(act.activation(ka[0:64, h, :], b[0:64, :], ACT.Copy), "act")
                for j in range(4):
                    b = full(act, f"va_{l}", j)
                    emptied(act.activation(va[:, j, :], b[:, 0:384], ACT.Copy), "act")
                for s in range(n // T):
                    sc = slice(cols.start + s * T, cols.start + (s + 1) * T)
                    for ft in range(2):
                        b = full(act, f"fa{s}_{l}", ft)
                        emptied(act.activation(fa[:, ft, :, :], b[:, :].rearrange("p (a t) -> p a t", a=2),
                                               ACT.Copy), "act")
                    for ft in range(2):
                        b = full(act, f"fy{s}_{l}", ft)
                        emptied(act.activation(yf[:, ft, sc], b[:, 0:T], ACT.Copy), "act")
                units = range(UNIT0["mctx0"], UNIT0["mlat1"]) if l == 0 else range(UNIT0["mlat1"], len(UNITS))
                for i in range(units.start, units.stop + 1):
                    if i < units.stop:
                        softmax(i)
                    if i > units.start:
                        transposed(i - 1)
                for h in range(MH):
                    round_u(f"y_{l}", h, [(uh[0:MD, h, cols], ya[:, h, cols], None)],
                            ("sm_out", UNIT0[f"mlat{l}"] + TB * (h + 1)))
                for j in range(2):
                    round_u(f"y_{l}", MH + j, [(yfh[:, j, cols], yf[:, j, cols], None)],
                            JOBS.emptied(JOBS.number(f"fy1_{l}" if l == 0 else f"fy0_{l}", j)))

                def head_round(h):
                    round_u(f"y_{l}", MH + 2 + h, [(uh[0:MD, MH + h, cols], mo[:, h, cols], None)])

                def head_ln(h):
                    act.wait_ge(S("ml_v"), 4 * (l * MH + h + 1))
                    for d in range(2):
                        b = bank[mlb(l, 2 * (h % 2) + d)]
                        last = act.activation(den[d][:, cols], b[MD:MD + 1, cols], ACT.Abs)
                    ch.link(last)
                    for d in range(2):
                        act.activation(den[d][:, cols], den[d][:, cols], ACT.Ln,
                                       bias=table[MD:MD + 1, COL["tiny"][0]:COL["tiny"][0] + 1]).then_inc(S("ml_ln2"), 1)

                def head_exp(h):
                    for d in range(2):
                        act.wait_ge(S("ml_min"), 2 * (l * MH + h) + d + 1)
                        act.activation(den[d][:, cols], den[d][:, cols], ACT.Exp).then_inc(S("ml_rden"), 1)

                def head_square(h):
                    act.wait_ge(S("ml_sum"), l * MH + h + 1)
                    square(f"head_{l}_{h}", 0, quot[0][:, cols], MD, n)

                def exps(h, kb):
                    for d in range(2):
                        if kb >= 2 or l == 0:
                            act.wait_ge(S("ml_arg"), ml_args(l, h, kb, d))
                        if 4 * (l * MH + h) + kb >= 2:
                            act.wait_ge(S("ml_v"), 4 * (l * MH + h) + kb - 1)
                        bias = gcol[:, d, kb, h:h + 1]
                        e = sq[:, 2 * (kb % 2) + d, :]
                        if kb < 2:
                            if l == 0:
                                act.activation(e[:, CTX], arg[d][:, CTX], ACT.Exp, bias=bias)
                            last = act.activation(e[:, LAT], rb[d][:, LAT], ACT.Exp, bias=bias)
                        else:
                            last = act.activation(e[:, LAT], arg[d][:, LAT], ACT.Exp, bias=bias)
                        last.then_inc(S("ml_e"), 1)

                for h in range(MH):
                    for d in range(2):
                        c = 2 * (l * MH + h) + d + 1
                        act.wait_ge(S("ml_b"), c)
                        act.activation(rb[d][:, cols], bank[6][:, cols], ACT.Copy).then_inc(S("ml_b_in"), 1)
                    act.wait_ge(S("ml_b_in"), c)
                    exps(h, 0)
                    if h:
                        head_ln(h - 1)
                    if h >= 2:
                        head_round(h - 2)
                    exps(h, 1)
                    if h:
                        head_exp(h - 1)
                    exps(h, 2)
                    if h:
                        head_square(h - 1)
                    exps(h, 3)
                    if h:
                        root(f"head_{l}_{h - 1}", MD, n, MD)
                head_ln(MH - 1)
                head_round(MH - 2)
                head_exp(MH - 1)
                head_square(MH - 1)
                root(f"head_{l}_{MH - 1}", MD, n, MD)
                head_round(MH - 1)
                lag = l
                for m in range(KT + lag):
                    if m < KT:
                        split(p0 + N_IN2 + min(m, KT - 2) + AHEAD)
                    if m >= lag:
                        wait_emptied(act, f"out_{l}", m - lag)
                        square(f"n2_{l}", m - lag, res[:, m - lag, cols], P, n)
                split(p0 + N_IN2 + KT - 1 + AHEAD)
                root(f"n2_{l}", P, n, D)
                round_mod(l, 1)
                for half, name in enumerate("ab"):
                    pu = p0 + N_IN2 + N_OUT2 + half * 32
                    b0, f0 = JOBS.number(f"up{name}_{l}"), JOBS.full(JOBS.number(f"up{name}_{l}"))
                    h0 = (2 * l + half) * MC
                    split(pu + AHEAD - 1)
                    with act.Fori(0, MC // 4) as i:
                        for j in range(4):
                            split_turn(i, 4, pu, j + AHEAD, j + AHEAD)
                            act.wait_ge(S("job_full"), i * 4 + (f0 + j))
                            r = sq[:, j % 2, 0:n]
                            v = sq[:, 2 + j % 2, 0:n]
                            act.wait_ge(S("hid_lo"), i * 4 + (h0 + j + 1))
                            act.activation(r, bank[(b0 + j) % 4][:, 0:n], ACT.Relu).then_inc(
                                S("job_emptied_act"), 1)
                            act.wait_ge(S("job_emptied_act"),
                                        i * 4 + (JOBS.emptied(b0)[1] + j))
                            act.activation(v, r, ACT.Square)
                            act.activation(hh[:, bass.ds(i * 4 + j, 1), 0:n].rearrange("p a b -> p (a b)"), r,
                                           ACT.Square).then_inc(S("hid_hi"), 1)
                    hi_at[0] = pu + MC + AHEAD
                    pd = pu + MC
                    if half == 0:
                        with act.Fori(0, 4) as i:
                            split_turn(i, 4, pd, AHEAD, AHEAD + 3)
                    else:
                        nxt = "n1_1" if l == 0 else "fin2"
                        turns = 4 if l < NL - 1 else 3
                        b1 = JOBS.emptied(JOBS.number(f"dnb_{l}"))[1]

                        def down_squares(i, fixed=None):
                            for j in range(2):
                                act.wait_ge(S("job_emptied_dve"), i * 2 + (b1 + j))
                                act.wait_ge(S("norm_add"), i * 2 + ADD_AT[nxt] + j - 1)
                                c = ALL if l == 0 else LAT
                                src = res[:, bass.ds(i * 2 + j, 1), c] if fixed is None else res[:, 2 * fixed + j, c]
                                if fixed is None:
                                    src = src.rearrange("p a b -> p (a b)")
                                act.activation(sq[:, j, 0:n], src, ACT.Square).then_inc(S("norm_sq"), 1)

                        with act.Fori(0, turns) as i:
                            split_turn(i, 4, pd, AHEAD, AHEAD + 3)
                            down_squares(i)
                        if turns == 3:
                            hi_at[0] = pd + 12 + AHEAD
                            split(pd + 15)
                            down_squares(3, 3)
                    hi_at[0] = pd + MC + AHEAD
            root("fin2", P, T, D)

        @block.tensor
        def _(pe):
            begun = []

            def mm(*operands, **flags):
                ins = pe.matmul(*operands, **flags)
                if begun:
                    begun.clear()
                    ins.then_inc(S("piece_used"), 1)
                return ins

            def claim(phase, j=0):
                n = JOBS.number(phase, j)
                if n >= 4:
                    sem, count = JOBS.emptied(n - 4)
                    pe.wait_ge(S(sem), count)
                return bank[n % 4]

            def parts(n):
                pe.wait_ge(S("w_lo"), n + 1)
                if n:
                    begun.append(n)

            def parts_turn(i, per, n):
                pe.wait_ge(S("w_lo"), i * per + (n + 1))
                begun.append(n)

            def prod(o, n, j, xh, xl, start, stop, m=P, nr=P, **flags):
                h, lo = (w[0:nr, n % RING, j * P:j * P + m] for w in (wh, wl))
                mm(o, h, xh, start=start, stop=False, **flags)
                mm(o, h, xl, start=False, stop=False, **flags)
                return mm(o, lo, xh, start=False, stop=stop, **flags)

            def prod_t(o, n, c0, w, xh, xl, start, stop, **flags):
                h, lo = (x[:, n % RING, c0:c0 + w] for x in (wh, wl))
                mm(o, xh, h, start=start, stop=False, **flags)
                mm(o, xh, lo, start=False, stop=False, **flags)
                return mm(o, xl, h, start=False, stop=stop, **flags)

            def finish(ins):
                ins.then_inc(S("job_full"), 1)

            def norm(name, p, n):
                if STEPS[name] > 1:
                    end = ADD_AT[name] + STEPS[name] - (0 if name in LOOPED else 1)
                    pe.wait_ge(S("norm_add"), end)
                else:
                    pe.wait_ge(S("norm_sq"), SQ_AT[name] + 1)
                s = 4 if name.startswith("head") else 3
                for j in range(HALVES[name]):
                    last = mm(bank[7][0:p, 0:n], ones[0:p, 0:p], sq[0:p, s, j * n:(j + 1) * n],
                              start=(j == 0), stop=(j == HALVES[name] - 1))
                last.then_inc(S("norm_ms"), 1)

            def together(ready, n, outs):
                parts(n)
                pe.wait_ge(S("w_lo"), n + 3)
                for k in range(KT):
                    pe.wait_ge(S("u_l"), U_AT[ready] + k + 1)
                    for j, (o, m, cc, begins, signal) in enumerate(outs):
                        if k == KT - 1 and j:
                            begun.append(n + j)
                        last = prod(o, n + j, k, uh[:, k, cc], ul[:, k, cc], k == 0 and begins, k == KT - 1, m=m,
                                    skip_group_check=True)
                        if k == KT - 1 and signal:
                            last.then_inc(S(signal), 1)

            def linear(phase, j, n, cols, first=0, ready=None):
                b = bank[JOBS.number(phase, j) % 4] if first else claim(phase, j)
                for m in range(first, 2):
                    parts(n + m)
                    for k in range(KT):
                        if ready and m == 0:
                            pe.wait_ge(S("u_l"), U_AT[ready] + (k // 2 if ready == "xo" else k) + 1)
                        last = prod(b[:, m * T:(m + 1) * T], n + m, k, uh[:, k, cols], ul[:, k, cols],
                                    m + k == 0, k == KT - 1, skip_group_check=True)
                finish(last)

            def linears(phase, n, cols, ready):
                b = [claim(phase, j) for j in range(2)]
                together(ready, n, [(b[0][:, 0:T], P, cols, True, None), (b[0][:, T:2 * T], P, cols, False, "job_full"),
                                    (b[1][:, 0:T], P, cols, True, None)])
                linear(phase, 1, n + 2, cols, first=1)
                for j in range(2, 4):
                    linear(phase, j, n + 2 * j, cols)

            def token_major(phase, j, n, c0):
                b = claim(phase, j)
                for p in range(2):
                    parts(n + p)
                    for tb in range(TB):
                        for k in range(4):
                            t = slice(c0 + tb * P, c0 + (tb + 1) * P)
                            last = prod_t(b[:, tb * T:(tb + 1) * T], n + p, k * T, T, uh[:, 4 * p + k, t],
                                          ul[:, 4 * p + k, t], p + tb + k == 0, p == 1 and k == 3,
                                          skip_group_check=True)
                finish(last)

            pe.wait_ge(S("early_in"), 16)
            norm("mix", P, T)
            linears("qk", S_QK, LAT, "mix")
            norm("mem", P, T)
            for s in range(4, 8):
                linear("qk", s, S_QK + 2 * s, LAT)

            def few_rows(n, b, cc, ready):
                parts(n)
                for k in range(KT):
                    pe.wait_ge(S("u_l"), U_AT[ready] + k + 1)
                    last = prod(b[:, 0:cc.stop - cc.start], n, k, uh[:, k, cc], ul[:, k, cc], k == 0, k == KT - 1)
                return last

            few_rows(S_F, bank[6], LAT, "mix").then_inc(S("fox_f_full"), 1)
            for s in range(4):
                token_major("v", s, S_V + 2 * s, T)

            def scores(i):
                kind, h, q = UNITS[i]
                b = bank[4 + i % 2]
                if i >= 2:
                    pe.wait_ge(S("sm_exp"), i - 1)
                if kind == "fox":
                    r = slice((h % 2) * HD, (h % 2) * HD + HD)
                    for qb in range(TB):
                        o = b[:, qb * T:(qb + 1) * T]
                        mm(o, qk[r, h // 2, qb * P:(qb + 1) * P], qk[r, 4 + h // 2, :], start=True, stop=False)
                        mm(o, ident[0:NF, h:h + 1].to_broadcast([NF, P]), crow[:, 4, :], start=False, stop=False)
                        last = mm(o, ident, tab("m_le")[:, qb * T:(qb + 1) * T], start=False, stop=True)
                elif kind == "xat":
                    for qb in range(TB):
                        for k in range(2):
                            last = mm(b[:, qb * T:(qb + 1) * T], qx[:, 2 * h + k, qb * P:(qb + 1) * P],
                                      kx[:, 2 * h + k, :], start=(k == 0), stop=(k == 1))
                elif q is None:
                    for qb in range(TB):
                        last = mm(b[:, qb * T:(qb + 1) * T], qa[:, h, qb * P:(qb + 1) * P], ka[:, h, CTX],
                                  start=True, stop=True)
                else:
                    last = mm(b[:, :], qa[:, h, T + q * P:T + (q + 1) * P], ka[:, h, :], start=True, stop=True)
                last.then_inc(S("sm_s"), 1)

            def transposes(i):
                q = UNITS[i][2]
                pe.wait_ge(S("sm_p"), i + 1)
                if i:
                    pe.wait_ge(S("sm_pt"), i)
                for j in range(4):
                    to = j if q is not None else (j % 2) * 2 + j // 2
                    last = pe.transpose(bank[6][:, to * P:(to + 1) * P], prob[i % 2][:, j * P:(j + 1) * P], ident)
                last.then_inc(S("sm_tr"), 1)

            def weighted(i):
                kind, h, q = UNITS[i]
                pe.wait_ge(S("sm_pt"), i + 1)
                if i:
                    pe.wait_ge(S("sm_out"), i)
                pt = probT[i % 2].rearrange("p (k q) -> p k q", k=2 if q is None else 4)
                if kind == "fox":
                    r = slice((h % 2) * HD, (h % 2) * HD + HD)
                    for kb in range(TB):
                        last = mm(bank[7][r, 0:T], v1[:, kb, h * HD:(h + 1) * HD], pt[:, kb, :],
                                  start=(kb == 0), stop=(kb == TB - 1))
                elif kind == "xat":
                    for m in range(2):
                        for kb in range(TB):
                            c = h * 256 + m * P
                            last = mm(bank[7][:, m * T:(m + 1) * T], vx[:, kb, c:c + P], pt[:, kb, :],
                                      start=(kb == 0), stop=(kb == TB - 1))
                else:
                    nk, nq = (2, T) if q is None else (4, P)
                    for kb in range(nk):
                        last = mm(bank[7][0:MD, 0:nq], va[:, kb, h * MD:(h + 1) * MD], pt[:, kb, :],
                                  start=(kb == 0), stop=(kb == nk - 1))
                last.then_inc(S("sm_o"), 1)

            wait_emptied(pe, "v", 3)
            pe.wait_ge(S("table_in"), 16)
            pe.wait_ge(S("fox_c"), 1)
            pe.wait_ge(S("u_l"), U_AT["mem"] + 8)
            for i in range(NF + 2):
                if i < NF:
                    scores(i)
                    if i < 4:
                        linear("xkv", i, S_XKV + 2 * i, CTX)
                    else:
                        token_major("xkv", i, S_XKV + 2 * i, 0)
                if 1 <= i <= NF:
                    transposes(i - 1)
                if i >= 2:
                    weighted(i - 2)

            def sb_z(h, b):
                r = slice((h % 2) * HD, (h % 2) * HD + HD)
                return [(b[:, kb * T:(kb + 1) * T], qk[r, 12 + h // 2, kb * P:(kb + 1) * P], qk[r, 8 + h // 2, :])
                        for kb in range(TB)]

            for h in range(NF + 2):
                if h < NF:
                    if h >= 2:
                        pe.wait_ge(S("sb_softplus"), h - 1)
                    else:
                        pe.wait_ge(S("sm_exp"), NF)
                    for o, a, b in sb_z(h, bank[4 + h % 2]):
                        last = mm(o, a, b, start=True, stop=True)
                    last.then_inc(S("sb_z"), 1)
                if 1 <= h <= NF:
                    g = h - 1
                    pe.wait_ge(S("sb_log"), g + 1)
                    if g:
                        pe.wait_ge(S("sb_arg"), g)
                    else:
                        pe.wait_ge(S("sm_pt"), NF)
                    logs = sbt[g % 2][:, 1, :].rearrange("p (k t) -> p k t", k=2)
                    for kb, (o, a, b) in enumerate(sb_z(g, bank[6])):
                        mm(o, a, b, start=True, stop=False)
                        last = mm(o, tab("ntri"), logs[:, kb, :], start=False, stop=(kb == 1))
                        if kb == 0:
                            last = mm(o, tab("nones"), logs[:, 1, :], start=False, stop=True)
                    last.then_inc(S("sb_t"), 1)
                if h == 2:
                    pe.wait_ge(S("sm_out"), NF)
                    norm("fox", P, T)
                    pe.wait_ge(S("norm_rstd"), NORM["fox"] + 1)
                if h >= 2:
                    g = h - 2
                    pe.wait_ge(S("sb_w"), g + 1)
                    if g:
                        pe.wait_ge(S("sb_out"), g)
                    r = slice((g % 2) * HD, (g % 2) * HD + HD)
                    wts = sbt[g % 2][:, 3, :].rearrange("p (k t) -> p k t", k=2)
                    for kb in range(TB):
                        last = mm(bank[7][r, 0:T], v1[:, kb, 512 + g * HD:512 + (g + 1) * HD], wts[:, kb, :],
                                  start=(kb == 0), stop=(kb == TB - 1))
                    last.then_inc(S("sb_o"), 1)
            norm("sb", P, T)
            for s in range(4):
                linear("out1", s, S_OUT + 2 * s, LAT, ready="fox" if s == 0 else None)
            norm("xattn", P, T)
            linears("xq", S_XQ, LAT, "xattn")
            wait_emptied(pe, "xq", 3)
            a = UNIT0["xat"]
            for i in range(NX + 2):
                if i < NX:
                    scores(a + i)
                if 1 <= i <= NX:
                    transposes(a + i - 1)
                if i >= 2:
                    weighted(a + i - 2)
            for s in range(4):
                linear("xo", s, S_XO + 2 * s, LAT, ready="xo" if s == 0 else None)
            norm("ffn", P, T)
            few_rows(S_RT, bank[6], LAT, "ffn").then_inc(S("rt_logits"), 1)
            pe.wait_ge(S("rt_rows"), 1)
            for b in range(TB):
                last = pe.transpose(bank[6][:, T + b * 32:T + b * 32 + 20], logit_rows[0:20, b * P:(b + 1) * P],
                                    ident[0:20, 0:20])
            last.then_inc(S("rt_full"), 1)
            pe.wait_ge(S("rt_gate"), 1)
            for e in range(NE // 2):
                if e >= 2:
                    pe.wait_ge(S("gate_in"), e - 1)
                for j in range(2):
                    for b in range(TB):
                        w = 96 + 64 * b + 44 + 2 * e + j
                        last = mm(bank[4 + e % 2][:, j * T + b * P:j * T + (b + 1) * P],
                                  small[:, w:w + 1].to_broadcast([P, P]), ident, start=True, stop=True)
                last.then_inc(S("gate_full"), 1)
            pe.wait_ge(S("moe_lo"), 1)
            for j in range(4):
                b = claim("moe_y", j)
                mm(b[:, :], hidl[:, 0, 0:P], uh[:, 0, :], start=True, stop=False, skip_group_check=True)
            y0 = JOBS.number("moe_y")
            pe.wait_ge(S("gate_in"), NE // 2)
            pe.wait_ge(S("c_parts"), 1)
            with pe.Fori(0, NE // 2) as i:
                for step, (what, e, m) in enumerate(TURN):
                    n = S_MOE + step
                    if what in ("gate", "up"):
                        b = 4 if what == "gate" else 5
                        if what == "gate" and m == 0:
                            pe.wait_ge(S("moe_lo"), i * 2 + (e + 1))
                        parts_turn(i, N_TURN, n)
                        for k in range(KT):
                            last = prod(bank[b][:, m * T:(m + 1) * T], n, k, uh[:, k, LAT], ul[:, k, LAT],
                                        k == 0, k == KT - 1)
                        if m == 1:
                            last.then_inc(S(f"moe_{what}"), 1)
                    elif what == "mod":
                        q, b = e, bank[6 + e % 2]
                        if m == 0:
                            pe.wait_ge(S("mod_in"), i * 3 + (2 if q == 2 else 1))
                        parts_turn(i, N_TURN, n)
                        for k in range(2):
                            c = cparts[:, 4 * (2 * m + k):4 * (2 * m + k) + 68]
                            mm(b[0:68, :], c, wh[:, n % RING, k * 512:(k + 1) * 512], start=(m + k == 0), stop=False)
                            last = mm(b[0:68, :], c, wl[:, n % RING, k * 512:(k + 1) * 512], start=False,
                                      stop=(m == 3 and k == 1))
                        if m == 3:
                            last.then_inc(S("mod_full"), 1)
                    else:
                        if m == 0:
                            pe.wait_ge(S("moe_lo"), i * 2 + (e + 2))
                        parts_turn(i, N_TURN, n)
                        for o in range(KT):
                            last = prod(bank[(y0 + o // 2) % 4][:, (o % 2) * T:(o % 2 + 1) * T], n, o, hidh[:, m, :],
                                        hidl[:, m, :], False, False, skip_group_check=True)
                            if m == 1 and o % 2:
                                last.then_inc(S("moe_down"), 1)
            norm("fin1", P, T)

            for l in range(NL):
                cols = lin_cols(l)
                n = cols.stop - cols.start
                p0 = S_L + l * LAYER_PIECES + 1
                norm(f"n1_{l}", P, 2 * T)

                def tiles_of(phase, j, p, width, cc):
                    b = claim(phase, j)
                    w = cc.stop - cc.start
                    parts(p)
                    for k in range(KT):
                        last = prod(b[0:width, 0:w], p, k, uh[:, k, cc], ul[:, k, cc], k == 0, k == KT - 1, m=width)
                    finish(last)

                b = [claim(f"mqk_{l}", j) for j in range(2)]
                together(f"n1_{l}", p0 - 1, [(bank[4][:, :], P, ALL, True, "ml_g_full"),
                                             (b[0][0:MD, 0:n], MD, cols, True, "job_full"),
                                             (b[1][0:MD, 0:n], MD, cols, True, "job_full")])
                for j in range(2, 8):
                    tiles_of(f"mqk_{l}", j, p0 + j, MD if j < 7 else P, cols if j < 4 else ALL)
                banks = [claim(f"mv_{l}", j) for j in range(4)]
                for s in range(4):
                    parts(p0 + 8 + s)
                    for tb in range(4):
                        for k in range(2):
                            t = slice(tb * P, (tb + 1) * P)
                            last = prod_t(banks[tb][:, 0:384], p0 + 8 + s, k * 384, 384, uh[:, 2 * s + k, t],
                                          ul[:, 2 * s + k, t], s + k == 0, s == 3 and k == 1)
                        if s == 3:
                            finish(last)
                for j in range(4):
                    tiles_of(f"mo_{l}", j, p0 + 12 + j, MD, cols)
                for j in range(2):
                    tiles_of(f"cq_{l}", j, p0 + 16 + j, P, cols)
                tiles_of(f"ckv_{l}", 0, p0 + 18, P, ALL)
                for j in range(2):
                    tiles_of(f"pf_{l}", j, p0 + 19 + j, P, cols)
                for d in range(2):
                    pe.wait_ge(S("ml_rows"), 2 * l + d + 1)
                    for kb in range(4):
                        last = mm(bank[4 + d][:, kb * MH:(kb + 1) * MH], rows[d][:, 0, kb * P:(kb + 1) * P],
                                  row_ident[d], start=True, stop=True)
                    last.then_inc(S("gcol_full"), 1)
                norm(f"cq_{l}", P, n)
                norm_ckv = f"ckv_{l}"
                pe.wait_ge(S("norm_rstd"), NORM[f"cq_{l}"] + 1)
                norm(norm_ckv, P, 512)
                pe.wait_ge(S("norm_out"), normed(f"cq_{l}")[1])
                pe.wait_ge(S(f"lw_in{l}"), 16)
                uq = ltab("uq").rearrange("p (k c) -> p k c", k=2)
                for h in range(MH):
                    b = claim(f"uq_{l}", h)
                    for k in range(2):
                        last = mm(b[0:MD, 0:n], uq[:, k, h * MD:(h + 1) * MD], cq[:, k, cols],
                                  start=(k == 0), stop=(k == 1))
                    finish(last)
                for h in range(MH + 1):
                    b = claim(f"rot_{l}", h)
                    if h < MH:
                        wait_emptied(pe, f"uq_{l}", h)
                    src = qa[:, h, LAT] if h < MH else kr[:, LAT]
                    finish(mm(b[0:MD, 0:T], tab("rot", MD), src, start=True, stop=True))
                pe.wait_ge(S("norm_out"), normed(f"ckv_{l}")[1])
                ukv = ltab("ukv")
                for h in range(MH):
                    b = claim(f"kn_{l}", h)
                    finish(mm(b[0:64, :], ukv[:, h * 64:(h + 1) * 64], ckv[:, :], start=True, stop=True))
                for j in range(4):
                    b = claim(f"va_{l}", j)
                    finish(mm(b[:, 0:384], ckv[:, j * P:(j + 1) * P], ukv[:, 256:640], start=True, stop=True))
                cn = tab("cn").rearrange("p (b n) -> p b n", b=2)
                sn = tab("sn").rearrange("p (b n) -> p b n", b=2)
                for s in range(n // T):
                    c0 = cols.start + s * T
                    for ft in range(2):
                        b = claim(f"fa{s}_{l}", ft)
                        wait_emptied(pe, f"pf_{l}", ft)
                        for nb in range(TB):
                            last = mm(b[:, nb * T:(nb + 1) * T], pf[:, ft, c0 + nb * P:c0 + (nb + 1) * P],
                                      tab("cdsd"), start=True, stop=True)
                        finish(last)
                    for ft in range(2):
                        b = claim(f"fy{s}_{l}", ft)
                        wait_emptied(pe, f"fa{s}_{l}", ft)
                        for nb in range(TB):
                            mm(b[:, 0:T], fa[:, ft, nb, 0:P], cn[:, nb, :], start=(nb == 0), stop=False)
                            last = mm(b[:, 0:T], fa[:, ft, nb, P:2 * P], sn[:, nb, :], start=False, stop=(nb == 1))
                        finish(last)
                pe.wait_ge(S("mla_keys"), l + 1)
                wait_emptied(pe, f"va_{l}", 3)
                units = range(UNIT0["mctx0"], UNIT0["mlat1"]) if l == 0 else range(UNIT0["mlat1"], len(UNITS))
                for i in range(units.start, units.stop + 2):
                    if i < units.stop:
                        scores(i)
                    if units.start < i <= units.stop:
                        transposes(i - 1)
                    if i >= units.start + 2:
                        weighted(i - 2)
                pe.wait_ge(S("sm_out"), units.stop)
                pe.wait_ge(S("conv_done"), 8 * l + 8)
                def spread(h, d):
                    g = l * MH + h
                    if d:
                        pe.wait_ge(S("ml_b_in"), 2 * g + 1)
                    elif g >= 2:
                        pe.wait_ge(S("ml_sum"), g - 1)
                    mm(bank[6][:, cols], row_ident[d][:, h:h + 1].to_broadcast([MH, P]), rows[d][:, 3, cols],
                       start=True, stop=True).then_inc(S("ml_b"), 1)

                def keys(h, kb):
                    kk = 4 * (l * MH + h) + kb
                    if kk >= 2:
                        pe.wait_ge(S("ml_p"), kk - 1)
                    tc = cols if kb < 2 else LAT
                    mm(bank[4 + kb % 2][:, tc], qc[:, 4 + h, kb * P:(kb + 1) * P], qc[:, h, tc],
                       start=True, stop=True).then_inc(S("ml_s"), 1)

                def values(h, kb):
                    kk = 4 * (l * MH + h) + kb
                    pe.wait_ge(S("ml_p"), kk + 1)
                    tc = cols if kb < 2 else LAT
                    for d in range(2):
                        b = bank[mlb(l, 2 * (h % 2) + d)]
                        last = mm(b[0:MD + 1, tc], mv[:, kb, h, :], sq[:, 2 * (kb % 2) + d, tc],
                                  start=(kb == 0), stop=(kb == 3), skip_group_check=True)
                    last.then_inc(S("ml_v"), 1)

                def head_m(h):
                    g = l * MH + h
                    if g:
                        pe.wait_ge(S("norm_rstd"), NORM[f"head_{l}_{h - 1}"] + 1 if h else NORM[f"n1_{l}"] + 1)
                    pe.wait_ge(S("ml_b_in"), 2 * min(g + 2, (l + 1) * MH))
                    for d in range(2):
                        mm(bank[7 - d][MD:MD + 1, cols], row_ident[d][:, h:h + 1], rows[d][:, 4, cols],
                           start=True, stop=True).then_inc(S("ml_m"), 1)

                def head_spread(h):
                    for d in range(2):
                        pe.wait_ge(S("ml_rden"), 2 * (l * MH + h) + d + 1)
                        mm(bank[7 - d][0:MD, cols], ones[MD:MD + 1, 0:MD], den[d][:, cols],
                           start=True, stop=True).then_inc(S("ml_bc"), 1)

                for h in range(MH):
                    spread(h, 0)
                    keys(h, 0)
                    spread(h, 1)
                    if h:
                        values(h - 1, 3)
                    keys(h, 1)
                    if h:
                        head_m(h - 1)
                        if h >= 2:
                            pe.wait_ge(S("ml_sum"), l * MH + h - 1)
                    else:
                        for j in range(4):
                            claim(f"mlstm_{l}", j)
                    values(h, 0)
                    keys(h, 2)
                    if h:
                        head_spread(h - 1)
                    values(h, 1)
                    if h:
                        norm(f"head_{l}_{h - 1}", MD, n)
                    keys(h, 3)
                    values(h, 2)
                values(MH - 1, 3)
                s = p0 + N_IN2

                def output(b, m, k):
                    if m < 2:
                        pe.wait_ge(S("u_l"), U_AT[f"y_{l}"] + (k + 1 if k < MH else k + 3))
                    return prod(b[:, 0:n], s + m, k, uh[:, k, cols], ul[:, k, cols], k == 0, k == KT - 1)

                head_m(MH - 1)
                pe.wait_ge(S("ml_sum"), l * MH + MH - 1)
                pe.wait_ge(S("y_moved"), 16 * (l + 1))
                early = [bank[JOBS.number(f"out_{l}", m) % 4] for m in range(2)]
                parts(s)
                pe.wait_ge(S("w_lo"), s + 2)
                for k in range(4):
                    for m in range(2):
                        output(early[m], m, k)
                head_spread(MH - 1)
                for k in range(4, KT - 1):
                    for m in range(2):
                        output(early[m], m, k)
                norm(f"head_{l}_{MH - 1}", MD, n)
                for m in range(2):
                    if m:
                        begun.append(s + m)
                    finish(output(early[m], m, KT - 1))
                for m in range(2, KT):
                    b = claim(f"out_{l}", m)
                    parts(s + m)
                    for k in range(KT):
                        last = output(b, m, k)
                    finish(last)
                norm(f"n2_{l}", P, n)
                for half, name in enumerate("ab"):
                    pu = p0 + N_IN2 + N_OUT2 + half * 32
                    b0 = JOBS.number(f"up{name}_{l}")
                    e_dve, e_act = JOBS.emptied(b0 - 1)[1], JOBS.emptied(b0)[1]
                    if half == 0:
                        together(f"n2_{l}", pu, [(claim(f"upa_{l}", j)[:, 0:n], P, cols, True, "job_full")
                                                 for j in range(3)])
                        b = claim(f"upa_{l}", 3)
                        parts(pu + 3)
                        for k in range(KT):
                            last = prod(b[:, 0:n], pu + 3, k, uh[:, k, cols], ul[:, k, cols], k == 0, k == KT - 1)
                        finish(last)
                    with pe.Fori(1 if half == 0 else 0, MC // 4) as i:
                        for j in range(4):
                            parts_turn(i, 4, pu + j)
                            pe.wait_ge(S("job_emptied_dve"), e_dve - (j == 0))
                            pe.wait_ge(S("job_emptied_act"), i * 4 + (e_act - 4 + j))
                            for k in range(KT):
                                last = prod(bank[(b0 + j) % 4][:, 0:n], pu + j, k, uh[:, k, cols], ul[:, k, cols],
                                            k == 0, k == KT - 1)
                            last.then_inc(S("job_full"), 1)
                    pd = pu + MC
                    b0 = JOBS.number(f"dn{name}_{l}")
                    e_dve, e_act = JOBS.emptied(b0)[1], JOBS.emptied(b0 - 1)[1]
                    ready = 2 + MC * (2 * l + half)
                    pe.wait_ge(S("hid_lo"), ready + MC // 2)
                    with pe.Fori(0, 4) as i:
                        for m in range(2):
                            pe.wait_ge(S("job_emptied_dve"), i * 2 + (e_dve - 2 + m))
                            for part in range(2):
                                parts_turn(i, 4, pd + 2 * m + part)
                                for k in range(8):
                                    if part and m == 0 and k in (0, 4, 6, 7):
                                        pe.wait_ge(S("hid_lo"), ready + MC // 2 + {0: 4, 4: 6, 6: 7, 7: 8}[k])
                                    last = prod(bank[(b0 + m) % 4][:, 0:n],
                                                pd + 2 * m + part, k, hh[:, part * 8 + k, 0:n],
                                                hl[:, part * 8 + k, 0:n], part + k == 0, part == 1 and k == 7)
                            last.then_inc(S("job_full"), 1)
            norm("fin2", P, T)

        @block.vector
        def _(dve):
            ch = Chain(dve, "dve_step")
            tt, ts, stt = dve.tensor_tensor, dve.tensor_scalar, dve.scalar_tensor_tensor
            lo_at = [0]

            def lo_part(s, count):
                dve.wait_ge(S("w_hi"), count)
                tt(wl[:, s, :], ring[:, s, :], wh[:, s, :].bitcast(F32), ALU.subtract).then_inc(S("w_lo"), 1)

            def split(to):
                while lo_at[0] <= min(to, N_PIECES - 1):
                    lo_part(lo_at[0] % RING, lo_at[0] + 1)
                    lo_at[0] += 1

            def split_turn(i, per, base, lo, hi):
                for j in range(lo, hi + 1):
                    lo_part((base + j) % RING, i * per + (base + j + 1))

            def add_square(name, t, p, n):
                first = 0 if name in LOOPED else 1
                dve.wait_ge(S("norm_sq"), SQ_AT[name] + t + 1)
                if t > first:
                    dve.wait_ge(S("norm_add"), ADD_AT[name] + t - first)
                tt(sq[0:p, 3, 0:n], sq[0:p, 3, 0:n], sq[0:p, t % 2, 0:n], ALU.add).then_inc(S("norm_add"), 1)

            def add_squares(name, n):
                for t in range(1, STEPS[name]):
                    add_square(name, t, P, n)

            def rest(name, i, parts):
                dve.wait_ge(S("u_h"), U_AT[name] + i + 1)
                for lo, v, hi, shift in parts:
                    if shift is None:
                        last = tt(lo, v, hi.bitcast(F32), ALU.subtract)
                    else:
                        last = stt(lo, v, shift, hi.bitcast(F32), ALU.add, ALU.subtract)
                last.then_inc(S("u_l"), 1)

            def norm(name, steps):
                dve.wait_ge(S("norm_rstd"), NORM[name] + 1)
                done = []
                for i, (parts, lows) in enumerate(steps):
                    for o, src, g, r in parts:
                        last = stt(o, src, g, r, ALU.mult, ALU.mult)
                    last.then_inc(S("u_v"), 1)
                    done.append(lows)
                    if i >= 2:
                        rest(name, i - 2, done[i - 2])
                for i in range(max(0, len(done) - 2), len(done)):
                    rest(name, i, done[i])
                return last

            def norm_tiles(name, src, gain, cols, scols, first=0, k=KT):
                g = tab(gain)
                steps = []
                for j in range(k):
                    t = first + j
                    steps.append(([(uv[:, t, cols], src[:, t, scols], g[:, j:j + 1], rstd[:, 0:T])],
                                  [(ul[:, t, cols], uv[:, t, cols], uh[:, t, cols], None)]))
                norm(name, steps)

            def smv(i, what, k, w=1):
                a = (i % 2) * 8 + what * 2 + k
                return small[:, a:a + w]

            def neg_max(i):
                g = 1 if UNITS[i][2] is not None else 2
                dve.wait_ge(S("sm_s"), i + 1)
                b = bank[4 + i % 2][:, :].rearrange("p (g w) -> p g w", g=g)
                dve.tensor_reduce(smv(i, 0, 0, g), b, AX_X, ALU.max, negate=True).then_inc(S("sm_max"), 1)

            def divide(i):
                g = 1 if UNITS[i][2] is not None else 2
                w = 512 // g
                dve.wait_ge(S("sm_exp"), i + 1)
                ch.link(dve.reciprocal(smv(i, 1, 0, g), smv(i, 2, 0, g)))
                for k in range(g):
                    p = prob[i % 2][:, k * w:(k + 1) * w]
                    last = ts(p, p, smv(i, 1, k), None, ALU.mult)
                last.then_inc(S("sm_p"), 1)

            def out_of(i):
                kind, h, q = UNITS[i]
                dve.wait_ge(S("sm_o"), i + 1)
                if kind == "fox":
                    r = slice((h % 2) * HD, (h % 2) * HD + HD)
                    last = dve.tensor_copy(heads[r, h // 2, :], bank[7][r, 0:T])
                elif kind == "xat":
                    last = dve.tensor_copy(uv[:, 2 * h:2 * h + 2, LAT],
                                           bank[7][:, :].rearrange("p (a t) -> p a t", a=2))
                elif q is None:
                    last = dve.tensor_copy(ya[:, h, CTX], bank[7][0:MD, 0:T])
                else:
                    last = dve.tensor_copy(ya[:, h, T + q * P:T + (q + 1) * P], bank[7][0:MD, 0:P])
                last.then_inc(S("sm_out"), 1)

            add_squares("mix", 512)
            split(2)
            norm_tiles("mix", res, "g_mix", LAT, LAT)
            dve.wait_ge(S("c_exp"), 1)
            ch.link(ts(small[:, 64:80], small[:, 64:80], 1.0, None, ALU.add))
            ch.link(dve.reciprocal(small[:, 64:80], small[:, 64:80]))
            ch.link(tt(small[:, 64:80], small[:, 64:80], tab("c"), ALU.mult))
            ch.link(ts(cparts[:, :], ones[:, 0:100], 0.0, None, ALU.mult))
            silu_c = small[:, 64:80].rearrange("p (k c) -> p k c", k=KT)
            cp = cparts[:, 0:32].rearrange("p (k c) -> p k c", k=KT)
            ch.link(dve.tensor_copy(cp[:, :, 0:2], silu_c))
            tt(cp[:, :, 2:4], silu_c, cp[:, :, 0:2].bitcast(F32), ALU.subtract).then_inc(S("c_parts"), 1)
            for s in range(8):
                split(S_QK + 2 * s + 1 + AHEAD)
                if s == 0:
                    add_squares("mem", 512)
                if s == 4:
                    norm_tiles("mem", res, "g_mem", CTX, CTX)
            split(S_V + AHEAD)
            dve.wait_ge(S("fox_f_full"), 1)
            ts(crow[:, 0, :], bank[6][0:NF, 0:T], tab("b_forget", NF), None, ALU.add).then_inc(S("fox_f"), 1)
            split(S_V + 5 + AHEAD)
            dve.wait_ge(S("fox_ln"), 1)
            ch.link(stt(crow[:, 2, :], crow[:, 0, :], 0.0, crow[:, 1, :], ALU.min, ALU.subtract))
            ch.link(dve.tensor_tensor_scan(out=crow[:, 3, :], data0=crow[:, 2, :], data1=crow[:, 2, :],
                                           initial=0.0, op0=ALU.add, op1=ALU.bypass))
            ts(crow[:, 4, :], crow[:, 3, :], -1.0, None, ALU.mult).then_inc(S("fox_c"), 1)
            split(S_V + 7 + AHEAD)
            for i in range(NF + 2):
                if i < NF:
                    neg_max(i)
                    divide(i)
                    split(S_XKV + 2 * i + 1 + AHEAD)
                if i >= 2:
                    out_of(i - 2)

            for h in range(NF + 2):
                if h < NF:
                    t = sbt[h % 2]
                    dve.wait_ge(S("sb_ln"), h + 1)
                    stt(t[:, 1, :], bank[4 + h % 2][:, :], 0.0, t[:, 0, :], ALU.max,
                        ALU.add).then_inc(S("sb_softplus"), 1)
                    dve.wait_ge(S("sb_softplus"), h + 1)
                    logs = t[:, 1, :].rearrange("p (k t) -> p k t", k=2)
                    stt(logs, m_ge[:, :, 0:T], 0.0, logs, ALU.is_ge, ALU.mult).then_inc(S("sb_log"), 1)
                if 1 <= h <= NF:
                    g = h - 1
                    dve.wait_ge(S("sb_t"), g + 1)
                    tt(sbt[g % 2][:, 2, :].rearrange("p (k t) -> p k t", k=2),
                       bank[6][:, :].rearrange("p (k t) -> p k t", k=2), m_ge[:, :, 0:T],
                       ALU.add).then_inc(S("sb_arg"), 1)
                if h == 2:
                    add_squares("fox", 512)
                if h >= 2:
                    g = h - 2
                    r = slice((g % 2) * HD, (g % 2) * HD + HD)
                    dve.wait_ge(S("sb_o"), g + 1)
                    dve.tensor_copy(heads[r, 4 + g // 2, :], bank[7][r, 0:T]).then_inc(S("sb_out"), 1)
                if h == 4:
                    dve.wait_ge(S("norm_rstd"), NORM["fox"] + 1)
                    g = tab("g_fox")
                    for j in range(4):
                        stt(uv[:, j, LAT], heads[:, j, :], g[:, j:j + 1], rstd[:, 0:T], ALU.mult,
                            ALU.mult).then_inc(S("u_v"), 1)
            add_squares("sb", 512)
            for j in range(4):
                rest("fox", j, [(ul[:, j, LAT], uv[:, j, LAT], uh[:, j, LAT], None)])
            g = tab("g_sb")
            norm("sb", [([(uv[:, 4 + j, LAT], heads[:, 4 + j, :], g[:, j:j + 1], rstd[:, 0:T])],
                         [(ul[:, 4 + j, LAT], uv[:, 4 + j, LAT], uh[:, 4 + j, LAT], None)]) for j in range(4)])

            def add_to_res(phase, name, first):
                for s in range(4):
                    split(first + 2 * s + 1 + AHEAD - (s == 3))
                    b = full(dve, phase, s)
                    r = res[:, 2 * s:2 * s + 2, LAT]
                    emptied(tt(r, b[:, :].rearrange("p (a t) -> p a t", a=2), r, ALU.add), "dve")
                    if s >= 2:
                        add_square(name, s - 1, P, 512)
                add_square(name, 3, P, 512)
                split(first + 7 + AHEAD)

            add_to_res("out1", "xattn", S_OUT)
            norm_tiles("xattn", res, "g_xattn", LAT, LAT)
            split(S_XQ + 7 + AHEAD)
            a = UNIT0["xat"]
            for i in range(NX + 3):
                if i < NX:
                    neg_max(a + i)
                    divide(a + i)
                if 2 <= i < NX + 2:
                    out_of(a + i - 2)
                if i >= 3:
                    j = 2 * (i - 3)
                    rest("xo", i - 3, [(ul[:, j:j + 2, LAT], uv[:, j:j + 2, LAT], uh[:, j:j + 2, LAT], None)])
            add_to_res("xo", "ffn", S_XO)
            norm_tiles("ffn", res, "g_ffn", LAT, LAT)

            split(S_RT + AHEAD)

            def spare(a, n):
                return small[:, a:a + TB * n].rearrange("p (b c) -> p b c", b=TB)

            def over(col, n=4):
                return col.to_broadcast([P, TB, n])

            tmp, tmp2, oh2, picked = spare(80, 4), spare(48, 4), spare(224, 4), spare(16, 16)
            w4 = tab("w4").rearrange("p (b c) -> p b c", b=TB)
            ones_g, in_g, oh1, weights = rt[:, :, 32:36], rt[:, :, 36:40], rt[:, :, 40:44], rt[:, :, 44:60]
            nbest, total, e2, diff, top, best, m1, m2, wa, wb = (
                rt[:, :, c:c + 1] for c in (20, 21, 22, 23, 28, 29, 30, 31, 60, 61))

            def first_of(dst, src, most):
                ch.link(tt(tmp, src, over(most), ALU.is_ge))
                ch.link(tt(tmp, tmp, w4, ALU.mult))
                ch.link(dve.tensor_reduce(top, tmp, AX_X, ALU.max))
                ch.link(tt(dst, tmp, over(top), ALU.is_equal))

            dve.wait_ge(S("rt_full"), 1)
            ch.link(dve.tensor_copy(rt[:, :, 0:20],
                                    bank[6][:, T:T + 64].rearrange("p (b c) -> p b c", b=TB)[:, :, 0:20]))
            ch.link(dve.tensor_reduce(best, rt[:, :, 0:4], AX_X, ALU.max))
            ts(nbest, best, -1.0, None, ALU.mult).then_inc(S("rt_max"), 1)
            first_of(ones_g, rt[:, :, 0:4], best)
            for b in range(TB):
                last = tt(picked[:, b, :].rearrange("p (g j) -> p g j", g=4),
                          rt[:, b, 4:20].rearrange("p (g j) -> p g j", g=4),
                          ones_g[:, b, :].rearrange("p (g o) -> p g o", o=1).to_broadcast([P, 4, 4]), ALU.mult)
            ch.link(last)
            ch.link(dve.tensor_reduce(in_g, picked.rearrange("p b (g j) -> p b j g", g=4), AX_X, ALU.add))
            ch.link(dve.tensor_reduce(m1, in_g, AX_X, ALU.max))
            first_of(oh1, in_g, m1)
            ch.link(stt(in_g, oh1, BIG, in_g, ALU.mult, ALU.add))
            ch.link(dve.tensor_reduce(m2, in_g, AX_X, ALU.max))
            tt(diff, m2, m1, ALU.subtract).then_inc(S("rt_diff"), 1)
            first_of(oh2, in_g, m2)
            dve.wait_ge(S("rt_exp"), 1)
            ch.link(stt(wa, e2, 1.0, total, ALU.add, ALU.mult))
            ch.link(dve.reciprocal(wa, wa))
            ch.link(tt(wb, wa, e2, ALU.mult))
            tt(tmp2, oh2, over(wb), ALU.mult)
            ch.link(tt(tmp, oh1, over(wa), ALU.mult))
            ch.link(tt(tmp, tmp, tmp2, ALU.add))
            for g in range(4):
                last = tt(weights[:, :, 4 * g:4 * g + 4], tmp, over(ones_g[:, :, g:g + 1]), ALU.mult)
            last.then_inc(S("rt_gate"), 1)

            ts(hidl[:, 0, 0:P], ones, 0.0, None, ALU.mult).then_inc(S("moe_lo"), 1)
            dve.memset(modv[:, 0:8], 0.0).then_inc(S("mod_in"), 1)
            split(S_MOE + 2)
            dve.wait_ge(S("gate_in"), NE // 2)
            with dve.Fori(0, NE // 2) as i:
                ch.loop(i, 2 + 3)

                def modulation(q):
                    dve.wait_ge(S("mod_full"), i * 3 + (q + 1))
                    ch.link(dve.transpose(turned[:, :, :].rearrange("p a b -> p (a b)"), bank[6 + q % 2][0:32, :]))
                    for c in range(4):
                        o = modv[32 * c:32 * c + 32, bass.ds(i * 24 + 8 * q, 8)].rearrange("p (t w) -> p t w", w=2)
                        last = tt(o, turned[:, c:16:4, 0:2], turned[:, c:16:4, 2:4], ALU.add)
                    last.then_inc(S("mod_in"), 1)
                    dve.wait_ge(S("mod_in"), i * 3 + (q + 2))

                for step, (what, e, m) in enumerate(TURN):
                    split_turn(i, N_TURN, S_MOE, step + AHEAD, step + AHEAD)
                    if (what, m) == ("gate", 1):
                        dve.wait_ge(S("moe_silu"), i * 2 + (e + 1))
                        for k in range(2):
                            e_k = eg[:, k * T:(k + 1) * T]
                            last = tt(e_k, e_k, gates[:, bass.ds(i * 2 + e, 1), :].rearrange("p a t -> p (a t)"),
                                      ALU.mult)
                        ch.link(last)
                    elif (what, m) == ("up", 1):
                        dve.wait_ge(S("moe_up"), i * 2 + (e + 1))
                        tt(eg[:, :], bank[5][:, :], eg[:, :], ALU.mult).then_inc(S("moe_v"), 1)
                        dve.wait_ge(S("moe_hi"), i * 2 + (e + 1))
                        tt(hidl[:, :, :].rearrange("p a t -> p (a t)"), eg[:, :],
                           hidh[:, :, :].rearrange("p a t -> p (a t)").bitcast(F32),
                           ALU.subtract).then_inc(S("moe_lo"), 1)
                    if step in MOD_STEPS:
                        modulation(MOD_STEPS.index(step))
            ch.end(NE // 2)
            lo_at[0] = S_L + AHEAD
            for s in range(4):
                dve.wait_ge(S("moe_down"), 4 * (NE - 1) + s + 1)
                b = bank[JOBS.number("moe_y", s) % 4]
                r = res[:, 2 * s:2 * s + 2, LAT]
                emptied(tt(r, b[:, :].rearrange("p (a t) -> p a t", a=2), r, ALU.add), "dve")
                if s >= 2:
                    add_square("fin1", s - 1, P, 512)
            add_square("fin1", 3, P, 512)
            ch.link(tt(modv[:, :], modv[:, :], tab("b_mod"), ALU.add))
            for l in range(NL):
                for k2 in range(2):
                    c = 2 * (l * 48 + 8 + 24 * k2)
                    ch.link(stt(gmod[:, 2 * l + k2, :], modv[:, c:c + 16], 1.0, tab(f"g{k2 + 1}_{l}"),
                                ALU.add, ALU.mult))
            dve.wait_ge(S("norm_rstd"), NORM["fin1"] + 1)
            g = tab("g_fin1")
            for j in range(KT):
                stt(res[:, j, LAT], res[:, j, LAT], g[:, j:j + 1], rstd[:, 0:T], ALU.mult,
                    ALU.mult).then_inc(S("fin1_tile"), 1)
                if j >= 3:
                    add_square("n1_0", j - 2, P, 512)

            def norm_mod(l, k2):
                g = gmod[:, 2 * l + k2, :]
                first = l * 48 + (0 if k2 == 0 else 24)
                off = 0 if (k2 == 0 or l == 0) else T
                steps = []
                for k in range(KT):
                    vals, lows = [], []
                    for which, cols in ((0, LAT), (1, CTX)):
                        if off and which:
                            continue
                        vals.append((uv[:, k, cols], res[:, k, cols], g[:, 2 * k + which:2 * k + which + 1],
                                     rstd[:, cols.start - off:cols.stop - off]))
                        c = 2 * (first + k) + which
                        lows.append((ul[:, k, cols], uv[:, k, cols], uh[:, k, cols], modv[:, c:c + 1]))
                    steps.append((vals, lows))
                norm(f"n{k2 + 1}_{l}", steps)
    
            for l in range(NL):
                cols = lin_cols(l)
                n = cols.stop - cols.start
                p0 = S_L + l * LAYER_PIECES + 1
                if l == 0:
                    for t in (6, 7):
                        add_square("n1_0", t, P, 512)
                norm_mod(l, 0)
                split(p0 + 3)
                bg = tab(f"b_g_{l}")
                for d in range(2):
                    dve.wait_ge(S("ml_g_full"), l + 1)
                    ri, rf = slice(32 * d, 32 * d + MH), slice(64 + 32 * d, 64 + 32 * d + MH)
                    ts(rows[d][:, 0, :], bank[4][ri, :], bg[ri, :], None, ALU.add)
                    ts(rows[d][:, 1, :], bank[4][rf, :], bg[rf, :], None, ALU.add).then_inc(S("ml_f"), 1)
                dve.wait_ge(S("ml_f"), 2 * l + 2)
                dve.memset(qkp[:, :, :, 0:2], 0.0)
                dve.memset(mv[:, :, :, MD:MD + 1], 1.0)
                dve.memset(kr[0:64, :], 0.0)
                ch.link(dve.memset(qkp[:, :, :, 258:260], 0.0))

                def gate_rows(d):
                    rr = rows[d]
                    dve.wait_ge(S("ml_ln"), 2 * l + d + 1)
                    ch.link(stt(rr[:, 1, :], rr[:, 1, :], 0.0, rr[:, 2, :], ALU.min, ALU.subtract))
                    if d == 0:
                        runs = [(slice(0, 512), False)]
                    else:
                        runs = [(slice(255, None, -1), False), (slice(511, 255, -1), True)]

                    def scan(dst, src, op):
                        for r, goes_on in runs:
                            init = rr[:, dst, 0:1] if goes_on else 0.0
                            ch.link(dve.tensor_tensor_scan(out=rr[:, dst, r], data0=rr[:, src, r],
                                                           data1=rr[:, src, r], initial=init, op0=op,
                                                           op1=ALU.bypass))

                    scan(2, 1, ALU.add)
                    ch.link(tt(rr[:, 0, :], rr[:, 0, :], rr[:, 2, :], ALU.subtract))
                    scan(3, 0, ALU.max)
                    ch.link(tt(rr[:, 4, :], rr[:, 2, :], rr[:, 3, :], ALU.add))
                    ts(rr[:, 3, :], rr[:, 3, :], -1.0, None, ALU.mult).then_inc(S("ml_rows"), 1)

                taps = tab(f"conv_{l}", MD).rearrange("p (h t) -> p h t", h=8)

                def conv(j):
                    wait_emptied(dve, f"mqk_{l}", j)
                    segs = slice(0, 2) if (l == 0 or j >= 4) else slice(1, 2)
                    cc = cols if j < 4 else ALL
                    o = qc[:, j, cc].rearrange("p (s t) -> p s t", t=T)
                    ch.link(ts(o, qkp[:, j, segs, 0:T], taps[:, j, 0:1], None, ALU.mult))
                    for t in range(1, 5):
                        last = stt(o, qkp[:, j, segs, t:t + T], taps[:, j, t:t + 1], o, ALU.mult, ALU.add)
                        if t < 4:
                            ch.link(last)
                    last.then_inc(S("conv_sum"), 1)

                for j in range(16):
                    split(p0 + j + AHEAD)
                    if j in (2, 3):
                        gate_rows(j - 2)
                    if 2 <= j < 10:
                        conv(j - 2)
                split(p0 + 18 + AHEAD)
                if l == 0:
                    add_squares("cq_0", 512)
                split(p0 + 20 + AHEAD)
                g = tab(f"g_qn_{l}")
                dve.wait_ge(S("norm_rstd"), NORM[f"cq_{l}"] + 1)
                for j in range(2):
                    last = stt(cq[:, j, cols], cq[:, j, cols], g[:, j:j + 1], rstd[:, 0:n], ALU.mult, ALU.mult)
                last.then_inc(S("norm_out"), 1)
                dve.wait_ge(S("norm_rstd"), NORM[f"ckv_{l}"] + 1)
                stt(ckv[:, :], ckv[:, :], tab(f"g_kvn_{l}"), rstd[:, :], ALU.mult, ALU.mult).then_inc(S("norm_out"), 1)
                for h in range(MH + 1):
                    b = full(dve, f"rot_{l}", h)
                    o = qa[:, h, LAT] if h < MH else kr[:, LAT]
                    t1 = sq[0:MD, 2 + h // 2, (h % 2) * T:(h % 2 + 1) * T]
                    tt(t1, b[0:MD, 0:T], tab("sin", MD), ALU.mult)
                    ch.link(tt(o, o, tab("cos", MD), ALU.mult))
                    emptied(tt(o, o, t1, ALU.add), "dve")
                dve.wait_ge(S("job_emptied_dve"), JOBS.emptied(JOBS.number(f"rot_{l}", MH))[1])
                for h in range(MH):
                    last = dve.tensor_copy(ka[64:96, h, :], kr[64:96, :])
                last.then_inc(S("mla_keys"), 1)
                units = range(UNIT0["mctx0"], UNIT0["mlat1"]) if l == 0 else range(UNIT0["mlat1"], len(UNITS))
                for i in range(units.start, units.stop + 2):
                    if i < units.stop:
                        neg_max(i)
                        divide(i)
                    if i >= units.start + 2:
                        out_of(i - 2)
                dve.wait_ge(S("sm_out"), units.stop)
                for h in range(MH):
                    rest(f"y_{l}", h, [(ul[0:MD, h, cols], ya[:, h, cols], uh[0:MD, h, cols], None)])
                for j in range(2):
                    rest(f"y_{l}", MH + j, [(yfl[:, j, cols], yf[:, j, cols], yfh[:, j, cols], None)])

                masks = [m_ge[:, :, 1:T + 1], tab("m_le").rearrange("p (k t) -> p k t", k=2)]
                gm = tab(f"g_ml_{l}", MD)

                def args(h, kb):
                    if kb < 2 and l:
                        return
                    for d in range(2):
                        if kb == 0:
                            dve.wait_ge(S("ml_b_in"), 2 * (l * MH + h) + d + 1)
                        if kb:
                            dve.wait_ge(S("ml_e"), 2 * (4 * (l * MH + h) + kb - 1) + d + 1)
                        tc = CTX if kb < 2 else LAT
                        tt(arg[d][:, tc], rb[d][:, tc], masks[d][:, kb % 2, :], ALU.add).then_inc(S("ml_arg"), 1)

                def weigh(h, kb):
                    kk = 4 * (l * MH + h) + kb
                    tc = cols if kb < 2 else LAT
                    dve.wait_ge(S("ml_s"), kk + 1)
                    for d in range(2):
                        e = sq[:, 2 * (kb % 2) + d, :]
                        dve.wait_ge(S("ml_e"), 2 * kk + d + 1)
                        last = stt(e[:, tc], bank[4 + kb % 2][:, tc], MD ** -0.5, e[:, tc], ALU.mult, ALU.mult)
                    last.then_inc(S("ml_p"), 1)

                def head_min(h):
                    for d in range(2):
                        c = 2 * (l * MH + h) + d + 1
                        dve.wait_ge(S("ml_ln2"), c)
                        dve.wait_ge(S("ml_m"), c)
                        stt(den[d][:, cols], den[d][:, cols], -1.0, bank[7 - d][MD:MD + 1, cols], ALU.mult,
                            ALU.min).then_inc(S("ml_min"), 1)

                def head_sum(h):
                    for d in range(2):
                        dve.wait_ge(S("ml_bc"), 2 * (l * MH + h) + d + 1)
                        ch.link(dve.tensor_copy(quot[d][:, cols], bank[7 - d][0:MD, cols]))
                        last = tt(quot[d][:, cols], bank[mlb(l, 2 * (h % 2) + d)][0:MD, cols], quot[d][:, cols], ALU.mult)
                    ch.link(last)
                    tt(quot[0][:, cols], quot[0][:, cols], quot[1][:, cols], ALU.add).then_inc(S("ml_sum"), 1)

                def head_value(h):
                    dve.wait_ge(S("norm_rstd"), NORM[f"head_{l}_{h}"] + 1)
                    q = quot[0][:, cols]
                    stt(q, q, gm[:, h:h + 1], rstd[0:MD, 0:n], ALU.mult, ALU.mult).then_inc(S("norm_out"), 1)
                    dve.wait_ge(S("norm_out"), normed(f"head_{l}_{h}")[1])
                    tt(mo[:, h, cols], q, mo[:, h, cols], ALU.mult).then_inc(S("u_v"), 1)

                def head_rest(h):
                    rest(f"y_{l}", MH + 2 + h,
                         [(ul[0:MD, MH + h, cols], mo[:, h, cols], uh[0:MD, MH + h, cols], None)])

                for h in range(MH):
                    args(h, 0)
                    weigh(h, 0)
                    args(h, 1)
                    if h:
                        head_min(h - 1)
                    weigh(h, 1)
                    args(h, 2)
                    if h:
                        head_sum(h - 1)
                    if h >= 2:
                        head_rest(h - 2)
                    weigh(h, 2)
                    args(h, 3)
                    weigh(h, 3)
                    if h:
                        head_value(h - 1)
                head_min(MH - 1)
                head_rest(MH - 2)
                head_sum(MH - 1)
                head_value(MH - 1)
                head_rest(MH - 1)

                def gated(l, m, b, chunk):
                    for which, cc in ((1, CTX), (0, LAT)):
                        if l and which:
                            continue
                        c = 2 * (l * 48 + 8 * chunk + m) + which
                        src = b[:, cc] if l == 0 else b[:, 0:T]
                        last = stt(res[:, m, cc], src, modv[:, c:c + 1], res[:, m, cc], ALU.mult, ALU.add)
                    return last

                for m in range(KT):
                    split(p0 + N_IN2 + min(m, KT - 2) + AHEAD)
                    b = full(dve, f"out_{l}", m)
                    emptied(gated(l, m, b, 2), "dve")
                    if m >= 2 + l:
                        add_square(f"n2_{l}", m - 1 - l, P, n)
                for m in range(KT - 1 - l, KT):
                    add_square(f"n2_{l}", m, P, n)
                split(p0 + N_IN2 + KT - 1 + AHEAD)
                norm_mod(l, 1)
                if l == 0:
                    for j in range(2):
                        dve.memset(small[:, 94 + j:95 + j], 0.0).then_inc(S("hid_lo"), 1)
                for half, name in enumerate("ab"):
                    pu = p0 + N_IN2 + N_OUT2 + half * 32
                    h0 = (2 * l + half) * MC
                    split(pu + AHEAD - 1)
                    with dve.Fori(0, MC // 4) as i:
                        for j in range(4):
                            split_turn(i, 4, pu, j + AHEAD, j + AHEAD)
                            dve.wait_ge(S("hid_hi"), i * 4 + (h0 + j + 1))
                            d = bass.ds(i * 4 + j, 1)
                            tt(hl[:, d, 0:n].rearrange("p a b -> p (a b)"), sq[:, 2 + j % 2, 0:n],
                               hh[:, d, 0:n].rearrange("p a b -> p (a b)").bitcast(F32),
                               ALU.subtract).then_inc(S("hid_lo"), 1)
                    lo_at[0] = pu + MC + AHEAD
                    pd = pu + MC
                    nxt = ("n1_1" if l == 0 else "fin2") if half else None
                    b0, f0 = JOBS.number(f"dn{name}_{l}"), JOBS.full(JOBS.number(f"dn{name}_{l}"))
                    if nxt:
                        dve.wait_ge(S("hid_lo"), 2 + MC * (2 * l + half + 1))
                        ch.link(dve.memset(sq[:, 3, :], 0.0))
                    ends = nxt and l == NL - 1

                    def down_turn(i, fixed=None):
                        for j in range(2):
                            dve.wait_ge(S("job_full"), i * 2 + (f0 + j))
                            for which, cc in ((1, CTX), (0, LAT)):
                                if l and which:
                                    continue
                                c = 2 * (l * 48 + 40 + j) + which
                                b = bank[(b0 + j) % 4]
                                src = b[:, cc] if l == 0 else b[:, 0:T]
                                if fixed is None:
                                    r = res[:, bass.ds(i * 2 + j, 1), cc].rearrange("p a b -> p (a b)")
                                    gate = modv[:, bass.ds(i * 4 + c, 1)]
                                else:
                                    r = res[:, 2 * fixed + j, cc]
                                    gate = modv[:, 4 * fixed + c:4 * fixed + c + 1]
                                last = stt(r, src, gate, r, ALU.mult, ALU.add)
                            last.then_inc(S("job_emptied_dve"), 1)
                        if nxt:
                            for j in range(2):
                                dve.wait_ge(S("norm_sq"), i * 2 + (SQ_AT[nxt] + j + 1))
                                dve.wait_ge(S("norm_add"), i * 2 + (ADD_AT[nxt] + j))
                                tt(sq[:, 3, 0:n], sq[:, 3, 0:n], sq[:, j, 0:n], ALU.add).then_inc(S("norm_add"), 1)

                    turns = 3 if ends else 4
                    with dve.Fori(0, turns) as i:
                        split_turn(i, 4, pd, AHEAD, AHEAD + 3)
                        down_turn(i)
                    if ends:
                        lo_at[0] = pd + 12 + AHEAD
                        split(pd + 15)
                        down_turn(3, 3)
                    lo_at[0] = pd + MC + AHEAD
            dve.wait_ge(S("norm_rstd"), NORM["fin2"] + 1)
            g = tab("g_fin2")
            for j in range(KT):
                last = stt(res[:, j, LAT], res[:, j, LAT], g[:, j:j + 1], rstd[:, 0:T], ALU.mult, ALU.mult)
            last.then_inc(S("norm_out"), 1)


def pack(inputs):
    f = {k: np.asarray(v) for k, v in inputs.items()}

    def fm(w, c0, c1, width=P, at=0):
        out = []
        for c in range(c0, c1, width):
            t = np.zeros((P, KT, P), np.float32)
            t[:, :, at:at + width] = w[:, c:c + width].reshape(KT, P, width).transpose(1, 0, 2)
            out.append(t.reshape(P, PIECE))
        return out

    def moving(w, c0, c1, k, width):
        out = []
        for c in range(c0, c1, width):
            for g in range(KT // k):
                t = np.zeros((P, PIECE), np.float32)
                part = w[g * k * P:(g + 1) * k * P, c:c + width].reshape(k, P, width).transpose(1, 0, 2)
                t[:, 0:k * width] = part.reshape(P, k * width)
                out.append(t)
        return out

    def placed(groups):
        t = np.zeros((P, KT, P), np.float32)
        for c, w in groups:
            t[:, :, c:c + w.shape[1]] = w.reshape(KT, P, -1).transpose(1, 0, 2)
        return [t.reshape(P, PIECE)]

    w = f["w_in"][0]
    slots = fm(w, 0, 1024) + fm(w, 1536, 2560) + placed([(0, w[:, 3072:])]) + moving(w, 1024, 1536, 4, T) + moving(w, 2560, 3072, 4, T)
    slots += fm(f["w_xkv"][0], 0, 1024) + moving(f["w_xkv"][0], 1024, 2048, 4, T)
    slots += fm(f["w_out"][0], 0, 1024) + fm(f["w_xq"][0], 0, 1024) + fm(f["w_xo"][0], 0, 1024)
    slots += placed([(0, f["w_router_group"][0]), (4, f["w_router_expert"][0])])
    mods = [s for l in range(NL) for s in moving(f["w_mod_2"][l], 0, 6 * D, 2, 512)]
    mods = iter(mods)
    for turn in range(NE // 2):
        for what, e, m in TURN:
            if what == "mod":
                slots.append(next(mods))
            elif what == "down":
                slots.append(f["w_exp_down"][0, 2 * turn + e][m * P:(m + 1) * P, :])
            else:
                slots += fm(f[f"w_exp_{what}"][0, 2 * turn + e], m * P, (m + 1) * P)
    for l in range(NL):
        w = f["w_in_2"][l]
        slots += placed([(c, w[:, 1792 + 4 * i:1796 + 4 * i]) for i, c in enumerate((0, 64, 32, 96))])
        heads_qk = fm(w, 256, 256 + 768, MD)
        heads_qk[-1] = placed([(0, w[:, 928:1024]), (MD, w[:, 2192:2224])])[0]
        slots += heads_qk + moving(w, 1024, 1408, 2, 384) + fm(w, 1408, 1792, MD)
        slots += fm(w, 1808, 2064) + fm(w, 2064, 2192) + fm(w, 0, 256)
        wo = f["w_out_2"][l]
        t = np.zeros((P, KT, KT, P), np.float32)
        for k in range(KT):
            r0 = (640 if k < MH else 256) + MD * (k % MH)
            t[0:MD, :, k, :] = wo[r0:r0 + MD].reshape(MD, KT, P)
            t[MD:, :, k, :] = wo[32 * k:32 * k + 32].reshape(32, KT, P)
        slots += [t[:, m].reshape(P, PIECE) for m in range(KT)]
        wd = f["w_down_2"][l].reshape(2, 2, 8, P, KT, P).transpose(0, 4, 1, 3, 2, 5).reshape(2, 16, P, PIECE)
        for half in range(2):
            slots += fm(f["w_up_2"][l], half * FF // 2, (half + 1) * FF // 2) + list(wd[half])
    stream = np.stack(slots)
    assert stream.shape == (N_PIECES, P, PIECE), stream.shape

    table = np.zeros((P, N_COLS), np.float32)

    def put(name, a, rows=P):
        c, n = COL[name]
        table[0:rows, c:c + n] = a.reshape(rows, n)

    def cols_of(g, k=KT):
        return g.reshape(k, P).transpose(1, 0)

    p = np.arange(P)
    t = np.arange(T)
    key = (p[:, None] + P * np.arange(2)[None, :])[:, :, None]
    put("ident", np.eye(P, dtype=np.float32))
    put("ones", np.ones((P, P), np.float32))
    put("nones", -np.ones((P, P), np.float32))
    put("ntri", -(p[:, None] >= p[None, :]).astype(np.float32))
    put("m_le", np.where(t <= key, 0.0, BIG))
    put("m_ge", np.concatenate([np.full((P, 2, 1), BIG), np.where(t >= key, 0.0, BIG)], 2))
    a64 = 2 * np.pi * ((np.arange(64)[:, None] * np.arange(64)[None, :]) % 64) / 64
    cd = np.kron(np.eye(2), np.cos(a64))
    sd = np.kron(np.eye(2), np.sin(a64))
    put("cdsd", np.concatenate([cd, sd], 1) / 128.0)
    a256 = 2 * np.pi * ((t[:, None] * t[None, :]) % T) / T
    put("cn", np.cos(a256).reshape(2, P, T).transpose(1, 0, 2))
    put("sn", (-np.sin(a256)).reshape(2, P, T).transpose(1, 0, 2))
    nf = RD // 4
    freqs = (np.float32(10000.0) ** (-np.arange(nf, dtype=np.float32) / np.float32(nf))).astype(np.float32)
    ang = np.zeros((RD, T), np.float32)
    rot = np.zeros((MD, MD), np.float32)
    for axis in range(2):
        pos = (t // 64 if axis == 0 else t % 64).astype(np.float32)
        for half in range(2):
            for i in range(nf):
                r = axis * 16 + half * 8 + i
                ang[r] = pos * freqs[i]
                other = axis * 16 + (1 - half) * 8 + i
                rot[64 + other, 64 + r] = -1.0 if half == 0 else 1.0
    cos, sin = np.ones((MD, T)), np.zeros((MD, T))
    cos[64:], sin[64:] = np.cos(ang.astype(np.float64)), np.sin(ang.astype(np.float64))
    put("cos", cos, MD)
    put("sin", sin, MD)
    put("rot", rot, MD)
    put("w4", np.tile(np.arange(4, 0, -1), (P, 2)))
    put("eps", np.full((P, 1), EPS))
    put("tiny", np.full((P, 1), 1e-37))
    for name, key_ in (("g_mix", "norm_mix"), ("g_xattn", "norm_xattn"), ("g_mem", "norm_mem"), ("g_ffn", "norm_ffn")):
        put(name, cols_of(f[key_][0]))
    put("g_fin1", cols_of(f["norm_final"]))
    put("g_fin2", cols_of(f["g_final_2"]))
    put("g_fox", cols_of(f["norm_fox_out"][0], 4))
    put("g_sb", cols_of(f["norm_sb_out"][0], 4))
    put("b_forget", f["b_forget"][0], 8)
    put("b_route", np.concatenate([f["b_router_group"][0], f["b_router_expert"][0]]), 20)
    put("c", np.stack([cols_of(f["c_2"][0]), cols_of(f["c_ctx_2"])], 2))
    small = np.zeros((NL, P, N_LCOLS), np.float32)
    bm = f["b_mod_2"].reshape(NL * 48, P).transpose(1, 0)
    put("b_mod", np.stack([bm, bm], 2))
    for l in range(NL):
        for k2 in (1, 2):
            g = cols_of(f[f"g_norm{k2}_2"][l])
            put(f"g{k2}_{l}", np.stack([g, g], 2))
        put(f"g_ml_{l}", f["g_mlstm_2"][l].reshape(MH, MD).transpose(1, 0), MD)
        put(f"g_qn_{l}", cols_of(f["g_q_norm_2"][l], 2))
        put(f"g_kvn_{l}", f["g_kv_norm_2"][l])
        put(f"conv_{l}", f["conv_qk_2"][l].reshape(5, 8, MD).transpose(2, 1, 0), MD)
        bg = np.zeros((P, 1), np.float32)
        for i, row in enumerate((0, 64, 32, 96)):
            bg[row:row + MH, 0] = f["b_gates_2"][l][4 * i:4 * i + MH]
        put(f"b_g_{l}", bg)
        kv = f["w_ukv_2"][l].reshape(P, MH, 160)
        small[l, :, 0:768] = f["w_uq_2"][l].reshape(2, P, 384).transpose(1, 0, 2).reshape(P, 768)
        small[l, :, 768:1024] = kv[:, :, 0:64].reshape(P, 256)
        small[l, :, 1024:1408] = kv[:, :, 64:].reshape(P, 384)

    def act_fm(x):
        return np.ascontiguousarray(x.reshape(T, KT, P).transpose(2, 1, 0))

    return {"w_stream": stream, "table": table, "small": small, "x": act_fm(f["x"]), "mem": act_fm(f["mem"]), "ctx": act_fm(f["ctx_2"])}


def kernel(**inputs):
    import concourse.bacc as bacc
    from concourse.bass_utils import run_bass_kernel_spmd

    arrays = pack(inputs)
    nc = bacc.Bacc("TRN2", target_bir_lowering=False, num_devices=1)
    args = [nc.dram_tensor(f"in_{n}", a.shape, F32, kind="ExternalInput").ap() for n, a in arrays.items()]
    out = nc.dram_tensor("out_dram", (P, KT, T), F32, kind="ExternalOutput").ap()
    build(nc, *args, out)
    r = run_bass_kernel_spmd(nc, [{f"in_{n}": a for n, a in arrays.items()}], core_ids=[0])
    got = r.results[0]["out_dram"]
    return np.ascontiguousarray(got.transpose(2, 1, 0).reshape(1, T, D))
```
